# Optimizing a Trainium2 kernel written in Bass

```python
import jax, jax.numpy as jnp
from jax import lax
import numpy as np

D_MODEL = 1024
BATCH = 1
SEQ = 1024
DEPTH = 1
DEC_BATCH = 8
DEC_SEQ = 8
PAST_LEN = 1024
PAGE_SIZE = 128

SB_HEADS = 8
SB_HEAD_DIM = 64
SB_WIDTH = SB_HEADS * SB_HEAD_DIM
SB_BLOCK = 128
SB_BIAS_INIT = -6.0
GLA_HEADS = 4
GLA_KEY_DIM = 64
GLA_VAL_DIM = 128
GLA_QK_WIDTH = GLA_HEADS * GLA_KEY_DIM
GLA_V_WIDTH = GLA_HEADS * GLA_VAL_DIM
GLA_GATE_RANK = 16
GLA_GATE_TEMP = 16.0
GLA_CHUNK = 16
MIX_WIDTH = SB_WIDTH + GLA_V_WIDTH
D_FF = 4 * D_MODEL
NORM_EPS = 1e-6
IN_SPLITS = (SB_WIDTH, SB_WIDTH, SB_WIDTH, GLA_QK_WIDTH, GLA_QK_WIDTH, GLA_V_WIDTH, GLA_V_WIDTH, GLA_GATE_RANK)
IN_WIDTH = 3 * SB_WIDTH + 2 * GLA_QK_WIDTH + 2 * GLA_V_WIDTH + GLA_GATE_RANK

kernel_name = "stickbreak_gla_hybrid_step"

def rms_norm(x, gain):
    xf = x.astype(jnp.float32)
    y = xf * lax.rsqrt(jnp.mean(xf * xf, axis=-1, keepdims=True) + NORM_EPS)
    return (y * gain.astype(jnp.float32)).astype(x.dtype)

def split_columns(p):
    parts, start = [], 0
    for w in IN_SPLITS:
        parts.append(p[..., start:start + w])
        start += w
    return parts

def sb_block(q, k, v, q_pos, k_pos, bias):
    z = (jnp.einsum("bqhd,bkhd->bhqk", q, k).astype(jnp.float32) * (SB_HEAD_DIM ** -0.5)
         + bias.astype(jnp.float32)[None, :, None, None])
    causal = (k_pos[None, :] < q_pos[:, None])[None, None]
    log_stay = jnp.where(causal, jax.nn.log_sigmoid(-z), 0.0)
    log_after = lax.cumsum(log_stay, axis=3, reverse=True) - log_stay
    w = jnp.where(causal, jnp.exp(jax.nn.log_sigmoid(z) + log_after), 0.0)
    return jnp.einsum("bhqk,bkhd->bqhd", w.astype(v.dtype), v)

def stick_breaking_attention(q, k, v, q_offset, bias):
    B, Tq, H, Dh = q.shape
    Tk = k.shape[1]
    blk = SB_BLOCK if Tq % SB_BLOCK == 0 else Tq
    n = Tq // blk
    k_pos = jnp.arange(Tk, dtype=jnp.int32)
    q_pos = (q_offset + jnp.arange(Tq, dtype=jnp.int32)).reshape(n, blk)
    qb = q.reshape(B, n, blk, H, Dh).transpose(1, 0, 2, 3, 4)
    ob = lax.map(lambda a: sb_block(a[0], k, v, a[1], k_pos, bias), (qb, q_pos))
    return ob.transpose(1, 0, 2, 3, 4).reshape(B, Tq, H, Dh)

def gla_chunked(q, k, v, log_a, s0):
    B, T, H, DK = q.shape
    DV = v.shape[-1]
    C = GLA_CHUNK if T % GLA_CHUNK == 0 else T
    n = T // C

    def blocks(t):
        return t.astype(jnp.float32).reshape(B, n, C, H, t.shape[-1]).transpose(0, 3, 1, 2, 4)

    qc = blocks(q) * (DK ** -0.5)
    kc, vc, ac = blocks(k), blocks(v), blocks(log_a)
    b = jnp.cumsum(ac, axis=3)
    b_end = b[:, :, :, -1:, :]
    q_dec = qc * jnp.exp(b)
    k_inv = kc * jnp.exp(-b)
    tri = jnp.tril(jnp.ones((C, C), dtype=bool))
    scores = jnp.where(tri, jnp.einsum("bhncd,bhnsd->bhncs", q_dec, k_inv), 0.0)
    o_intra = jnp.einsum("bhncs,bhnsv->bhncv", scores, vc)
    ds = jnp.einsum("bhncd,bhncv->nbhdv", kc * jnp.exp(b_end - b), vc)
    decay = jnp.exp(b_end[:, :, :, 0, :]).transpose(2, 0, 1, 3)

    def step(s, inp):
        dec, d = inp
        return dec[..., None] * s + d, s

    s_final, s_start = lax.scan(step, s0.astype(jnp.float32), (decay, ds))
    o_inter = jnp.einsum("bhncd,nbhdv->bhncv", q_dec, s_start)
    o = (o_intra + o_inter).transpose(0, 2, 3, 1, 4).reshape(B, T, H, DV)
    return o.astype(v.dtype), s_final

def hybrid_layer(x, c, k_past, v_past, gla_s0, q_offset, w_ada, b_ada, g_mix, w_in, b_sb,
                 w_gla_gate, b_gla_gate, g_gla_out, w_out, g_ffn, w_up, w_down):
    B, T, _ = x.shape
    mod = jax.nn.silu(c) @ w_ada + b_ada
    sh1, sc1, ga1, sh2, sc2, ga2 = [m[:, None, :] for m in jnp.split(mod, 6, axis=-1)]
    h = rms_norm(x, g_mix) * (1.0 + sc1) + sh1
    q_sb, k_sb, v_sb, q_g, k_g, v_g, r_g, a_low = split_columns(h @ w_in)
    q_sb = q_sb.reshape(B, T, SB_HEADS, SB_HEAD_DIM)
    k_sb = k_sb.reshape(B, T, SB_HEADS, SB_HEAD_DIM)
    v_sb = v_sb.reshape(B, T, SB_HEADS, SB_HEAD_DIM)
    k_all = k_sb if k_past is None else jnp.concatenate([k_past, k_sb], axis=1)
    v_all = v_sb if v_past is None else jnp.concatenate([v_past, v_sb], axis=1)
    o_sb = stick_breaking_attention(q_sb, k_all, v_all, q_offset, b_sb).reshape(B, T, SB_WIDTH)
    log_a = jax.nn.log_sigmoid((a_low @ w_gla_gate + b_gla_gate).astype(jnp.float32)) / GLA_GATE_TEMP
    o_g, s_new = gla_chunked(q_g.reshape(B, T, GLA_HEADS, GLA_KEY_DIM),
                             k_g.reshape(B, T, GLA_HEADS, GLA_KEY_DIM),
                             v_g.reshape(B, T, GLA_HEADS, GLA_VAL_DIM),
                             log_a.reshape(B, T, GLA_HEADS, GLA_KEY_DIM), gla_s0)
    o_g = rms_norm(o_g, g_gla_out).reshape(B, T, GLA_V_WIDTH) * jax.nn.silu(r_g)
    x = x + ga1 * (jnp.concatenate([o_sb, o_g], axis=-1) @ w_out)
    h2 = rms_norm(x, g_ffn) * (1.0 + sc2) + sh2
    x = x + ga2 * (jnp.square(jax.nn.relu(h2 @ w_up)) @ w_down)
    return x, k_sb, v_sb, s_new

def setup_inputs(seed: int = 0) -> dict:
    key = jax.random.key(seed)
    ks = jax.random.split(key, 24)
    n_pages = PAST_LEN // PAGE_SIZE
    n_used = DEC_BATCH * n_pages
    n_phys = n_used + max(1, n_used // 4)
    f32 = jnp.float32
    nrm = lambda k, s, sc: jax.random.normal(k, s, f32) * sc
    perm = jax.random.permutation(ks[7], n_phys)[:n_used].astype(jnp.int32)
    return {
        "x_prompt": nrm(ks[0], (BATCH, SEQ, D_MODEL), 1.0),
        "x_sample": nrm(ks[1], (DEC_BATCH, DEC_SEQ, D_MODEL), 1.0),
        "c_prompt": nrm(ks[2], (BATCH, D_MODEL), 1.0),
        "c_sample": nrm(ks[3], (DEC_BATCH, D_MODEL), 1.0),
        "cache_k": nrm(ks[4], (DEPTH, n_phys, PAGE_SIZE, SB_HEADS, SB_HEAD_DIM), 1.0),
        "cache_v": nrm(ks[5], (DEPTH, n_phys, PAGE_SIZE, SB_HEADS, SB_HEAD_DIM), 1.0),
        "state_gla": nrm(ks[6], (DEPTH, DEC_BATCH, GLA_HEADS, GLA_KEY_DIM, GLA_VAL_DIM), 0.3),
        "page_table": perm.reshape(DEC_BATCH, n_pages),
        "w_ada": nrm(ks[8], (DEPTH, D_MODEL, 6 * D_MODEL), 0.5 * D_MODEL ** -0.5),
        "b_ada": nrm(ks[9], (DEPTH, 6 * D_MODEL), 0.01),
        "g_mix": 1.0 + nrm(ks[10], (DEPTH, D_MODEL), 0.02),
        "w_in": nrm(ks[11], (DEPTH, D_MODEL, IN_WIDTH), D_MODEL ** -0.5),
        "b_sb": SB_BIAS_INIT + nrm(ks[20], (DEPTH, SB_HEADS), 0.5),
        "w_gla_gate": nrm(ks[12], (DEPTH, GLA_GATE_RANK, GLA_QK_WIDTH), GLA_GATE_RANK ** -0.5),
        "b_gla_gate": nrm(ks[13], (DEPTH, GLA_QK_WIDTH), 0.01),
        "g_gla_out": 1.0 + nrm(ks[14], (DEPTH, GLA_VAL_DIM), 0.02),
        "w_out": nrm(ks[15], (DEPTH, MIX_WIDTH, D_MODEL), MIX_WIDTH ** -0.5),
        "g_ffn": 1.0 + nrm(ks[16], (DEPTH, D_MODEL), 0.02),
        "w_up": nrm(ks[17], (DEPTH, D_MODEL, D_FF), D_MODEL ** -0.5),
        "w_down": nrm(ks[18], (DEPTH, D_FF, D_MODEL), D_FF ** -0.5),
        "g_final": 1.0 + nrm(ks[19], (D_MODEL,), 0.02),
    }

def reference(x_prompt, x_sample, c_prompt, c_sample, cache_k, cache_v, state_gla, page_table,
              w_ada, b_ada, g_mix, w_in, b_sb, w_gla_gate, b_gla_gate, g_gla_out, w_out,
              g_ffn, w_up, w_down, g_final):
    n_dec = x_sample.shape[0]
    past_len = page_table.shape[1] * cache_k.shape[2]
    xp, xs = x_prompt, x_sample
    kp_l, vp_l, sp_l, ks_l, vs_l, ss_l = [], [], [], [], [], []
    for l in range(DEPTH):
        wl = (w_ada[l], b_ada[l], g_mix[l], w_in[l], b_sb[l], w_gla_gate[l], b_gla_gate[l],
              g_gla_out[l], w_out[l], g_ffn[l], w_up[l], w_down[l])
        s0 = jnp.zeros((xp.shape[0], GLA_HEADS, GLA_KEY_DIM, GLA_VAL_DIM), jnp.float32)
        xp, kp, vp, sp = hybrid_layer(xp, c_prompt, None, None, s0, 0, *wl)
        k_past = cache_k[l][page_table].reshape(n_dec, past_len, SB_HEADS, SB_HEAD_DIM)
        v_past = cache_v[l][page_table].reshape(n_dec, past_len, SB_HEADS, SB_HEAD_DIM)
        xs, kn, vn, sn = hybrid_layer(xs, c_sample, k_past, v_past, state_gla[l], past_len, *wl)
        kp_l.append(kp); vp_l.append(vp); sp_l.append(sp)
        ks_l.append(kn); vs_l.append(vn); ss_l.append(sn)
    y_prompt = rms_norm(xp, g_final)
    y_sample = rms_norm(xs, g_final)
    return (y_prompt, y_sample, jnp.stack(kp_l), jnp.stack(vp_l), jnp.stack(sp_l),
            jnp.stack(ks_l), jnp.stack(vs_l), jnp.stack(ss_l))


_drawn_inputs = setup_inputs


def setup_inputs(seed=0):
    import zlib

    import numpy as np

    out = dict(_drawn_inputs(seed))
    spreads = {}
    factors = {'cache_k': 3.261,
     'b_sb': 7.384,
     'b_gla_gate': 8.0,
     'g_gla_out': 26.539,
     'g_ffn': 6.151,
     'g_final': 7.956}
    for name, (base, spread) in spreads.items():
        noise = np.random.default_rng([zlib.crc32(name.encode()), seed]).standard_normal(out[name].shape)
        drawn = base * np.exp(spread * noise) if base else spread * noise
        out[name] = __import__('jax').numpy.asarray(drawn.astype(out[name].dtype))
    for name, factor in factors.items():
        out[name] = (out[name] * factor).astype(out[name].dtype)
    return out
```

```python
from contextlib import ExitStack, contextmanager

import concourse.bass as bass
from concourse import mybir

F32 = mybir.dt.float32
F32R = mybir.dt.float32r
BF16 = mybir.dt.bfloat16
ALU = mybir.AluOpType
ACT = mybir.ActivationFunctionType

P = 128
D = 1024
KD = D // P
TP = 1024
NSEQ, NEW = 8, 8
TS = NSEQ * NEW
T = TP + TS
NT = TP // P
PAGE = 128
NPAGE = 8
HEADS, HD = 8, 64
SB = HEADS * HD
GH, GK, GV = 4, 64, 128
RANK = 16
IN_W = 3 * SB + 2 * GH * GK + 2 * GH * GV + RANK
FF = 4096
EPS = 1e-6
GATE = 1.0 / 16.0
NEG = -1e30
BIG = 3e38
PANEL = 256
NMOD = 1 + NSEQ
CHUNKS = [(0, 384), (384, 384), (768, 320)]
SUB = 32
ROW_Q, ROW_K, ROW_V = 0, SB, 2 * SB
ROW_QG = 3 * SB
ROW_KG = ROW_QG + GH * GK
ROW_VG = ROW_KG + GH * GK
ROW_RG = ROW_VG + GH * GV
ROW_A = ROW_RG + GH * GV
LAST = IN_W - P
SH1, SC1, GA1, SH2, SC2, GA2 = range(6)


class Program:

    def __init__(self, nc, io, ctx):
        self.nc, self.io, self.ctx = nc, io, ctx
        self.bank = [ctx.enter_context(nc.psum_tensor(f"bank{i}", [P, 512], F32)) for i in range(8)]
        self.ident = self.sb("ident", [P, P])
        self.ident16 = self.sb("ident16", [P, P], BF16)
        self.causal16 = self.sb("causal16", [P, P], BF16)
        self.modT = self.sb("modT", [P, 6 * KD, NMOD])
        self.vecT = self.sb("vecT", [P, 19])
        self.mul1 = self.sb("mul1", [P, KD, NMOD])
        self.mul2 = self.sb("mul2", [P, KD, NMOD])
        self.eps = self.sb("eps", [P, 1])
        self.projT = nc.dram_tensor("projT", [IN_W, T], F32, kind="Internal").ap()
        self.vgnat = nc.dram_tensor("vgnat", [T, GH * GV], F32, kind="Internal").ap()

    def sb(self, name, shape, dt=F32, ctx=None):
        return (ctx or self.ctx).enter_context(self.nc.sbuf_tensor(name, shape, dt))

    def sem(self, name):
        return self.nc.alloc_semaphore(name=name)

    @contextmanager
    def part(self):
        before = self.nc.snapshot_sems()
        yield
        self.nc.clear_and_free_semaphores(self.nc.allocated_since(before))
        self.nc.all_engine_barrier()

    def mod(self, part, kc, row=0):
        return self.modT[:, part * KD + kc, row:row + 1]


def stage_constants_and_adaln(g):
    nc, io = g.nc, g.io
    NCH = 6 * D // 512
    SLOTS = 3
    with ExitStack() as ctx:
        sb = lambda *a: g.sb(*a, ctx=ctx)
        c_in = sb("ada_c", [NMOD, D])
        c_e = sb("ada_e", [NMOD, D])
        cT = sb("ada_cT", [P, KD, NMOD])
        w = [sb(f"ada_w{i}", [P, KD, 512]) for i in range(SLOTS)]
        bias = sb("ada_bias", [NMOD, 6 * D])
        mod = sb("ada_mod", [NMOD, 6 * D])
        vec = sb("ada_vec", [19, P])
        s_small = g.sem("ada_small_loaded")
        s_w = [g.sem(f"ada_w{i}_loaded") for i in range(SLOTS)]
        s_const = g.sem("ada_const")
        s_e = g.sem("ada_exp")
        s_silu = g.sem("ada_silu")
        s_cT = g.sem("ada_cT_psum")
        s_cTs = g.sem("ada_cT_sbuf")
        s_mm = g.sem("ada_chunk_summed")
        s_ev = g.sem("ada_chunk_evacuated")
        s_mT = g.sem("ada_modT_psum")
        s_mTs = g.sem("ada_modT_sbuf")
        with nc.Block() as block:
            @block.sync
            def _(sp):
                sp.dma_start(c_in[0:1, :], io["c_prompt"]).then_inc(s_small, 16)
                sp.dma_start(c_in[1:NMOD, :], io["c_sample"]).then_inc(s_small, 16)
                sp.dma_start(vec[0:8, :], io["g_mix"].rearrange("a (k p) -> (a k) p", p=P)).then_inc(s_small, 16)
                sp.dma_start(vec[8:16, :], io["g_ffn"].rearrange("a (k p) -> (a k) p", p=P)).then_inc(s_small, 16)
                sp.dma_start(vec[16:18, :], io["b_gla_gate"].rearrange("a (k p) -> (a k) p", p=P)).then_inc(s_small, 16)
                sp.dma_start(vec[18:19, :], io["g_gla_out"]).then_inc(s_small, 16)
                sp.dma_start(bias[:, :], io["b_ada"].to_broadcast([NMOD, 6 * D])).then_inc(s_small, 16)
                with sp.Fori(0, NCH // SLOTS) as n:
                    for s in range(SLOTS):
                        sp.wait_ge(s_mm, n * SLOTS + s + 1)
                        src = io["w_ada"][0][:, bass.ds((n * SLOTS + s) * 512, 512)]
                        sp.dma_start(w[s][:], src.rearrange("(k p) c -> p k c", p=P)).then_inc(s_w[s], 16)

            @block.gpsimd
            def _(pool):
                pool.memset(g.ident[:], 0.0).then_inc(s_const, 1)
                pool.memset(g.causal16[:], NEG).then_inc(s_const, 1)
                pool.wait_ge(s_const, 2)
                pool.affine_select(out=g.ident[:], in_=g.ident[:], compare_op=ALU.not_equal, fill=1.0,
                                   base=0, pattern=[[-1, P]], channel_multiplier=1).then_inc(s_const, 1)
                pool.affine_select(out=g.causal16[:], in_=g.causal16[:], compare_op=ALU.is_ge, fill=0.0,
                                   base=0, pattern=[[1, P]], channel_multiplier=-1).then_inc(s_const, 1)
                pool.wait_ge(s_const, 4)
                pool.tensor_copy(g.ident16[:], g.ident[:]).then_inc(s_const, 1)

            @block.scalar
            def _(act):
                act.preload_act_table_set("natural_log_exp_and_others")
                act.wait_ge(s_small, 7 * 16)
                act.activation(c_e[:], c_in[:], ACT.Exp, scale=-1.0).then_inc(s_e, 1)

            @block.vector
            def _(dve):
                dve.memset(g.eps[:], EPS)
                dve.wait_ge(s_e, 1)
                dve.tensor_scalar(c_e[:], c_e[:], 1.0, None, ALU.add).then_inc(s_silu, 1)
                dve.wait_ge(s_silu, 1)
                dve.reciprocal(c_e[:], c_e[:]).then_inc(s_silu, 1)
                dve.wait_ge(s_silu, 2)
                dve.tensor_tensor(c_e[:], c_in[:], c_e[:], ALU.mult).then_inc(s_silu, 1)
                dve.wait_ge(s_cT, 1)
                dve.tensor_copy(cT[:].rearrange("p k r -> p (k r)"), g.bank[7][:, 0:KD * NMOD]).then_inc(s_cTs, 1)
                dve.tensor_copy(g.vecT[:], g.bank[6][:, 0:19]).then_inc(s_cTs, 1)
                with dve.Fori(0, NCH // SLOTS) as n:
                    for s in range(SLOTS):
                        dve.wait_ge(s_mm, SLOTS + n * SLOTS + s + 1)
                        cols = bass.ds((n * SLOTS + s) * 512, 512)
                        dve.tensor_tensor(mod[:, cols], g.bank[s][0:NMOD, :], bias[:, cols], ALU.add).then_inc(s_ev, 1)
                dve.wait_ge(s_mT, 1)
                dve.tensor_copy(g.modT[:].rearrange("p m r -> p (m r)"), g.bank[7][:, 0:6 * KD * NMOD]).then_inc(s_mTs, 1)
                dve.wait_ge(s_mTs, 1)
                for mul, part, at in ((g.mul1, SC1, 0), (g.mul2, SC2, KD)):
                    gain = g.vecT[:, at:at + KD].rearrange("p (k o) -> p k o", o=1).to_broadcast([P, KD, NMOD])
                    dve.scalar_tensor_tensor(out=mul[:], in0=g.modT[:, part * KD:(part + 1) * KD, :], scalar=1.0,
                                             in1=gain, op0=ALU.add, op1=ALU.mult)

            @block.tensor
            def _(pe):
                pe.sem_inc(s_mm, SLOTS)
                pe.wait_ge(s_silu, 3)
                pe.wait_ge(s_const, 5)
                for k in range(KD):
                    pe.transpose(g.bank[7][:, k * NMOD:(k + 1) * NMOD], c_e[:, k * P:(k + 1) * P], g.ident[0:NMOD, 0:NMOD])
                pe.transpose(g.bank[6][:, 0:19], vec[:], g.ident[0:19, 0:19]).then_inc(s_cT, 1)
                pe.wait_ge(s_cTs, 2)
                pe.sem_inc(s_ev, SLOTS)
                with pe.Fori(0, NCH // SLOTS) as n:
                    for s in range(SLOTS):
                        pe.wait_ge(s_w[s], n * 16 + 16)
                        pe.wait_ge(s_ev, n * SLOTS + s + 1)
                        for k in range(KD):
                            last = pe.matmul(g.bank[s][0:NMOD, :], cT[:, k, :], w[s][:, k, :],
                                             start=(k == 0), stop=(k == KD - 1))
                        last.then_inc(s_mm, 1)
                pe.wait_ge(s_ev, SLOTS + NCH)
                for m in range(6 * KD):
                    last = pe.transpose(g.bank[7][:, m * NMOD:(m + 1) * NMOD], mod[:, m * P:(m + 1) * P],
                                        g.ident[0:NMOD, 0:NMOD])
                last.then_inc(s_mT, 1)


def stage_norm_mix(g, hT_hi, hT_lo):
    nc, io = g.nc, g.io
    GROUPS = [(0, 4), (4, 4), (8, 1)]
    xp = io["x_prompt"][0]
    xs = io["x_sample"].rearrange("s t d -> (s t) d")
    with ExitStack() as ctx:
        sb = lambda *a: g.sb(*a, ctx=ctx)
        x = [sb(f"n1_x{i}", [P, D]) for i in range(9)]
        sq = sb("n1_sq", [P, D])
        ss = sb("n1_ss", [P, 9])
        tmp = [sb(f"n1_tmp{i}", [P, 512]) for i in range(2)]
        s_x = [g.sem(f"n1_x{i}_loaded") for i in range(9)]
        s_ss = g.sem("n1_sumsq")
        s_ln = g.sem("n1_ln")
        s_rstd = g.sem("n1_rstd")
        s_xn = g.sem("n1_normed")
        s_tr = g.sem("n1_transposed")
        s_tmp = g.sem("n1_modulated")
        s_dtmp = g.sem("n1_sample_scaled")
        s_hi = g.sem("n1_hi")
        s_lo = g.sem("n1_lo")
        steps = [(gi, t0, n, k) for gi, (t0, n) in enumerate(GROUPS) for k in range(KD)]
        NB = 4
        with nc.Block() as block:
            @block.sync
            def _(sp):
                for i in range(9):
                    src = xp[i * P:(i + 1) * P, :] if i < 8 else xs
                    sp.dma_start(x[i][0:src.shape[0], :], src).then_inc(s_x[i], 16)

            @block.scalar
            def _(act):
                for i in range(9):
                    n = P if i < 8 else TS
                    act.wait_ge(s_x[i], 16)
                    act.activation(sq[0:n, :], x[i][0:n, :], ACT.Square, accum_out=ss[0:n, i:i + 1]).then_inc(s_ss, 1)
                    act.wait_ge(s_ss, i + 1)
                    act.activation(ss[0:n, i:i + 1], ss[0:n, i:i + 1], ACT.Ln, scale=1.0 / D, bias=g.eps[0:n, :]).then_inc(s_ln, 1)
                    act.wait_ge(s_ln, i + 1)
                    act.activation(ss[0:n, i:i + 1], ss[0:n, i:i + 1], ACT.Exp, scale=-0.5).then_inc(s_rstd, 1)
                for j, (gi, t0, n, k) in enumerate(steps):
                    if n == 1:
                        continue
                    act.wait_ge(s_tr, j + 1)
                    if j >= 2:
                        act.wait_ge(s_lo, j - 1)
                    act.activation(tmp[j % 2][:], g.bank[j % NB][:], ACT.Identity, scale=g.mul1[:, k, 0:1],
                                   bias=g.mod(SH1, k)).then_inc(s_tmp, 1)

            @block.gpsimd
            def _(pool):
                for j, (gi, t0, n, k) in enumerate(steps):
                    w = 512 if n > 1 else TS
                    if n > 1:
                        pool.wait_ge(s_tmp, j + 1)
                    else:
                        pool.wait_ge(s_dtmp, 2 * (j - 16) + 2)
                    pool.tensor_copy(hT_hi[:, k, t0 * P:t0 * P + w], tmp[j % 2][:, 0:w]).then_inc(s_hi, 1)

            @block.vector
            def _(dve):
                for i in range(9):
                    n = P if i < 8 else TS
                    dve.wait_ge(s_rstd, i + 1)
                    dve.tensor_scalar(x[i][0:n, :], x[i][0:n, :], ss[0:n, i:i + 1], None, ALU.mult).then_inc(s_xn, 1)
                for j, (gi, t0, n, k) in enumerate(steps):
                    w = 512 if n > 1 else TS
                    if n == 1:
                        dve.wait_ge(s_tr, j + 1)
                        v = tmp[j % 2][:, 0:TS].rearrange("p (s t) -> p s t", s=NSEQ)
                        src = g.bank[j % NB][:, 0:TS].rearrange("p (s t) -> p s t", s=NSEQ)
                        row = lambda a: a.rearrange("p (s o) -> p s o", o=1).to_broadcast([P, NSEQ, NEW])
                        if j >= 2:
                            dve.wait_ge(s_lo, j - 1)
                        dve.tensor_tensor(v, src, row(g.mul1[:, k, 1:NMOD]), ALU.mult).then_inc(s_dtmp, 1)
                        dve.wait_ge(s_dtmp, 2 * (j - 16) + 1)
                        dve.tensor_tensor(v, v, row(g.modT[:, SH1 * KD + k, 1:NMOD]), ALU.add).then_inc(s_dtmp, 1)
                    dve.wait_ge(s_hi, j + 1)
                    dve.tensor_tensor(hT_lo[:, k, t0 * P:t0 * P + w], tmp[j % 2][:, 0:w],
                                      hT_hi[:, k, t0 * P:t0 * P + w], ALU.subtract).then_inc(s_lo, 1)

            @block.tensor
            def _(pe):
                for j, (gi, t0, n, k) in enumerate(steps):
                    pe.wait_ge(s_xn, t0 + n)
                    if j >= NB:
                        pe.wait_ge(s_lo, j - NB + 1)
                    for i in range(n):
                        m = P if n > 1 else TS
                        last = pe.transpose(g.bank[j % NB][:, i * P:i * P + m], x[t0 + i][0:m, k * P:(k + 1) * P],
                                            g.ident[0:m, 0:m])
                    last.then_inc(s_tr, 1)


class Panels:

    def __init__(self, g, ctx, tag):
        self.raw = [g.sb(f"{tag}_raw{i}", [P, KD, PANEL], ctx=ctx) for i in range(2)]
        self.hi = [g.sb(f"{tag}_hi{i}", [P, KD, PANEL], F32R, ctx=ctx) for i in range(2)]
        self.lo = [g.sb(f"{tag}_lo{i}", [P, KD, PANEL], F32R, ctx=ctx) for i in range(2)]
        self.loaded = [g.sem(f"{tag}_raw{i}_loaded") for i in range(2)]
        self.hi_done = g.sem(f"{tag}_hi_done")
        self.lo_done = g.sem(f"{tag}_lo_done")


def three_products(pe, out, w_hi, w_lo, x_hi, x_lo, k, nk):
    pe.matmul(out, w_hi, x_hi, start=(k == 0), stop=False)
    pe.matmul(out, w_hi, x_lo, start=False, stop=False)
    return pe.matmul(out, w_lo, x_hi, start=False, stop=(k == nk - 1))


def stage_project_in(g, hT_hi, hT_lo):
    nc, io = g.nc, g.io
    w_in = io["w_in"][0]
    NP = LAST // PANEL + 1
    assert NP == 12 and LAST > (NP - 1) * PANEL
    with ExitStack() as ctx:
        w = Panels(g, ctx, "in")
        stg = [g.sb(f"in_stage{i}", [P, T], ctx=ctx) for i in range(4)]
        s_mm = g.sem("in_group_summed")
        s_aev = g.sem("in_act_evacuated")
        s_dev = g.sem("in_dve_evacuated")
        s_out = [g.sem(f"in_stage{i}_stored") for i in range(4)]
        last_w = slice(0, P)
        with nc.Block() as block:
            @block.sync
            def _(sp):
                def load(s, cols, n):
                    src = w_in[:, cols].rearrange("(k p) c -> p k c", p=P)
                    sp.dma_start(w.raw[s][:, :, 0:n], src).then_inc(w.loaded[s], 16)

                with sp.Fori(0, NP // 2) as n:
                    for s in range(2):
                        sp.wait_ge(w.lo_done, n * 2 + s + 1)
                        load(s, bass.ds((n * 2 + s) * PANEL, PANEL), PANEL)
                sp.wait_ge(w.lo_done, NP + 1)
                load(0, slice(LAST, IN_W), P)

            @block.gpsimd
            def _(pool):
                pool.sem_inc(w.lo_done, 2)
                with pool.Fori(0, NP // 2) as n:
                    for s in range(2):
                        pool.wait_ge(w.hi_done, n * 2 + s + 1)
                        pool.tensor_tensor(w.lo[s][:], w.raw[s][:], w.hi[s][:], ALU.subtract).then_inc(w.lo_done, 1)
                pool.wait_ge(w.hi_done, NP + 1)
                pool.tensor_tensor(w.lo[0][:, :, last_w], w.raw[0][:, :, last_w], w.hi[0][:, :, last_w],
                                   ALU.subtract).then_inc(w.lo_done, 1)

            @block.tensor
            def _(pe):
                pe.sem_inc(s_mm, 12)

                def groups(s, n, tiles):
                    for m in range(tiles):
                        for c, (t0, tw) in enumerate(CHUNKS):
                            gi = m * 3 + c
                            pe.wait_ge(s_dev if gi % 2 else s_aev, n * 6 + s * 3 + gi // 2 + 1)
                            for k in range(KD):
                                cols = slice(m * P, (m + 1) * P)
                                last = three_products(pe, g.bank[gi][:, 0:tw], w.hi[s][:, k, cols], w.lo[s][:, k, cols],
                                                      hT_hi[:, k, t0:t0 + tw], hT_lo[:, k, t0:t0 + tw], k, KD)
                            last.then_inc(s_mm, 1)

                with pe.Fori(0, NP // 2) as n:
                    for s in range(2):
                        pe.wait_ge(w.lo_done, 2 + n * 2 + s + 1)
                        groups(s, n, 2)
                pe.wait_ge(w.lo_done, 2 + NP + 1)
                groups(0, NP // 2, 1)

            def evacuate(eng, copy, mine, s_ev, prime):
                if prime:
                    eng.sem_inc(s_ev, 3)

                def groups(s, n, tiles):
                    for gi in range(3 * tiles):
                        if gi % 2 != mine:
                            continue
                        m, c = divmod(gi, 3)
                        t0, tw = CHUNKS[c]
                        st = 2 * s + m
                        eng.wait_ge(s_mm, 12 + n * 12 + s * 6 + gi + 1)
                        eng.wait_ge(s_out[st], n * 16 + 16)
                        copy(stg[st][:, t0:t0 + tw], g.bank[gi][:, 0:tw]).then_inc(s_ev, 1)

                with eng.Fori(0, NP // 2) as n:
                    for s in range(2):
                        groups(s, n, 2)
                groups(0, NP // 2, 1)

            @block.vector
            def _(dve):
                evacuate(dve, dve.tensor_copy, 1, s_dev, True)

            @block.scalar
            def _(act):
                for i in range(4):
                    act.sem_inc(s_out[i], 16)
                act.sem_inc(s_aev, 3)

                def groups(s, n, tiles):
                    for gi in range(3 * tiles):
                        m, c = divmod(gi, 3)
                        t0, tw = CHUNKS[c]
                        st = 2 * s + m
                        if gi % 2 == 0:
                            act.wait_ge(s_mm, 12 + n * 12 + s * 6 + gi + 1)
                            act.wait_ge(s_out[st], n * 16 + 16)
                            act.copy(stg[st][:, t0:t0 + tw], g.bank[gi][:, 0:tw]).then_inc(s_aev, 1)
                        if c == 2:
                            act.wait_ge(s_aev, 3 + n * 6 + s * 3 + (gi // 2 + 1))
                            act.wait_ge(s_dev, 3 + n * 6 + s * 3 + (gi + 1) // 2)
                            if tiles == 2:
                                dst, src = g.projT[bass.ds((n * 4 + st) * P, P), :], stg[st][:]
                            else:
                                dst, src = g.projT[ROW_A:IN_W, :], stg[st][P - RANK:P, :]
                            act.dma_start(dst, src).then_inc(s_out[st], 16)

                def round_hi(s, n, cols):
                    act.wait_ge(w.loaded[s], n * 16 + 16)
                    act.wait_ge(s_mm, n * 12 + s * 6 + 6)
                    act.copy(w.hi[s][:, :, cols], w.raw[s][:, :, cols]).then_inc(w.hi_done, 1)

                round_hi(0, 0, slice(0, PANEL))
                with act.Fori(0, NP // 2 - 1) as n:
                    round_hi(1, n, slice(0, PANEL))
                    groups(0, n, 2)
                    round_hi(0, n + 1, slice(0, PANEL))
                    groups(1, n, 2)
                round_hi(1, NP // 2 - 1, slice(0, PANEL))
                groups(0, NP // 2 - 1, 2)
                round_hi(0, NP // 2, last_w)
                groups(1, NP // 2 - 1, 2)
                groups(0, NP // 2, 1)
                act.wait_ge(s_out[0], 16 * (NP // 2 + 2))
                for i in range(1, 4):
                    act.wait_ge(s_out[i], 16 * (NP // 2 + 1))


def stage_natural(g):
    nc, io = g.nc, g.io
    kinds = [(ROW_K, "k"), (ROW_V, "v"), (ROW_VG, "vg")]
    steps = [(a, tt) for a in range(3) for tt in range(NT + 1)]
    NB = 6
    with ExitStack() as ctx:
        src = [g.sb(f"nat_src{i}", [P, 4, T], ctx=ctx) for i in range(3)]
        knat = g.sb("nat_k", [P, NT + 1, SB], ctx=ctx)
        vgn = g.sb("nat_vg", [P, NT + 1, GH * GV], ctx=ctx)
        dst = [knat, g.vnat, vgn]
        stores = [(io[n + "_prompt"].rearrange("l b (n p) h d -> p (l b n) (h d)", p=P),
                   io[n + "_sample"].rearrange("l s t h d -> (l s t) (h d)")) for n in ("k", "v")]
        stores += [(g.vgnat[0:TP].rearrange("(n p) c -> p n c", p=P), g.vgnat[TP:T])]
        s_src = [g.sem(f"nat_src{i}_loaded") for i in range(3)]
        s_tr = g.sem("nat_transposed")
        s_act = g.sem("nat_act_copied")
        s_dve = g.sem("nat_dve_copied")
        s_out = g.sem("nat_stored")
        with nc.Block() as block:
            @block.sync
            def _(sp):
                for a, (row, _) in enumerate(kinds):
                    sp.dma_start(src[a][:], g.projT[row:row + SB, :].rearrange("(m p) t -> p m t", p=P)).then_inc(s_src[a], 16)
                for a, outs in enumerate(stores):
                    n = (a + 1) * (NT + 1)
                    sp.wait_ge(s_act, (n + 1) // 2)
                    sp.wait_ge(s_dve, n // 2)
                    sp.dma_start(outs[0], dst[a][:, 0:NT, :]).then_inc(s_out, 16)
                    sp.dma_start(outs[1], dst[a][0:TS, NT, :]).then_inc(s_out, 16)
                sp.wait_ge(s_out, 6 * 16)

            @block.tensor
            def _(pe):
                for j, (a, tt) in enumerate(steps):
                    m = P if tt < NT else TS
                    if tt == 0:
                        pe.wait_ge(s_src[a], 16)
                    if j >= NB:
                        pe.wait_ge(s_dve if j % 2 else s_act, (j - NB) // 2 + 1)
                    for f in range(4):
                        last = pe.transpose(g.bank[j % NB][0:m, f * P:(f + 1) * P], src[a][:, f, tt * P:tt * P + m], g.ident[:])
                    last.then_inc(s_tr, 1)

            def copies(eng, copy, s_done, mine):
                for j, (a, tt) in enumerate(steps):
                    if j % 2 == mine:
                        m = P if tt < NT else TS
                        eng.wait_ge(s_tr, j + 1)
                        copy(dst[a][0:m, tt, :], g.bank[j % NB][0:m, :]).then_inc(s_done, 1)

            @block.scalar
            def _(act):
                copies(act, act.copy, s_act, 0)

            @block.vector
            def _(dve):
                copies(dve, dve.tensor_copy, s_dve, 1)


def at_least(eng, sem, value):
    if not isinstance(value, int) or value > 0:
        eng.wait_ge(sem, value)


def stage_sample_attention(g):
    nc, io = g.nc, g.io
    NCOL = HEADS * NEW
    with ExitStack() as ctx:
        sb = lambda *a: g.sb(*a, ctx=ctx)
        kpg = [sb(f"sa_k{i}", [P, NPAGE, SB]) for i in range(2)]
        vpg = [sb(f"sa_v{i}", [P, NPAGE, SB]) for i in range(2)]
        kT = sb("sa_kT", [P, NPAGE, 4, P])
        qnew = sb("sa_qnew", [P, 4, TS])
        knew = sb("sa_knew", [P, 4, TS])
        qbd = sb("sa_qbd", [P, 4, NSEQ, 2, NEW])
        table = ctx.enter_context(nc.sbuf_tensor("sa_table", [1, NSEQ * NPAGE], mybir.dt.int32))
        bsb = sb("sa_bsb", [1, HEADS])
        brow = sb("sa_brow", [1, NPAGE, HEADS, NEW])
        ones = sb("sa_ones", [1, P])
        negtri = sb("sa_negtri", [P, P])
        negone = sb("sa_negone", [P, P])
        mask16 = sb("sa_mask16", [TS, NSEQ, HEADS, NEW], BF16)
        spn = sb("sa_spn", [P, NSEQ, NCOL])
        wn = sb("sa_wn", [TS, NSEQ, NCOL])
        a = sb("sa_a", [P, 512])
        sp_ = sb("sa_sp", [P, NPAGE, NCOL])
        r = sb("sa_r", [P, NPAGE, NCOL])
        w = [sb(f"sa_w{i}", [P, 512]) for i in range(2)]
        o = sb("sa_o", [P, 4, NSEQ, NEW])
        s_in = g.sem("sa_inputs_loaded")
        s_tab = g.sem("sa_table_loaded")
        s_k = [g.sem(f"sa_k{i}_loaded") for i in range(2)]
        s_v = [g.sem(f"sa_v{i}_loaded") for i in range(2)]
        s_c = g.sem("sa_constants")
        s_cd = g.sem("sa_dve_constants")
        s_kt = g.sem("sa_k_transposed")
        s_kta = g.sem("sa_kT_act_copied")
        s_ktd = g.sem("sa_kT_dve_copied")
        s_qk = g.sem("sa_scored")
        s_zn = g.sem("sa_new_scored")
        s_act = g.sem("sa_act_chain")
        s_sp = g.sem("sa_softplus")
        s_r = g.sem("sa_later_pages_summed")
        s_sum = g.sem("sa_stay_subtracted")
        s_w = g.sem("sa_weights")
        s_pv = g.sem("sa_v_multiplied")
        s_o = g.sem("sa_out")
        O, ZN = g.bank[6], g.bank[7]
        Z = [g.bank[4], g.bank[5]]

        def sequences(eng, step):
            step(0, 0)
            with eng.Fori(0, NSEQ // 2 - 1) as n:
                step(n * 2 + 1, 1)
                step(n * 2 + 2, 0)
            step(NSEQ - 1, 1)

        with nc.Block() as block:
            @block.sync
            def _(sp):
                sp.dma_start(table[:], io["page_table"].rearrange("s (o n) -> o (s n)", o=1)).then_inc(s_tab, 16)
                for t, row in ((qnew, ROW_Q), (knew, ROW_K)):
                    sp.dma_start(t[:], g.projT[row:row + SB, TP:T].rearrange("(m p) t -> p m t", p=P)).then_inc(s_in, 16)
                sp.dma_start(bsb[:], io["b_sb"]).then_inc(s_in, 16)
                sp.wait_ge(s_tab, 16)
                kc = io["cache_k"][0].rearrange("n p h d -> n p (h d)")
                vc = io["cache_v"][0].rearrange("n p h d -> n p (h d)")

                def step(s, slot):
                    page = [sp.value_load(table[0:1, bass.ds(s * NPAGE + j, 1)], min_val=0, max_val=kc.shape[0] - 1)
                            for j in range(NPAGE)]
                    at_least(sp, s_kt, (s - 2) * NPAGE + NPAGE)
                    for j in range(NPAGE):
                        sp.dma_start(kpg[slot][:, j, :], kc[bass.ds(page[j], 1)].rearrange("o p d -> (o p) d")).then_inc(s_k[slot], 16)
                    at_least(sp, s_pv, s - 1)
                    for j in range(NPAGE):
                        sp.dma_start(vpg[slot][:, j, :], vc[bass.ds(page[j], 1)].rearrange("o p d -> (o p) d")).then_inc(s_v[slot], 16)

                sequences(sp, step)

            @block.gpsimd
            def _(pool):
                pool.memset(qbd[:], 0.0).then_inc(s_c, 1)
                pool.memset(spn[:], 0.0).then_inc(s_c, 1)
                pool.memset(ones[:], 1.0).then_inc(s_c, 1)
                pool.memset(negone[:], -1.0).then_inc(s_c, 1)
                pool.memset(negtri[:], -1.0).then_inc(s_c, 1)
                pool.memset(mask16[:], 0.0).then_inc(s_c, 1)
                pool.wait_ge(s_c, 6)
                pool.affine_select(out=negtri[:], in_=negtri[:], compare_op=ALU.is_ge, fill=0.0, base=0,
                                   pattern=[[-1, P]], channel_multiplier=1).then_inc(s_c, 1)
                pool.affine_select(out=mask16[:], in_=mask16[:], compare_op=ALU.is_ge, fill=NEG, base=0,
                                   pattern=[[-NEW, NSEQ], [0, HEADS], [0, NEW]], channel_multiplier=1).then_inc(s_c, 1)
                pool.wait_ge(s_c, 8)
                pool.affine_select(out=mask16[:], in_=mask16[:], compare_op=ALU.is_gt, fill=NEG, base=0,
                                   pattern=[[NEW, NSEQ], [0, HEADS], [1, NEW]], channel_multiplier=-1).then_inc(s_c, 1)

            @block.tensor
            def _(pe):
                pe.wait_ge(s_in, 48)
                pe.wait_ge(s_c, 9)
                pe.wait_ge(s_cd, 3)
                bias = brow[:].rearrange("o j h q -> o (j h q)")
                pe.matmul(ZN[0:TS, :], ones[:, 0:TS], bias, start=True, stop=False, skip_group_check=True)
                zn = ZN[0:TS, :].rearrange("k (s p c) -> k p s c", s=NSEQ, p=4)
                for p in range(4):
                    pe.matmul(zn[:, p], knew[:, p, :], qbd[:, p].rearrange("k s h q -> k s (h q)"),
                              start=False, stop=False, skip_group_check=True)
                pe.matmul(ZN[0:TS, :], g.ident16[0:TS, 0:TS], mask16[:].rearrange("p s h q -> p (s h q)"),
                          start=False, stop=True, skip_group_check=True).then_inc(s_zn, 1)
                pe.wait_ge(s_sp, 1)
                pe.matmul(ZN[0:TS, :], negtri[0:TS, 0:TS], spn[0:TS].rearrange("k s c -> k (s c)"),
                          start=False, stop=True, skip_group_check=True).then_inc(s_zn, 1)
                pe.wait_ge(s_w, 1)
                ov = O[:].rearrange("d (s p c) -> d p s c", s=NSEQ, p=4)
                wv = wn[:].rearrange("k s (p c) -> k p s c", p=4)
                for p in range(4):
                    pe.matmul(ov[:, p], g.vnat[0:TS, NT, p * P:(p + 1) * P], wv[:, p],
                              start=(p == 0), stop=False, skip_group_check=True)

                def score(s, slot):
                    at_least(pe, s_w, s)
                    pe.wait_ge(s_k[slot], ((s - slot) // 2 if isinstance(s, int) else s_half(s, slot)) * 128 + 128)
                    pe.matmul(Z[slot][:], ones[:], bias, start=True, stop=False, skip_group_check=True)
                    for j in range(NPAGE + 1):
                        if j < NPAGE:
                            at_least(pe, s_ktd if j % 2 else s_kta, s * 4 + j // 2 - 1)
                            for p in range(4):
                                last = pe.transpose(g.bank[j % 4][:, p * P:(p + 1) * P], kpg[slot][:, j, p * P:(p + 1) * P], g.ident[:])
                            last.then_inc(s_kt, 1)
                        if j > 0:
                            i = j - 1
                            pe.wait_ge(s_ktd if i % 2 else s_kta, s * 4 + i // 2 + 1)
                            for p in range(4):
                                c = i * NCOL + p * 16
                                q = qbd[:, p].rearrange("k s h q -> k (s h q)")
                                last = pe.matmul(Z[slot][:, c:c + 16], kT[:, i, p, :], q[:, bass.ds(s * 16, 16)],
                                                 start=False, stop=(i == NPAGE - 1), skip_group_check=True)
                            last.then_inc(s_qk, 1)

                def subtract(s, slot):
                    pe.wait_ge(s_r, s * 8 + 8)
                    pe.matmul(Z[slot][:], negtri[:], sp_[:].rearrange("k j c -> k (j c)"), start=False, stop=False, skip_group_check=True)
                    pe.matmul(Z[slot][:], negone[:], r[:].rearrange("k j c -> k (j c)"), start=False, stop=True,
                              skip_group_check=True).then_inc(s_sum, 1)

                def values(s, slot):
                    pe.wait_ge(s_w, s + 2)
                    pe.wait_ge(s_v[slot], ((s - slot) // 2 if isinstance(s, int) else s_half(s, slot)) * 128 + 128)
                    for j in range(NPAGE):
                        for p in range(4):
                            c = j * NCOL + p * 16
                            last = pe.matmul(O[:, bass.ds(s * NCOL + p * 16, 16)], vpg[slot][:, j, p * P:(p + 1) * P],
                                             w[slot][:, c:c + 16], start=False, stop=(j == NPAGE - 1), skip_group_check=True)
                    last.then_inc(s_pv, 1)

                score(0, 0)
                subtract(0, 0)
                with pe.Fori(0, NSEQ // 2 - 1) as n:
                    s_half = lambda s, slot: n + (0 if slot else 1)
                    score(n * 2 + 1, 1)
                    s_half = lambda s, slot: n
                    values(n * 2, 0)
                    subtract(n * 2 + 1, 1)
                    s_half = lambda s, slot: n + 1
                    score(n * 2 + 2, 0)
                    s_half = lambda s, slot: n
                    values(n * 2 + 1, 1)
                    subtract(n * 2 + 2, 0)
                score(NSEQ - 1, 1)
                values(NSEQ - 2, 0)
                subtract(NSEQ - 1, 1)
                values(NSEQ - 1, 1)

            @block.scalar
            def _(act):
                def chain(z, out, i):
                    act.activation(out, z, ACT.Abs).then_inc(s_act, 1)
                    act.wait_ge(s_act, i * 3 + 1)
                    act.activation(out, out, ACT.Exp, scale=-1.0).then_inc(s_act, 1)
                    act.wait_ge(s_act, i * 3 + 2)
                    act.activation(out, out, ACT.Ln, bias=1.0).then_inc(s_act, 1)

                act.wait_ge(s_zn, 1)
                chain(ZN[0:TS, :], a[0:TS, :], 0)
                act.wait_ge(s_zn, 2)
                act.activation(wn[:].rearrange("k s c -> k (s c)"), ZN[0:TS, :], ACT.Exp).then_inc(s_w, 1)

                def step(s, slot):
                    for j in range(0, NPAGE, 2):
                        act.wait_ge(s_kt, s * NPAGE + j + 1)
                        at_least(act, s_qk, (s - 1) * NPAGE + j + 1)
                        act.copy(kT[:, j].rearrange("k p c -> k (p c)"), g.bank[j % 4][:]).then_inc(s_kta, 1)
                    act.wait_ge(s_qk, s * NPAGE + NPAGE)
                    act.wait_ge(s_sp, s + 1)
                    chain(Z[slot][:], a[:], s + 1)
                    at_least(act, s_pv, s - 1)
                    act.wait_ge(s_sum, s + 1)
                    act.activation(w[slot][:], Z[slot][:], ACT.Exp).then_inc(s_w, 1)

                sequences(act, step)

            @block.vector
            def _(dve):
                dve.wait_ge(s_in, 48)
                dve.wait_ge(s_c, 2)
                b = bsb[:].rearrange("o (j h q) -> o j h q", j=1, q=1).to_broadcast([1, NPAGE, HEADS, NEW])
                dve.tensor_copy(brow[:], b).then_inc(s_cd, 1)
                for h in range(2):
                    rows = slice(h * HD, (h + 1) * HD)
                    src = qnew[rows].rearrange("k p (s q) -> k p s q", s=NSEQ)
                    dve.tensor_scalar(qbd[rows, :, :, h, :], src, HD ** -0.5, None, ALU.mult).then_inc(s_cd, 1)
                dve.wait_ge(s_act, 3)
                dve.scalar_tensor_tensor(out=spn[0:TS].rearrange("k s c -> k (s c)"), in0=ZN[0:TS, :], scalar=0.0,
                                         in1=a[0:TS, :], op0=ALU.max, op1=ALU.add).then_inc(s_sp, 1)

                def step(s, slot):
                    for j in range(1, NPAGE, 2):
                        dve.wait_ge(s_kt, s * NPAGE + j + 1)
                        at_least(dve, s_qk, (s - 1) * NPAGE + j + 1)
                        dve.tensor_copy(kT[:, j].rearrange("k p c -> k (p c)"), g.bank[j % 4][:]).then_inc(s_ktd, 1)
                    dve.wait_ge(s_act, (s + 1) * 3 + 3)
                    at_least(dve, s_sum, s)
                    dve.scalar_tensor_tensor(out=sp_[:].rearrange("k j c -> k (j c)"), in0=Z[slot][:], scalar=0.0,
                                             in1=a[:], op0=ALU.max, op1=ALU.add).then_inc(s_sp, 1)
                    spn_s = spn[:].rearrange("k s c -> k (s c)")[:, bass.ds(s * NCOL, NCOL)]
                    dve.tensor_copy(r[:, NPAGE - 1, :], spn_s).then_inc(s_r, 1)
                    dve.wait_ge(s_sp, s + 2)
                    for j in range(NPAGE - 2, -1, -1):
                        dve.wait_ge(s_r, s * 8 + NPAGE - 1 - j)
                        dve.tensor_tensor(r[:, j, :], r[:, j + 1, :], sp_[:, j + 1, :], ALU.add).then_inc(s_r, 1)

                sequences(dve, step)
                dve.wait_ge(s_pv, NSEQ)
                for h in range(2):
                    rows = slice(h * HD, (h + 1) * HD)
                    src = O[rows, :].rearrange("d (s p h q) -> d p s h q", s=NSEQ, p=4, h=2)[:, :, :, h, :]
                    dve.tensor_copy(o[rows], src).then_inc(s_o, 1)
                dve.wait_ge(s_o, 2)
                ov = o[:].rearrange("d p s q -> d p (s q)")
                dve.tensor_copy(g.op_hi[:, 0:4, TP:T], ov).then_inc(s_o, 1)
                dve.wait_ge(s_o, 3)
                dve.tensor_tensor(g.op_lo[:, 0:4, TP:T], ov, g.op_hi[:, 0:4, TP:T], ALU.subtract)


def stage_prompt_attention(g):
    nc, io = g.nc, g.io
    HALF = slice(0, HD), slice(HD, P)
    TILES = 4
    steps = []
    for i in range(NT):
        c, w = i // TILES, (i + 1) * P
        if w > 512:
            steps.append((c, i, 512, w - 512))
        steps.append((c, i, 0, min(w, 512)))
    group_steps = [[t for t, s in enumerate(steps) if s[0] == c] for c in range(2)]
    NS, NU = len(steps), 3 * TILES
    NZ = 4
    with ExitStack() as ctx:
        sb = lambda *a: g.sb(*a, ctx=ctx)
        qraw = [sb(f"pa_qraw{i}", [P, TP]) for i in range(2)]
        kraw = [sb(f"pa_kraw{i}", [P, TP]) for i in range(2)]
        qh = sb("pa_qh", [P, TP], F32R)
        qa = [sb(f"pa_qa{i}", [P, TP], F32R) for i in range(2)]
        qb = [sb(f"pa_qb{i}", [P, TP], F32R) for i in range(2)]
        ka = [sb(f"pa_ka{i}", [P, TP], F32R) for i in range(2)]
        kb = [sb(f"pa_kb{i}", [P, TP], F32R) for i in range(2)]
        vhl = [sb(f"pa_vhl{i}", [P, NT, P], F32R) for i in range(2)]
        bq = sb("pa_bias", [P, HEADS])
        bh = sb("pa_bias_hi", [P, HEADS], F32R)
        a = [sb(f"pa_a{i}", [P, 512]) for i in range(NZ)]
        s = [sb(f"pa_s{i}", [P, 512]) for i in range(NZ)]
        w = [sb(f"pa_w{c}", [P, TILES, 512 * (c + 1)]) for c in range(2)]
        wth = [sb(f"pa_wth{i}", [P, 512], F32R) for i in range(2)]
        wtl = [sb(f"pa_wtl{i}", [P, 512], F32R) for i in range(2)]
        ot = [sb(f"pa_ot{i}", [P, 512]) for i in range(2)]
        s_in = [g.sem(f"pa_qk{i}_loaded") for i in range(2)]
        s_b = g.sem("pa_bias_loaded")
        s_bd = g.sem("pa_bias_split")
        s_c = g.sem("pa_constants")
        s_pra = g.sem("pa_act_prepared")
        s_prp = g.sem("pa_pool_prepared")
        s_prd = g.sem("pa_dve_prepared")
        s_z = g.sem("pa_scored")
        s_a = g.sem("pa_act_chain")
        s_sp = g.sem("pa_softplus")
        s_sc = g.sem("pa_scanned")
        s_x = g.sem("pa_log_weight")
        s_w = g.sem("pa_weight")
        s_tp = g.sem("pa_transposed")
        s_hi = g.sem("pa_wT_hi")
        s_lo = g.sem("pa_wT_lo")
        s_pv = g.sem("pa_v_multiplied")
        s_oa = g.sem("pa_out_half")
        s_o = g.sem("pa_out_summed")
        s_oh = g.sem("pa_out_hi")
        Z, TB, O = g.bank[0:4], g.bank[4:6], g.bank[6:8]

        def pairs(eng, prep, score, value):
            def pair(n, more):
                score(2 * n, 0, 0)
                score(2 * n, 0, 1)
                value(2 * n, 0, 0, n)
                score(2 * n + 1, 1, 0)
                value(2 * n, 0, 1, n)
                if more:
                    prep(2 * n + 2, 0)
                score(2 * n + 1, 1, 1)
                value(2 * n + 1, 1, 0, n)
                value(2 * n + 1, 1, 1, n)
                if more:
                    prep(2 * n + 3, 1)

            prep(0, 0)
            prep(1, 1)
            pair(0, True)
            with eng.Fori(1, HEADS // 2 - 1) as n:
                pair(n, True)
            pair(HEADS // 2 - 1, False)

        def nothing(*_):
            pass

        with nc.Block() as block:
            @block.sync
            def _(sp):
                sp.dma_start(bq[:], io["b_sb"].to_broadcast([P, HEADS])).then_inc(s_b, 16)

                def load(h, slot):
                    at_least(sp, s_prp, 3 * (h - 2) + 3)
                    at_least(sp, s_pra, 4 * (h - 2) + 4)
                    for raw, row in ((qraw, ROW_Q), (kraw, ROW_K)):
                        for half in HALF:
                            sp.dma_start(raw[slot][half, :], g.projT[bass.ds(h * HD + row, HD), 0:TP]).then_inc(s_in[slot], 16)

                pairs(sp, load, nothing, nothing)

            @block.gpsimd
            def _(pool):
                for i in range(2):
                    pool.memset(kb[i][HALF[1], :].bitcast(F32), 1.0 / 32).then_inc(s_c, 1)

                def prep(h, slot):
                    lo, hi = HALF
                    pool.wait_ge(s_pra, 4 * h + 4)
                    pool.tensor_tensor(kb[slot][lo, :], kraw[slot][lo, :], ka[slot][lo, :], ALU.subtract).then_inc(s_prp, 1)
                    pool.tensor_scalar(qraw[slot][hi, :], qraw[slot][hi, :], HD ** -0.5, 0.0, ALU.mult, ALU.add).then_inc(s_prp, 1)
                    pool.wait_ge(s_prp, 3 * h + 2)
                    pool.tensor_tensor(qa[slot][hi, :], qraw[slot][hi, :], qh[hi, :], ALU.subtract).then_inc(s_prp, 1)

                pairs(pool, prep, nothing, nothing)

            @block.tensor
            def _(pe):
                pe.wait_ge(s_c, 2)

                def score(h, slot, c):
                    if c == 0:
                        pe.wait_ge(s_prp, 3 * h + 3)
                        pe.wait_ge(s_prd, 3 * h + 3)
                    for t in group_steps[c]:
                        _, i, k0, kw = steps[t]
                        z = Z[t % NZ][:, 0:kw]
                        q = slice(i * P, (i + 1) * P)
                        at_least(pe, s_x, h * NS + t - NZ + 1)
                        diagonal = k0 + kw == (i + 1) * P
                        pe.matmul(z, qa[slot][:, q], ka[slot][:, k0:k0 + kw], start=True, stop=False)
                        last = pe.matmul(z, qb[slot][:, q], kb[slot][:, k0:k0 + kw], start=False, stop=not diagonal)
                        if diagonal:
                            last = pe.matmul(z[:, kw - P:kw], g.ident16[:], g.causal16[:], start=False, stop=True)
                        last.then_inc(s_z, 1)

                def value(h, slot, c, n):
                    pe.wait_ge(s_w, h * NS + group_steps[c][-1] + 1)
                    nj = TILES * (c + 1)
                    for j in range(nj + 1):
                        if j < nj:
                            u = c * TILES + j
                            i0 = max(0, j - c * TILES)
                            at_least(pe, s_lo, h * NU + u - 1)
                            for i in range(i0, TILES):
                                last = pe.transpose(TB[u % 2][:, i * P:(i + 1) * P], w[c][:, i, j * P:(j + 1) * P], g.ident[:])
                            last.then_inc(s_tp, 1)
                        if j > 0:
                            j_, u = j - 1, c * TILES + j - 1
                            i0 = max(0, j_ - c * TILES)
                            if j_ == 0:
                                at_least(pe, s_o, 2 * h + c - 1)
                            cols = slice(i0 * P, 512)
                            pe.wait_ge(s_lo, h * NU + u + 1)
                            pe.matmul(O[c][:, cols], vhl[slot][:, j_, :], wth[u % 2][:, cols], start=(j_ == 0), stop=False)
                            pe.matmul(O[c][:, cols], vhl[slot][:, j_, :], wtl[u % 2][:, cols], start=False,
                                      stop=(j_ == nj - 1)).then_inc(s_pv, 1)

                pairs(pe, nothing, score, value)

            @block.scalar
            def _(act):
                def prep(h, slot):
                    lo, hi = HALF
                    act.wait_ge(s_in[slot], (h - slot + 2) * 32)
                    at_least(act, s_z, (h - 2) * NS + NS)
                    at_least(act, s_prp, 3 * h)
                    act.activation(qa[slot][lo, :], qraw[slot][lo, :], ACT.Copy, scale=HD ** -0.5).then_inc(s_pra, 1)
                    act.activation(qb[slot][lo, :], qraw[slot][lo, :], ACT.Copy, scale=HD ** -0.5).then_inc(s_pra, 1)
                    act.activation(qh[hi, :], qraw[slot][hi, :], ACT.Copy, scale=HD ** -0.5).then_inc(s_pra, 1)
                    act.copy(ka[slot][:], kraw[slot][:]).then_inc(s_pra, 1)

                def weight(h, c, t):
                    _, i, k0, kw = steps[t]
                    act.wait_ge(s_x, h * NS + t + 1)
                    if t == group_steps[c][0]:
                        at_least(act, s_tp, (h - 1) * NU + (TILES if c == 0 else NU))
                    act.activation(w[c][:, i % TILES, k0:k0 + kw], a[t % NZ][:, 0:kw], ACT.Exp).then_inc(s_w, 1)

                def score(h, slot, c):
                    ts = group_steps[c]
                    for t in ts:
                        kw = steps[t][3]
                        out = a[t % NZ][:, 0:kw]
                        act.wait_ge(s_z, h * NS + t + 1)
                        act.activation(out, Z[t % NZ][:, 0:kw], ACT.Abs).then_inc(s_a, 1)
                        act.wait_ge(s_a, (h * NS + t) * 3 + 1)
                        act.activation(out, out, ACT.Exp, scale=-1.0).then_inc(s_a, 1)
                        act.wait_ge(s_a, (h * NS + t) * 3 + 2)
                        act.activation(out, out, ACT.Ln, bias=1.0).then_inc(s_a, 1)
                        if t > ts[0]:
                            weight(h, c, t - 1)
                    weight(h, c, ts[-1])

                def value(h, slot, c, n):
                    nj = TILES * (c + 1)
                    for j in range(nj):
                        u = c * TILES + j
                        cols = slice(max(0, j - c * TILES) * P, 512)
                        act.wait_ge(s_tp, h * NU + u + 1)
                        at_least(act, s_pv, h * NU + u - 1)
                        act.copy(wth[u % 2][:, cols], TB[u % 2][:, cols]).then_inc(s_hi, 1)
                    other = HALF[1 - slot]
                    act.wait_ge(s_pv, h * NU + c * TILES + nj)
                    at_least(act, s_o, 2 * h + c - 1)
                    act.copy(ot[c][HALF[slot], :], O[c][other, :]).then_inc(s_oa, 1)

                pairs(act, prep, score, value)

            @block.vector
            def _(dve):
                dve.wait_ge(s_b, 16)
                dve.tensor_copy(bh[:], bq[:]).then_inc(s_bd, 1)
                dve.wait_ge(s_bd, 1)
                lo_rows = slice(96, P)
                dve.tensor_tensor(bq[lo_rows], bq[lo_rows], bh[lo_rows].bitcast(F32), ALU.subtract).then_inc(s_bd, 1)
                dve.wait_ge(s_bd, 2)

                def prep(h, slot):
                    at_least(dve, s_z, (h - 2) * NS + NS)
                    b = bq[HALF[1], bass.ds(h, 1)].to_broadcast([HD, TP])
                    dve.tensor_scalar(qb[slot][HALF[1], :], b, 1.0, None, ALU.mult).then_inc(s_prd, 1)
                    at_least(dve, s_pv, (h - 2) * NU + NU)
                    v = g.vnat[:, 0:NT, bass.ds(h * HD, HD)]
                    dve.tensor_scalar(vhl[slot][:, :, 0:HD], v, 1.0, None, ALU.mult).then_inc(s_prd, 1)
                    dve.wait_ge(s_prd, 3 * h + 2)
                    dve.tensor_tensor(vhl[slot][:, :, HD:P], v, vhl[slot][:, :, 0:HD], ALU.subtract).then_inc(s_prd, 1)

                def score(h, slot, c):
                    for t in group_steps[c]:
                        _, i, k0, kw = steps[t]
                        step = h * NS + t
                        z, at, st = Z[t % NZ][:, 0:kw], a[t % NZ][:, 0:kw], s[t % NZ][:, 0:kw]
                        dve.wait_ge(s_a, step * 3 + 3)
                        dve.scalar_tensor_tensor(out=at, in0=z, scalar=0.0, in1=at, op0=ALU.max, op1=ALU.add).then_inc(s_sp, 1)
                        dve.wait_ge(s_sp, step + 1)
                        later = s[(t - 1) % NZ][:, 0:1] if i >= TILES and k0 == 0 else 0.0
                        dve.tensor_tensor_scan(st[:, ::-1], at[:, ::-1], at[:, ::-1], later, ALU.add, ALU.max).then_inc(s_sc, 1)
                        dve.wait_ge(s_sc, step + 1)
                        dve.tensor_tensor(at, z, st, ALU.subtract).then_inc(s_x, 1)

                def value(h, slot, c, n):
                    nj = TILES * (c + 1)
                    for j in range(nj):
                        u = c * TILES + j
                        cols = slice(max(0, j - c * TILES) * P, 512)
                        dve.wait_ge(s_hi, h * NU + u + 1)
                        dve.tensor_tensor(wtl[u % 2][:, cols], TB[u % 2][:, cols], wth[u % 2][:, cols], ALU.subtract).then_inc(s_lo, 1)
                    rows, G = HALF[slot], 2 * h + c
                    dve.wait_ge(s_oa, G + 1)
                    dve.tensor_tensor(ot[c][rows, :], ot[c][rows, :], O[c][rows, :], ALU.add).then_inc(s_o, 1)
                    hi, lo = (m[rows, bass.ds(n, 1), c * 512:(c + 1) * 512].rearrange("d o t -> d (o t)") for m in (g.op_hi, g.op_lo))
                    dve.wait_ge(s_o, G + 1)
                    dve.tensor_scalar(hi, ot[c][rows, :], 1.0, None, ALU.mult).then_inc(s_oh, 1)
                    dve.wait_ge(s_oh, G + 1)
                    dve.tensor_tensor(lo, ot[c][rows, :], hi, ALU.subtract)

                pairs(dve, prep, score, value)


def stage_gla(g):
    nc, io = g.nc, g.io
    NSUB = P // SUB
    MID = SUB // 2 - 1
    QS = GK ** -0.5
    HALF = slice(0, GK), slice(GK, P)
    with ExitStack() as ctx:
        sb = lambda *a: g.sb(*a, ctx=ctx)
        q = sb("gl_q", [P, 2, T])
        k = sb("gl_k", [P, 2, T])
        rg = sb("gl_r", [P, GH, T])
        sr = [sb(f"gl_silu{i}", [P, GH, P]) for i in range(2)]
        v = [sb(f"gl_v{i}", [P, GH * GV]) for i in range(3)]
        al = sb("gl_alow", [RANK, T])
        wg = sb("gl_wgate", [RANK, GH * GK])
        negb = sb("gl_negb", [P, 2])
        bc = sb("gl_bc", [P, 2, T])
        nx = sb("gl_nx", [P, 2, T])
        kend = sb("gl_kend", [P, 2, T])
        reset = kend[:, 0, :]
        eb = [sb(f"gl_eb{i}", [P, 2, P]) for i in range(2)]
        qdec = [sb(f"gl_qdec{i}", [P, 2, P]) for i in range(2)]
        qi = [sb(f"gl_qi{i}", [P, 2, 2, P]) for i in range(2)]
        dec = sb("gl_dec", [P, 2, NT + NSEQ])
        ki = [sb(f"gl_ki{i}", [P, 2, NSUB, P]) for i in range(2)]
        kn = [sb(f"gl_kn{i}", [P, 2 * P]) for i in range(2)]
        pt = [sb(f"gl_pt{i}", [P, GH, P]) for i in range(2)]
        st = sb("gl_state", [P, GH, GV])
        on = [sb(f"gl_on{i}", [P, GH, GV]) for i in range(2)]
        fin = [sb(f"gl_fin{i}", [P, GH, P]) for i in range(2)]
        sq = sb("gl_sq", [P, GH, GV])
        rs = sb("gl_rstd", [P, NT + 1, GH])
        tri = sb("gl_tri", [P, P])
        tri8 = sb("gl_tri8", [TS, TS])
        rowm = sb("gl_rowmask", [TS, NSEQ])
        colm = sb("gl_colmask", [P, NSEQ, TS])
        kinv = sb("gl_kinv", [P, 2, TS])
        qs = sb("gl_qs", [P, 2, 2, TS])
        qm = sb("gl_qm", [P, 2, NSEQ, TS])
        kem = [sb(f"gl_kem{i}", [TS, 2 * P]) for i in range(2)]
        s0 = sb("gl_s0", [P, NSEQ, GH, GV])
        s_gin = g.sem("gl_gate_inputs_loaded")
        s_k = g.sem("gl_k_loaded")
        s_q = g.sem("gl_q_loaded")
        s_r = g.sem("gl_r_loaded")
        s_s0 = g.sem("gl_s0_loaded")
        s_c = g.sem("gl_constants")
        s_z = g.sem("gl_zeroed")
        s_nb = g.sem("gl_negb_done")
        s_gate = g.sem("gl_gate_product")
        s_a = g.sem("gl_act_pre")
        s_d = g.sem("gl_dve_pre")
        s_E = g.sem("gl_ki_exp")
        s_D = g.sem("gl_ki_diff")
        s_ki = g.sem("gl_ki_done")
        s_kt = g.sem("gl_kend_transposed")
        s_kn = g.sem("gl_kn_copied")
        s_sc = g.sem("gl_scored")
        s_cl = g.sem("gl_clamped")
        s_pt = g.sem("gl_masked")
        s_oo = g.sem("gl_o")
        s_ds = g.sem("gl_ds")
        s_st = g.sem("gl_state_updated")
        s_sq = g.sem("gl_squares")
        s_rl = g.sem("gl_rstd_ln")
        s_rs = g.sem("gl_rstd_done")
        s_on = g.sem("gl_on_done")
        s_ot = g.sem("gl_on_transposed")
        s_fin = g.sem("gl_fin_done")
        s_fh = g.sem("gl_fin_hi")
        s_fl = g.sem("gl_fin_lo")
        s_out = g.sem("gl_stored")
        s_v = [g.sem(f"gl_v{i}_loaded") for i in range(3)]
        s_eb = g.sem("gl_exp_bc")
        s_qd = g.sem("gl_qdec_done")
        s_se = g.sem("gl_silu_exp")
        s_sd = g.sem("gl_silu_steps")
        s_km = g.sem("gl_kem_done")
        s_x = g.sem("gl_sample_dve")
        s_xp = g.sem("gl_sample_pe")
        KT, SC, OB, DS, OT = g.bank[0], g.bank[1:3], g.bank[3:5], g.bank[5], g.bank[6:8]
        N9 = NT + 1

        def tile(i):
            return slice(i * P, i * P + (P if i < NT else TS))

        with nc.Block() as block:
            @block.sync
            def _(sp):
                sp.dma_start(al[:], g.projT[ROW_A:IN_W, :]).then_inc(s_gin, 16)
                sp.dma_start(wg[:], io["w_gla_gate"][0]).then_inc(s_gin, 16)
                sp.dma_start(k[:], g.projT[ROW_KG:ROW_VG, :].rearrange("(m p) t -> p m t", p=P)).then_inc(s_k, 16)
                sp.dma_start(q[:], g.projT[ROW_QG:ROW_KG, :].rearrange("(m p) t -> p m t", p=P)).then_inc(s_q, 16)
                for i in range(2):
                    sp.dma_start(v[i][:], g.vgnat[tile(i)]).then_inc(s_v[i], 16)
                sp.dma_start(rg[:], g.projT[ROW_RG:ROW_A, :].rearrange("(m p) t -> p m t", p=P)).then_inc(s_r, 16)
                sp.wait_ge(s_z, 4)
                s0d = io["state_gla"][0].rearrange("s (m h) k v -> h m k s v", h=2)
                for h in range(2):
                    for m in range(2):
                        sp.dma_start(s0[HALF[h], :, 2 * m + h, :], s0d[h, m]).then_inc(s_s0, 16)
                for i in range(2, N9):
                    if i >= 3:
                        sp.wait_ge(s_ds, i - 2)
                        sp.wait_ge(s_oo, i - 2)
                    sp.dma_start(v[i % 3][0:P if i < NT else TS, :], g.vgnat[tile(i)]).then_inc(s_v[i % 3], 16)
                sp.wait_ge(s_st, 4 * NT)
                outp = io["state_prompt"][0, 0].rearrange("(m h) k v -> h m k v", h=2)
                for h in range(2):
                    for m in range(2):
                        sp.dma_start(outp[h, m], st[HALF[h], 2 * m + h, :]).then_inc(s_out, 16)
                sp.wait_ge(s_x, 1 + 4 * NSEQ)
                outs = io["state_sample"][0].rearrange("s (m h) k v -> h m k s v", h=2)
                for h in range(2):
                    for m in range(2):
                        sp.dma_start(outs[h, m], s0[HALF[h], :, 2 * m + h, :]).then_inc(s_out, 16)
                sp.wait_ge(s_out, 8 * 16)

            @block.gpsimd
            def _(pool):
                pool.memset(st[:], 0.0).then_inc(s_z, 1)
                pool.memset(qi[0][:], 0.0).then_inc(s_z, 1)
                pool.memset(qi[1][:], 0.0).then_inc(s_z, 1)
                pool.memset(s0[:], 0.0).then_inc(s_z, 1)
                pool.memset(qs[:], 0.0).then_inc(s_z, 1)
                pool.memset(reset, 1.0).then_inc(s_c, 1)
                pool.memset(tri[:], 1.0).then_inc(s_c, 1)
                pool.memset(tri8[:], 1.0).then_inc(s_c, 1)
                pool.memset(rowm[:], 1.0).then_inc(s_c, 1)
                pool.memset(colm[:], 1.0).then_inc(s_c, 1)
                pool.wait_ge(s_c, 5)
                pool.memset(reset[:, 0:TP:P], 0.0).then_inc(s_c, 1)
                pool.memset(reset[:, TP:T:NEW], 0.0).then_inc(s_c, 1)

                def keep(out, pattern, base, mult):
                    pool.affine_select(out=out, in_=out, compare_op=ALU.is_ge, fill=0.0, base=base,
                                       pattern=pattern, channel_multiplier=mult).then_inc(s_c, 1)

                keep(tri[:], [[1, P]], 0, -1)
                t8 = tri8[:].rearrange("k (s q) -> k s q", s=NSEQ)
                keep(t8, [[NEW, NSEQ], [1, NEW]], 0, -1)
                keep(rowm[:], [[-NEW, NSEQ]], 0, 1)
                keep(colm[:], [[-NEW, NSEQ], [1, TS]], 0, 0)
                pool.wait_ge(s_c, 11)
                keep(t8, [[-NEW, NSEQ], [0, NEW]], 0, 1)
                keep(rowm[:], [[NEW, NSEQ]], NEW - 1, -1)
                keep(colm[:], [[NEW, NSEQ], [-1, TS]], NEW - 1, 0)
                for i in range(N9):
                    w = P if i < NT else TS
                    pool.wait_ge(s_fh, i + 1)
                    pool.tensor_tensor(g.op_lo[:, GH:2 * GH, tile(i)], fin[i % 2][:, :, 0:w],
                                       g.op_hi[:, GH:2 * GH, tile(i)], ALU.subtract).then_inc(s_fl, 1)

            @block.scalar
            def _(act):
                act.wait_ge(s_nb, 1)
                n = 0
                for m in range(2):
                    for c, (t0, tw) in enumerate(CHUNKS):
                        act.wait_ge(s_gate, 3 * m + c + 1)
                        act.activation(nx[:, m, t0:t0 + tw], g.bank[3 * m + c][:, 0:tw], ACT.Identity, scale=-1.0,
                                       bias=negb[:, m:m + 1]).then_inc(s_a, 1)
                act.wait_ge(s_a, 6)
                act.activation(bc[:], nx[:], ACT.Abs).then_inc(s_a, 1)
                act.wait_ge(s_a, 7)
                act.activation(bc[:], bc[:], ACT.Exp, scale=-1.0).then_inc(s_a, 1)
                act.wait_ge(s_a, 8)
                act.activation(bc[:], bc[:], ACT.Ln, bias=1.0).then_inc(s_a, 1)
                act.wait_ge(s_d, 3)
                act.activation(dec[:, :, 0:NT], bc[:, :, P - 1:TP:P], ACT.Exp, scale=-GATE)
                act.activation(dec[:, :, NT:], bc[:, :, TP + NEW - 1:T:NEW], ACT.Exp, scale=-GATE).then_inc(s_a, 1)
                act.wait_ge(s_d, 5)
                act.activation(kend[:], kend[:], ACT.Exp, scale=GATE).then_inc(s_a, 1)
                act.wait_ge(s_d, 7)
                act.activation(nx[:, :, 0:TP], nx[:, :, 0:TP], ACT.Exp, scale=-GATE).then_inc(s_a, 1)
                act.activation(kinv[:], bc[:, :, TP:T], ACT.Exp, scale=GATE).then_inc(s_a, 1)
                act.activation(nx[:, :, TP:T], bc[:, :, TP:T], ACT.Exp, scale=-GATE).then_inc(s_a, 1)
                act.wait_ge(s_r, 16)

                def key_exps(i):
                    if i >= 2:
                        act.wait_ge(s_qd, 3 * (i - 1))
                    act.activation(eb[i % 2][:], bc[:, :, tile(i)], ACT.Exp, scale=-GATE).then_inc(s_eb, 1)
                    for m in range(2):
                        act.wait_ge(s_D, 2 * i + m + 1)
                        act.activation(ki[i % 2][:, m], ki[i % 2][:, m], ACT.Exp, scale=GATE).then_inc(s_E, 1)

                def copy_kn(i):
                    rows = P if i < NT else TS
                    act.wait_ge(s_kt, i + 1)
                    if 2 <= i < NT:
                        act.wait_ge(s_ds, i - 1)
                    act.copy(kn[i % 2][0:rows], KT[0:rows, 0:2 * P]).then_inc(s_kn, 1)

                def norms(i):
                    rows = P if i < NT else TS
                    act.wait_ge(s_oo, i + 1)
                    for h in range(GH):
                        act.activation(sq[0:rows, h], OB[i % 2][0:rows, h * GV:(h + 1) * GV], ACT.Square,
                                       accum_out=rs[0:rows, i, h:h + 1]).then_inc(s_sq, 1)
                    act.wait_ge(s_sq, GH * (i + 1))
                    act.activation(rs[0:rows, i], rs[0:rows, i], ACT.Ln, scale=1.0 / GV, bias=g.eps[0:rows, :]).then_inc(s_rl, 1)
                    act.wait_ge(s_rl, i + 1)
                    act.activation(rs[0:rows, i], rs[0:rows, i], ACT.Exp, scale=-0.5).then_inc(s_rs, 1)

                def gate_exp(i):
                    w = P if i < NT else TS
                    if i >= 2:
                        act.wait_ge(s_fin, i - 1)
                    act.activation(sr[i % 2][:, :, 0:w], rg[:, :, tile(i)], ACT.Exp, scale=-1.0).then_inc(s_se, 1)

                def fin_hi(i):
                    w = P if i < NT else TS
                    act.wait_ge(s_fin, i + 1)
                    act.copy(g.op_hi[:, GH:2 * GH, tile(i)], fin[i % 2][:, :, 0:w]).then_inc(s_fh, 1)

                key_exps(0)
                copy_kn(0)
                for i in range(N9):
                    if i + 1 < NT:
                        key_exps(i + 1)
                    if i + 1 < N9:
                        copy_kn(i + 1)
                    gate_exp(i)
                    norms(i)
                    if i > 0:
                        fin_hi(i - 1)
                fin_hi(N9 - 1)

            @block.vector
            def _(dve):
                nd = [0]

                def pre(ins):
                    nd[0] += 1
                    ins.then_inc(s_d, 1)

                dve.tensor_scalar(negb[:], g.vecT[:, 16:18], -1.0, None, ALU.mult).then_inc(s_nb, 1)
                dve.wait_ge(s_a, 9)
                dve.wait_ge(s_c, 7)
                pre(dve.scalar_tensor_tensor(out=nx[:].rearrange("k m t -> k (m t)"), in0=nx[:].rearrange("k m t -> k (m t)"),
                                             scalar=0.0, in1=bc[:].rearrange("k m t -> k (m t)"), op0=ALU.max, op1=ALU.add))
                dve.wait_ge(s_d, 1)
                for m in range(2):
                    pre(dve.tensor_tensor_scan(bc[:, m, :], reset, nx[:, m, :], 0.0, ALU.mult, ALU.add))
                dve.wait_ge(s_d, 3)
                for n, w, t0 in ((NT, P, 0), (NSEQ, NEW, TP)):
                    b = bc[:, :, t0:t0 + n * w].rearrange("k m (n w) -> k m n w", w=w)
                    pre(dve.tensor_tensor(kend[:, :, t0:t0 + n * w].rearrange("k m (n w) -> k m n w", w=w), b,
                                          b[:, :, :, w - 1:w].to_broadcast([P, 2, n, w]), ALU.subtract))
                dve.wait_ge(s_q, 16)
                dve.wait_ge(s_k, 16)
                for m in range(2):
                    b = bc[:, m, 0:TP].rearrange("k (n w) -> k n w", w=SUB)
                    pre(dve.tensor_tensor(nx[:, m, 0:TP].rearrange("k (n w) -> k n w", w=SUB), b,
                                          b[:, :, MID:MID + 1].to_broadcast([P, TP // SUB, SUB]), ALU.subtract))
                dve.wait_ge(s_a, 11)
                pre(dve.tensor_tensor(kend[:], kend[:], k[:], ALU.mult))
                dve.wait_ge(s_a, 14)
                dve.wait_ge(s_z, 5)
                pre(dve.scalar_tensor_tensor(out=kinv[:], in0=kinv[:], scalar=BIG, in1=k[:, :, TP:T], op0=ALU.min, op1=ALU.mult))
                for h in range(2):
                    pre(dve.scalar_tensor_tensor(out=qs[HALF[h], :, h, :], in0=nx[HALF[h], :, TP:T], scalar=QS,
                                                 in1=q[HALF[h], :, TP:T], op0=ALU.mult, op1=ALU.mult))
                dve.wait_ge(s_d, 11)
                dve.scalar_tensor_tensor(out=nx[:, :, TP:T], in0=nx[:, :, TP:T], scalar=QS, in1=q[:, :, TP:T],
                                         op0=ALU.mult, op1=ALU.mult).then_inc(s_x, 1)
                dve.wait_ge(s_x, 1)
                dve.wait_ge(s_c, 14)
                for m in range(2):
                    pre(dve.tensor_tensor(qm[:, m], nx[:, m, TP:T].rearrange("k (o t) -> k o t", o=1).to_broadcast([P, NSEQ, TS]),
                                          colm[:], ALU.mult))

                def keys(i):
                    b = bc[:, :, tile(i)]
                    mid = b.rearrange("k m (n w) -> k m n w", w=SUB)[:, :, :, MID:MID + 1]
                    if i >= 2:
                        dve.wait_ge(s_sc, i - 1)
                    for m in range(2):
                        dve.tensor_tensor(ki[i % 2][:, m], b[:, m:m + 1, :].to_broadcast([P, NSUB, P]),
                                          mid[:, m].to_broadcast([P, NSUB, P]), ALU.subtract).then_inc(s_D, 1)
                    for m in range(2):
                        dve.wait_ge(s_E, 2 * i + m + 1)
                        dve.scalar_tensor_tensor(out=ki[i % 2][:, m], in0=ki[i % 2][:, m], scalar=BIG,
                                                 in1=k[:, m:m + 1, tile(i)].to_broadcast([P, NSUB, P]),
                                                 op0=ALU.min, op1=ALU.mult).then_inc(s_ki, 1)
                    if i >= 2:
                        dve.wait_ge(s_oo, i - 1)
                    dve.wait_ge(s_eb, i + 1)
                    dve.scalar_tensor_tensor(out=qdec[i % 2][:], in0=eb[i % 2][:], scalar=QS, in1=q[:, :, tile(i)],
                                             op0=ALU.mult, op1=ALU.mult).then_inc(s_qd, 1)
                    for h in range(2):
                        dve.scalar_tensor_tensor(out=qi[i % 2][HALF[h], :, h, :], in0=nx[HALF[h], :, tile(i)], scalar=QS,
                                                 in1=q[HALF[h], :, tile(i)], op0=ALU.mult, op1=ALU.mult).then_inc(s_qd, 1)

                def scores(i):
                    rows = P if i < NT else TS
                    s = SC[i % 2][0:rows].rearrange("k (h t) -> k h t", h=GH)[:, :, 0:rows]
                    p = pt[i % 2][0:rows, :, 0:rows]
                    dve.wait_ge(s_sc, i + 1)
                    if i >= 2:
                        dve.wait_ge(s_oo, i - 1)
                    dve.tensor_scalar(p, s, BIG, -BIG, ALU.min, ALU.max).then_inc(s_cl, 1)
                    dve.wait_ge(s_cl, i + 1)
                    mask = (tri if i < NT else tri8)[:].rearrange("k (o t) -> k o t", o=1).to_broadcast([rows, GH, rows])
                    dve.tensor_tensor(p, p, mask, ALU.mult).then_inc(s_pt, 1)

                def normed(i):
                    rows = P if i < NT else TS
                    dve.wait_ge(s_rs, i + 1)
                    if i >= 2:
                        dve.wait_ge(s_ot, i - 1)
                    dve.tensor_tensor(on[i % 2][0:rows], OB[i % 2][0:rows].rearrange("t (h v) -> t h v", h=GH),
                                      rs[0:rows, i].rearrange("t (h o) -> t h o", o=1).to_broadcast([rows, GH, GV]),
                                      ALU.mult).then_inc(s_on, 1)

                def gated(i):
                    w = P if i < NT else TS
                    dve.wait_ge(s_ot, i + 1)
                    if i >= 2:
                        dve.wait_ge(s_fl, i - 1)
                    x = sr[i % 2][:, :, 0:w]
                    dve.wait_ge(s_se, i + 1)
                    dve.tensor_scalar(x, x, 1.0, None, ALU.add).then_inc(s_sd, 1)
                    dve.wait_ge(s_sd, 3 * i + 1)
                    dve.reciprocal(x, x).then_inc(s_sd, 1)
                    dve.wait_ge(s_sd, 3 * i + 2)
                    dve.tensor_tensor(x, x, rg[:, :, tile(i)], ALU.mult).then_inc(s_sd, 1)
                    dve.wait_ge(s_sd, 3 * i + 3)
                    dve.scalar_tensor_tensor(out=fin[i % 2][:, :, 0:w], in0=OT[i % 2][:].rearrange("v (h t) -> v h t", h=GH)[:, :, 0:w],
                                             scalar=g.vecT[:, 18:19], in1=x, op0=ALU.mult,
                                             op1=ALU.mult).then_inc(s_fin, 1)

                def state(i):
                    dve.wait_ge(s_ds, i + 1)
                    for h in range(GH):
                        r = HALF[h % 2]
                        dve.scalar_tensor_tensor(out=st[r, h, :], in0=st[r, h, :], scalar=dec[r, h // 2, i:i + 1],
                                                 in1=DS[r, h * GV:(h + 1) * GV], op0=ALU.mult, op1=ALU.add).then_inc(s_st, 1)

                keys(0)
                for i in range(N9):
                    if i + 1 < NT:
                        keys(i + 1)
                    scores(i)
                    if i > 0:
                        normed(i - 1)
                    if i < NT:
                        if i > 0:
                            dve.wait_ge(s_st, 4 * i)
                        state(i)
                    if i > 0:
                        gated(i - 1)
                normed(NT)
                gated(NT)
                dve.wait_ge(s_kn, N9)
                dve.wait_ge(s_s0, 64)
                dve.wait_ge(s_oo, N9)
                for s in range(NSEQ + 1):
                    if s < NSEQ:
                        if s >= 2:
                            dve.wait_ge(s_xp, s - 1)
                        dve.tensor_scalar(kem[s % 2][:], kn[NT % 2][0:TS], rowm[:, s:s + 1], None, ALU.mult).then_inc(s_km, 1)
                    if s == 0:
                        continue
                    dve.wait_ge(s_xp, s)
                    for h in range(GH):
                        r = HALF[h % 2]
                        dve.scalar_tensor_tensor(out=s0[r, s - 1, h, :], in0=s0[r, s - 1, h, :], scalar=dec[r, h // 2, NT + s - 1:NT + s],
                                                 in1=g.bank[s - 1][r, h * GV:(h + 1) * GV], op0=ALU.mult, op1=ALU.add).then_inc(s_x, 1)

            @block.tensor
            def _(pe):
                pe.wait_ge(s_gin, 32)
                for m in range(2):
                    for c, (t0, tw) in enumerate(CHUNKS):
                        pe.matmul(g.bank[3 * m + c][:, 0:tw], wg[:, m * P:(m + 1) * P], al[:, t0:t0 + tw],
                                  start=True, stop=True).then_inc(s_gate, 1)

                def turn_keys(i):
                    rows = P if i < NT else TS
                    if i > 0:
                        pe.wait_ge(s_kn, i)
                    for m in range(2):
                        last = pe.transpose(KT[0:rows, m * P:(m + 1) * P], kend[:, m, tile(i)], g.ident[:])
                    last.then_inc(s_kt, 1)

                def score(i):
                    if i >= 2:
                        pe.wait_ge(s_pt, i - 1)
                    if i < NT:
                        pe.wait_ge(s_qd, 3 * i + 3)
                        out = SC[i % 2][:].rearrange("k (m h t) -> k m h t", m=2, h=2)
                        for m in range(2):
                            for n in range(NSUB):
                                c = slice(n * SUB, (n + 1) * SUB)
                                last = pe.matmul(out[:, m, :, n * SUB:(n + 1) * SUB], ki[i % 2][:, m, n, :], qi[i % 2][:, m, :, c],
                                                 start=True, stop=True)
                    else:
                        out = SC[i % 2][0:TS].rearrange("k (m h t) -> k m h t", m=2, h=2)
                        for m in range(2):
                            last = pe.matmul(out[:, m, :, 0:TS], kinv[:, m, :], qs[:, m], start=True, stop=True)
                    last.then_inc(s_sc, 1)

                def output(i):
                    rows = P if i < NT else TS
                    o = OB[i % 2][0:rows, :]
                    if i >= 2:
                        pe.wait_ge(s_on, i - 1)
                    pe.wait_ge(s_pt, i + 1)
                    pe.wait_ge(s_v[i % 3], 16 * (i // 3 + 1))
                    for h in range(GH):
                        last = pe.matmul(o[:, h * GV:(h + 1) * GV], pt[i % 2][0:rows, h, 0:rows], v[i % 3][0:rows, h * GV:(h + 1) * GV],
                                         start=(h == 0), stop=False, skip_group_check=True)
                    if i < NT:
                        if i > 0:
                            pe.wait_ge(s_st, 4 * i)
                        for m in range(2):
                            last = pe.matmul(o[:, 2 * m * GV:(2 * m + 2) * GV], qdec[i % 2][:, m, :], st[:, 2 * m:2 * m + 2, :],
                                             start=False, stop=True, skip_group_check=True)
                    else:
                        pe.wait_ge(s_s0, 64)
                        for m in range(2):
                            for s in range(NSEQ):
                                last = pe.matmul(o[:, 2 * m * GV:(2 * m + 2) * GV], qm[:, m, s, :], s0[:, s, 2 * m:2 * m + 2, :],
                                                 start=False, stop=(s == NSEQ - 1), skip_group_check=True)
                    last.then_inc(s_oo, 1)

                def outer(i):
                    pe.wait_ge(s_kn, i + 1)
                    if i > 0:
                        pe.wait_ge(s_st, 4 * i)
                    for m in range(2):
                        last = pe.matmul(DS[:, 2 * m * GV:(2 * m + 2) * GV], kn[i % 2][:, m * P:(m + 1) * P],
                                         v[i % 3][:, 2 * m * GV:(2 * m + 2) * GV], start=True, stop=True)
                    last.then_inc(s_ds, 1)

                def turn_out(i):
                    rows = P if i < NT else TS
                    pe.wait_ge(s_on, i + 1)
                    if i >= 2:
                        pe.wait_ge(s_fin, i - 1)
                    for h in range(GH):
                        last = pe.transpose(OT[i % 2][:, h * P:h * P + rows], on[i % 2][0:rows, h, :], g.ident[0:rows, 0:rows])
                    last.then_inc(s_ot, 1)

                pe.wait_ge(s_d, 13)
                turn_keys(0)
                score(0)
                for i in range(N9):
                    if i + 1 < N9:
                        turn_keys(i + 1)
                        score(i + 1)
                    output(i)
                    if i < NT:
                        outer(i)
                    if i > 0:
                        turn_out(i - 1)
                turn_out(NT)
                pe.wait_ge(s_fin, N9)
                for s in range(NSEQ):
                    pe.wait_ge(s_km, s + 1)
                    for m in range(2):
                        last = pe.matmul(g.bank[s][:, 2 * m * GV:(2 * m + 2) * GV], kem[s % 2][:, m * P:(m + 1) * P],
                                         v[NT % 3][0:TS, 2 * m * GV:(2 * m + 2) * GV], start=True, stop=True)
                    last.then_inc(s_xp, 1)


def seq_row(a, n=NSEQ, w=NEW):
    return a.rearrange("p (s o) -> p s o", o=1).to_broadcast([P, n, w])


def by_seq(a):
    return a.rearrange("p (s t) -> p s t", s=NSEQ)


def stage_project_out(g):
    nc, io = g.nc, g.io
    w_out = io["w_out"][0]
    xp = io["x_prompt"][0]
    xs = io["x_sample"].rearrange("s t d -> (s t) d")
    NP = D // PANEL
    with ExitStack() as ctx:
        w = Panels(g, ctx, "out")
        x = [g.sb(f"out_x{i}", [P, D], ctx=ctx) for i in range(4)]
        tmp = [g.sb(f"out_tmp{i}", [P, TS], ctx=ctx) for i in range(2)]
        s_x = [g.sem(f"out_x{i}_loaded") for i in range(4)]
        s_xt = g.sem("out_x_transposed")
        s_xc = g.sem("out_x_copied")
        s_mm = g.sem("out_group_summed")
        s_ev = g.sem("out_added")
        s_tm = g.sem("out_sample_scaled")
        turns = [(t0, 4, k) for t0 in (0, 4) for k in range(KD)] + [(8, 1, 0)]
        groups = [(p, m, c) for p in range(NP) for m in range(2) for c in range(3)]
        with nc.Block() as block:
            @block.sync
            def _(sp):
                for i in range(4):
                    sp.dma_start(x[i][:], xp[i * P:(i + 1) * P]).then_inc(s_x[i], 16)
                for p in range(2):
                    sp.dma_start(w.raw[p][:], w_out[:, p * PANEL:(p + 1) * PANEL].rearrange("(k p) c -> p k c", p=P)).then_inc(w.loaded[p], 16)
                sp.wait_ge(s_xt, KD)
                for i in range(4, 8):
                    sp.dma_start(x[i - 4][:], xp[i * P:(i + 1) * P]).then_inc(s_x[i - 4], 16)
                sp.wait_ge(s_xt, 2 * KD)
                sp.dma_start(x[0][0:TS], xs).then_inc(s_x[0], 16)
                for p in range(2, NP):
                    sp.wait_ge(w.lo_done, p - 1)
                    sp.dma_start(w.raw[p % 2][:], w_out[:, p * PANEL:(p + 1) * PANEL].rearrange("(k p) c -> p k c", p=P)).then_inc(w.loaded[p % 2], 16)

            @block.gpsimd
            def _(pool):
                for p in range(NP):
                    pool.wait_ge(w.hi_done, p + 1)
                    pool.tensor_tensor(w.lo[p % 2][:], w.raw[p % 2][:], w.hi[p % 2][:], ALU.subtract).then_inc(w.lo_done, 1)

            @block.scalar
            def _(act):
                def round_hi(p):
                    act.wait_ge(w.loaded[p % 2], 16 * (p // 2 + 1))
                    if p >= 2:
                        act.wait_ge(s_mm, 6 * (p - 1))
                    act.copy(w.hi[p % 2][:], w.raw[p % 2][:]).then_inc(w.hi_done, 1)

                for j, (t0, n, k) in enumerate(turns):
                    if j in (4, 10):
                        round_hi(j // 10)
                    act.wait_ge(s_xt, j + 1)
                    if n > 1:
                        act.copy(g.x1T[:, k, t0 * P:(t0 + 4) * P], g.bank[6 + j % 2][:]).then_inc(s_xc, 1)
                    else:
                        act.copy(g.x1T[:, :, TP:T], g.bank[6 + j % 2][:].rearrange("p (k t) -> p k t", k=KD)).then_inc(s_xc, 1)
                for p in range(2, NP):
                    round_hi(p)

            @block.vector
            def _(dve):
                dve.wait_ge(s_xc, len(turns))
                for j, (p, m, c) in enumerate(groups):
                    t0, tw = CHUNKS[c]
                    pw = min(tw, TP - t0)
                    kc = 2 * p + m
                    b = g.bank[j % 6]
                    dve.wait_ge(s_mm, j + 1)
                    if c == 2:
                        t = tmp[(j // 3) % 2]
                        dve.tensor_tensor(by_seq(t[:]), by_seq(b[:, pw:tw]), seq_row(g.modT[:, GA1 * KD + kc, 1:NMOD]), ALU.mult).then_inc(s_tm, 1)
                        dve.wait_ge(s_tm, j // 3 + 1)
                        dve.tensor_tensor(g.x1T[:, kc, TP:T], g.x1T[:, kc, TP:T], t[:], ALU.add)
                    out = g.x1T[:, kc, t0:t0 + pw]
                    dve.scalar_tensor_tensor(out=out, in0=b[:, 0:pw], scalar=g.mod(GA1, kc), in1=out, op0=ALU.mult,
                                             op1=ALU.add).then_inc(s_ev, 1)

            @block.tensor
            def _(pe):
                for j, (t0, n, k) in enumerate(turns):
                    b = g.bank[6 + j % 2]
                    if j >= 2:
                        pe.wait_ge(s_xc, j - 1)
                    if n > 1:
                        for i in range(4):
                            if k == 0:
                                pe.wait_ge(s_x[i], 16 * (t0 // 4 + 1))
                            last = pe.transpose(b[:, i * P:(i + 1) * P], x[i][:, k * P:(k + 1) * P], g.ident[:])
                    else:
                        pe.wait_ge(s_x[0], 48)
                        for kk in range(KD):
                            last = pe.transpose(b[:, kk * TS:(kk + 1) * TS], x[0][0:TS, kk * P:(kk + 1) * P], g.ident[0:TS, 0:TS])
                    last.then_inc(s_xt, 1)
                for j, (p, m, c) in enumerate(groups):
                    t0, tw = CHUNKS[c]
                    if j % 6 == 0:
                        pe.wait_ge(w.lo_done, p + 1)
                    if j >= 6:
                        pe.wait_ge(s_ev, j - 5)
                    for k in range(KD):
                        cols = slice(m * P, (m + 1) * P)
                        last = three_products(pe, g.bank[j % 6][:, 0:tw], w.hi[p % 2][:, k, cols], w.lo[p % 2][:, k, cols],
                                              g.op_hi[:, k, t0:t0 + tw], g.op_lo[:, k, t0:t0 + tw], k, KD)
                    last.then_inc(s_mm, 1)


def stage_norm_ffn(g, h_hi, h_lo):
    nc = g.nc
    N9 = NT + 1
    WIN = [(0, 512), (512, 512), (TP, TS)]
    with ExitStack() as ctx:
        sb = lambda *a: g.sb(*a, ctx=ctx)
        sq = [sb(f"n2_sq{i}", [P, 512]) for i in range(2)]
        ss = sb("n2_ss", [P, N9, 2])
        rs = sb("n2_rstd", [P, N9])
        ones = sb("n2_ones", [P, P])
        diag = sb("n2_diag", [P, N9, P])
        xn = [sb(f"n2_xn{i}", [P, 512]) for i in range(2)]
        tmp = [sb(f"n2_tmp{i}", [P, 512]) for i in range(2)]
        s_c = g.sem("n2_constants")
        s_tr = g.sem("n2_turned")
        s_sq = g.sem("n2_squared")
        s_su = g.sem("n2_summed")
        s_ln = g.sem("n2_ln")
        s_rs = g.sem("n2_rstd_done")
        s_dg = g.sem("n2_diag_done")
        s_rb = g.sem("n2_rstd_spread")
        s_xn = g.sem("n2_normed")
        s_tm = g.sem("n2_modulated")
        s_hi = g.sem("n2_hi")
        s_lo = g.sem("n2_lo")
        turns = [(tt, half) for tt in range(N9) for half in range(2)]
        steps = [(wi, k) for wi in range(3) for k in range(KD)]
        NPR = 2 * KD
        with nc.Block() as block:
            @block.tensor
            def _(pe):
                for j, (tt, half) in enumerate(turns):
                    w = P if tt < NT else TS
                    if j >= 4:
                        pe.wait_ge(s_sq, j - 3)
                    for k in range(4):
                        last = pe.transpose(g.bank[j % 4][0:w, k * P:(k + 1) * P], g.x1T[:, half * 4 + k, tt * P:tt * P + w], g.ident[:])
                    last.then_inc(s_tr, 1)
                pe.wait_ge(s_dg, N9)
                for tt in range(N9):
                    w = P if tt < NT else TS
                    last = pe.matmul(g.bank[5 + tt // 4][:, (tt % 4) * P:(tt % 4) * P + w], ones[0:w, :], diag[0:w, tt, 0:w],
                                     start=True, stop=True)
                last.then_inc(s_rb, 1)

            @block.scalar
            def _(act):
                act.wait_ge(s_c, 2)
                for j, (tt, half) in enumerate(turns):
                    w = P if tt < NT else TS
                    act.wait_ge(s_tr, j + 1)
                    if j >= 2:
                        act.wait_ge(s_sq, j - 1)
                    act.activation(sq[j % 2][0:w], g.bank[j % 4][0:w], ACT.Square, accum_out=ss[0:w, tt, half:half + 1]).then_inc(s_sq, 1)
                act.wait_ge(s_su, 1)
                act.activation(rs[:], rs[:], ACT.Ln, scale=1.0 / D, bias=g.eps[:]).then_inc(s_ln, 1)
                act.wait_ge(s_ln, 1)
                act.activation(rs[:], rs[:], ACT.Exp, scale=-0.5).then_inc(s_rs, 1)
                for j, (wi, k) in enumerate(steps):
                    t0, tw = WIN[wi]
                    t = tmp[j % 2][:, 0:tw]
                    if wi < 2:
                        act.wait_ge(s_xn, j + 1)
                        if j >= 2:
                            act.wait_ge(s_lo, j - 1)
                        act.activation(t, xn[j % 2][:, 0:tw], ACT.Identity, scale=g.mul2[:, k, 0:1], bias=g.mod(SH2, k)).then_inc(s_tm, 1)
                        act.wait_ge(s_tm, j + 1)
                    else:
                        act.wait_ge(s_xn, NPR + 3 * (j - NPR) + 3)
                    act.copy(h_hi[:, k, t0:t0 + tw], t).then_inc(s_hi, 1)

            @block.gpsimd
            def _(pool):
                pool.memset(ones[:], 1.0).then_inc(s_c, 1)
                pool.memset(ss[:], 0.0).then_inc(s_c, 1)
                for j, (wi, k) in enumerate(steps):
                    t0, tw = WIN[wi]
                    pool.wait_ge(s_hi, j + 1)
                    pool.tensor_tensor(h_lo[:, k, t0:t0 + tw], tmp[j % 2][:, 0:tw], h_hi[:, k, t0:t0 + tw], ALU.subtract).then_inc(s_lo, 1)

            @block.vector
            def _(dve):
                dve.wait_ge(s_sq, len(turns))
                dve.tensor_tensor(rs[:], ss[:, :, 0], ss[:, :, 1], ALU.add).then_inc(s_su, 1)
                dve.wait_ge(s_rs, 1)
                for tt in range(N9):
                    dve.tensor_scalar(diag[:, tt, :], g.ident[:], rs[:, tt:tt + 1], None, ALU.mult).then_inc(s_dg, 1)
                dve.wait_ge(s_rb, 1)
                for j, (wi, k) in enumerate(steps):
                    t0, tw = WIN[wi]
                    x = xn[j % 2][:, 0:tw]
                    if j >= 2:
                        dve.wait_ge(s_lo, j - 1)
                    if j >= 1 and wi == 2:
                        dve.wait_ge(s_xn, NPR + 3 * (j - NPR))
                    dve.tensor_tensor(x, g.x1T[:, k, t0:t0 + tw], g.bank[5 + wi][:, 0:tw], ALU.mult).then_inc(s_xn, 1)
                    if wi == 2:
                        n = NPR + 3 * (j - NPR)
                        dve.wait_ge(s_xn, n + 1)
                        dve.tensor_tensor(by_seq(x), by_seq(x), seq_row(g.mul2[:, k, 1:NMOD]), ALU.mult).then_inc(s_xn, 1)
                        dve.wait_ge(s_xn, n + 2)
                        dve.tensor_tensor(by_seq(tmp[j % 2][:, 0:TS]), by_seq(x), seq_row(g.modT[:, SH2 * KD + k, 1:NMOD]),
                                          ALU.add).then_inc(s_xn, 1)


def stage_mlp(g, h_hi, h_lo):
    nc, io = g.nc, g.io
    w_up, w_down = io["w_up"][0], io["w_down"][0]
    FB = 512
    NG = FF // FB
    KF = FB // P
    NUP, NDN = 3 * KF, 3 * KD
    NGR = NUP + NDN
    NBANK = 6
    with ExitStack() as ctx:
        w = Panels(g, ctx, "mlp")
        a_hi = g.sb("mlp_a_hi", [P, KF, T], F32R, ctx=ctx)
        a_lo = g.sb("mlp_a_lo", [P, KF, T], F32R, ctx=ctx)
        r = [g.sb(f"mlp_relu{i}", [P, 384], ctx=ctx) for i in range(3)]
        q = [g.sb(f"mlp_sq{i}", [P, 384], ctx=ctx) for i in range(3)]
        tmp = [g.sb(f"mlp_tmp{i}", [P, TS], ctx=ctx) for i in range(2)]
        s_mm = g.sem("mlp_group_summed")
        s_re = g.sem("mlp_relu_done")
        s_sq = g.sem("mlp_squared")
        s_ah = g.sem("mlp_a_hi_done")
        s_al = g.sem("mlp_a_lo_done")
        s_dn = g.sem("mlp_added")
        s_tm = g.sem("mlp_sample_scaled")

        def down_view(t):
            return t[:].rearrange("p k c -> p (k c)").rearrange("p (k c) -> p k c", k=KF)

        def up_groups(u):
            return [(u * NUP // 2 + m * 3 + c, 2 * u + m, c) for m in range(2) for c in range(3)]

        def slot_free(q_):
            return [NUP + NDN // 2 - NGR, 0, NUP // 2, NUP][q_]

        with nc.Block() as block:
            @block.sync
            def _(sp):
                with sp.Fori(0, NG) as n:
                    for p in range(4):
                        s = p % 2
                        sp.wait_ge(w.lo_done, n * 4 + p + 1)
                        if p < 2:
                            src = w_up[:, bass.ds(n * FB + p * PANEL, PANEL)].rearrange("(k p) c -> p k c", p=P)
                            sp.dma_start(w.raw[s][:], src).then_inc(w.loaded[s], 16)
                        else:
                            src = w_down[bass.ds(n * FB, FB), (p - 2) * 512:(p - 1) * 512].rearrange("(k p) c -> p k c", p=P)
                            sp.dma_start(down_view(w.raw[s]), src).then_inc(w.loaded[s], 16)

            def blocks(eng, split, work):
                def block_(n, more):
                    for p in range(4):
                        if p < 3:
                            split(n, p + 1)
                        elif more:
                            split(n + 1, 0)
                        work(n, p)
                split(0, 0)
                with eng.Fori(0, NG - 1) as n:
                    block_(n, True)
                block_(NG - 1, False)

            @block.gpsimd
            def _(pool):
                pool.sem_inc(w.lo_done, 2)

                def split(n, p):
                    s = p % 2
                    pool.wait_ge(w.hi_done, n * 4 + p + 1)
                    pool.tensor_tensor(w.lo[s][:], w.raw[s][:], w.hi[s][:], ALU.subtract).then_inc(w.lo_done, 1)

                def work(n, p):
                    if p < 2:
                        for i, m, c in up_groups(p):
                            t0, tw = CHUNKS[c]
                            pool.wait_ge(s_ah, n * NUP + i + 1)
                            pool.tensor_tensor(a_lo[:, m, t0:t0 + tw], q[i % 3][:, 0:tw], a_hi[:, m, t0:t0 + tw],
                                               ALU.subtract).then_inc(s_al, 1)

                blocks(pool, split, work)

            @block.scalar
            def _(act):
                act.sem_inc(s_al, 3)

                def split(n, p):
                    s = p % 2
                    act.wait_ge(w.loaded[s], (n * 2 + p // 2) * 16 + 16)
                    act.wait_ge(s_mm, n * NGR + (NGR + slot_free(p)))
                    act.copy(w.hi[s][:], w.raw[s][:]).then_inc(w.hi_done, 1)

                def work(n, p):
                    if p < 2:
                        def hi(i, m, c):
                            t0, tw = CHUNKS[c]
                            act.wait_ge(s_sq, n * NUP + i + 1)
                            act.copy(a_hi[:, m, t0:t0 + tw], q[i % 3][:, 0:tw]).then_inc(s_ah, 1)
                        before = None
                        for i, m, c in up_groups(p):
                            tw = CHUNKS[c][1]
                            act.wait_ge(s_mm, NGR + n * NGR + i + 1)
                            act.wait_ge(s_al, n * NUP + i + 1)
                            act.activation(r[i % 3][:, 0:tw], g.bank[i % NBANK][:, 0:tw], ACT.Relu).then_inc(s_re, 1)
                            if before:
                                hi(*before)
                            before = (i, m, c)
                        hi(*before)

                blocks(act, split, work)

            @block.vector
            def _(dve):
                dve.sem_inc(s_dn, NDN)
                dve.sem_inc(s_tm, 2)
                with dve.Fori(0, NG) as n:
                    for i in range(NUP):
                        tw = CHUNKS[i % 3][1]
                        dve.wait_ge(s_re, n * NUP + i + 1)
                        dve.tensor_tensor(q[i % 3][:, 0:tw], r[i % 3][:, 0:tw], r[i % 3][:, 0:tw], ALU.mult).then_inc(s_sq, 1)
                    for i in range(NDN):
                        kc, c = divmod(i, 3)
                        t0, tw = CHUNKS[c]
                        pw = min(tw, TP - t0)
                        b = g.bank[(NUP + i) % NBANK]
                        dve.wait_ge(s_mm, NGR + n * NGR + NUP + i + 1)
                        dve.wait_ge(s_dn, n * NDN + i + 1)
                        if c == 2:
                            t = tmp[kc % 2]
                            dve.tensor_tensor(by_seq(t[:]), by_seq(b[:, pw:tw]), seq_row(g.modT[:, GA2 * KD + kc, 1:NMOD]),
                                              ALU.mult).then_inc(s_tm, 1)
                            dve.wait_ge(s_tm, n * KD + kc + 3)
                            dve.tensor_tensor(g.x1T[:, kc, TP:T], g.x1T[:, kc, TP:T], t[:], ALU.add)
                        out = g.x1T[:, kc, t0:t0 + pw]
                        dve.scalar_tensor_tensor(out=out, in0=b[:, 0:pw], scalar=g.mod(GA2, kc), in1=out, op0=ALU.mult,
                                                 op1=ALU.add).then_inc(s_dn, 1)

            @block.tensor
            def _(pe):
                pe.sem_inc(s_mm, NGR)
                with pe.Fori(0, NG) as n:
                    def bank_free(i):
                        p = i - NBANK
                        if p < 0:
                            pe.wait_ge(s_dn, n * NDN + NDN + p + 1)
                        elif p < NUP:
                            pe.wait_ge(s_re, n * NUP + p + 1)
                        else:
                            pe.wait_ge(s_dn, n * NDN + NDN + p - NUP + 1)

                    for u in range(2):
                        pe.wait_ge(w.lo_done, n * 4 + u + 3)
                        for i, m, c in up_groups(u):
                            t0, tw = CHUNKS[c]
                            bank_free(i)
                            cols = slice((m % 2) * P, (m % 2 + 1) * P)
                            for k in range(KD):
                                last = three_products(pe, g.bank[i % NBANK][:, 0:tw], w.hi[u][:, k, cols], w.lo[u][:, k, cols],
                                                      h_hi[:, k, t0:t0 + tw], h_lo[:, k, t0:t0 + tw], k, KD)
                            last.then_inc(s_mm, 1)
                    for d in range(2):
                        pe.wait_ge(w.lo_done, n * 4 + d + 5)
                        hi, lo = down_view(w.hi[d]), down_view(w.lo[d])
                        for j in range(NDN // 2):
                            m, c = divmod(j, 3)
                            i = NUP + d * NDN // 2 + j
                            t0, tw = CHUNKS[c]
                            bank_free(i)
                            cols = slice(m * P, (m + 1) * P)
                            for k in range(KF):
                                if d == 0 and j < 3:
                                    pe.wait_ge(s_al, 3 + n * NUP + 3 * k + c + 1)
                                last = three_products(pe, g.bank[i % NBANK][:, 0:tw], hi[:, k, cols], lo[:, k, cols],
                                                      a_hi[:, k, t0:t0 + tw], a_lo[:, k, t0:t0 + tw], k, KF)
                            last.then_inc(s_mm, 1)


def stage_final(g):
    nc, io = g.nc, g.io
    N9 = NT + 1
    yp = io["y_prompt"][0]
    ys = io["y_sample"].rearrange("s t d -> (s t) d")
    with ExitStack() as ctx:
        sb = lambda *a: g.sb(*a, ctx=ctx)
        gain = sb("fin_gain", [P, D])
        sq = [sb(f"fin_sq{i}", [P, D]) for i in range(2)]
        ss = sb("fin_ss", [P, N9, 2])
        rs = sb("fin_rstd", [P, N9])
        y = [sb(f"fin_y{i}", [P, D]) for i in range(3)]
        s_g = g.sem("fin_gain_loaded")
        s_tr = g.sem("fin_turned")
        s_sq = g.sem("fin_squared")
        s_su = g.sem("fin_summed")
        s_ln = g.sem("fin_ln")
        s_rs = g.sem("fin_rstd_done")
        s_y = g.sem("fin_y_done")
        s_out = [g.sem(f"fin_y{i}_stored") for i in range(3)]
        with nc.Block() as block:
            @block.sync
            def _(sp):
                sp.dma_start(gain[:], io["g_final"].rearrange("(o d) -> o d", o=1).to_broadcast([P, D])).then_inc(s_g, 16)
                for i in range(N9):
                    w = P if i < NT else TS
                    sp.wait_ge(s_y, 2 * i + 2)
                    sp.dma_start(yp[i * P:(i + 1) * P] if i < NT else ys, y[i % 3][0:w]).then_inc(s_out[i % 3], 16)
                for i in range(3):
                    sp.wait_ge(s_out[i], 16 * 3)

            @block.tensor
            def _(pe):
                for i in range(N9):
                    w = P if i < NT else TS
                    for half in range(2):
                        if i >= 4:
                            pe.wait_ge(s_y, 2 * (i - 4) + half + 1)
                        for k in range(4):
                            last = pe.transpose(g.bank[(2 * i + half) % 8][0:w, k * P:(k + 1) * P],
                                                g.x1T[:, half * 4 + k, i * P:i * P + w], g.ident[:])
                        last.then_inc(s_tr, 1)

            @block.scalar
            def _(act):
                for i in range(N9):
                    w = P if i < NT else TS
                    for half in range(2):
                        act.wait_ge(s_tr, 2 * i + half + 1)
                        if i >= 2:
                            act.wait_ge(s_sq, 2 * (i - 2) + half + 1)
                        act.activation(sq[i % 2][0:w, half * 512:half * 512 + 512], g.bank[(2 * i + half) % 8][0:w], ACT.Square,
                                       accum_out=ss[0:w, i, half:half + 1]).then_inc(s_sq, 1)
                    act.wait_ge(s_su, i + 1)
                    act.activation(rs[0:w, i:i + 1], rs[0:w, i:i + 1], ACT.Ln, scale=1.0 / D, bias=g.eps[0:w]).then_inc(s_ln, 1)
                    act.wait_ge(s_ln, i + 1)
                    act.activation(rs[0:w, i:i + 1], rs[0:w, i:i + 1], ACT.Exp, scale=-0.5).then_inc(s_rs, 1)

            @block.vector
            def _(dve):
                dve.wait_ge(s_g, 16)
                for i in range(N9):
                    w = P if i < NT else TS
                    dve.wait_ge(s_sq, 2 * i + 2)
                    dve.tensor_tensor(rs[0:w, i:i + 1], ss[0:w, i, 0:1], ss[0:w, i, 1:2], ALU.add).then_inc(s_su, 1)
                    dve.wait_ge(s_rs, i + 1)
                    if i >= 3:
                        dve.wait_ge(s_out[i % 3], 16 * (i // 3))
                    for half in range(2):
                        cols = slice(half * 512, half * 512 + 512)
                        dve.scalar_tensor_tensor(out=y[i % 3][0:w, cols], in0=g.bank[(2 * i + half) % 8][0:w], scalar=rs[0:w, i:i + 1],
                                                 in1=gain[0:w, cols], op0=ALU.mult, op1=ALU.mult).then_inc(s_y, 1)


def build(nc, io):
    with ExitStack() as ctx:
        g = Program(nc, io, ctx)
        stage_constants_and_adaln(g)
        g.op_hi = g.sb("op_hi", [P, KD, T], F32R)
        g.op_lo = g.sb("op_lo", [P, KD, T], F32R)
        stage_norm_mix(g, g.op_hi, g.op_lo)
        stage_project_in(g, g.op_hi, g.op_lo)
        with ExitStack() as c:
            g.vnat = g.sb("vnat", [P, NT + 1, SB], ctx=c)
            with g.part():
                stage_natural(g)
                stage_sample_attention(g)
                stage_prompt_attention(g)
        with g.part():
            stage_gla(g)
        g.x1T = g.sb("x1T", [P, KD, T])
        stage_project_out(g)
        stage_norm_ffn(g, g.op_hi, g.op_lo)
        stage_mlp(g, g.op_hi, g.op_lo)
        stage_final(g)


OUTS = [("y_prompt", (1, TP, D)), ("y_sample", (NSEQ, NEW, D)),
        ("k_prompt", (1, 1, TP, HEADS, HD)), ("v_prompt", (1, 1, TP, HEADS, HD)),
        ("state_prompt", (1, 1, GH, GK, GV)),
        ("k_sample", (1, NSEQ, NEW, HEADS, HD)), ("v_sample", (1, NSEQ, NEW, HEADS, HD)),
        ("state_sample", (1, NSEQ, GH, GK, GV))]

INS = ["x_prompt", "x_sample", "c_prompt", "c_sample", "cache_k", "cache_v", "state_gla", "page_table", "w_ada", "b_ada",
       "g_mix", "w_in", "b_sb", "w_gla_gate", "b_gla_gate", "g_gla_out", "w_out", "g_ffn", "w_up", "w_down", "g_final"]


def kernel(**inputs):
    import numpy as np
    from concourse import bacc
    from concourse.bass_utils import run_bass_kernel_spmd

    nc = bacc.Bacc("TRN2", target_bir_lowering=False, num_devices=1)
    arrays, io = {}, {}
    for name in INS:
        a = np.ascontiguousarray(inputs[name])
        arrays[f"in_{name}"] = a
        io[name] = nc.dram_tensor(f"in_{name}", a.shape, mybir.dt.from_np(a.dtype), kind="ExternalInput").ap()
    for name, shape in OUTS:
        io[name] = nc.dram_tensor(name, shape, F32, kind="ExternalOutput").ap()
    build(nc, io)
    r = run_bass_kernel_spmd(nc, [arrays], core_ids=[0])
    return tuple(r.results[0][name] for name, _ in OUTS)
```

```python
from contextlib import ExitStack, contextmanager

import concourse.bass as bass
from concourse import mybir

F32 = mybir.dt.float32
F32R = mybir.dt.float32r
BF16 = mybir.dt.bfloat16
ALU = mybir.AluOpType
ACT = mybir.ActivationFunctionType

P = 128
D = 1024
KD = D // P
TP = 1024
NSEQ, NEW = 8, 8
TS = NSEQ * NEW
T = TP + TS
NT = TP // P
PAGE = 128
NPAGE = 8
HEADS, HD = 8, 64
SB = HEADS * HD
GH, GK, GV = 4, 64, 128
RANK = 16
IN_W = 3 * SB + 2 * GH * GK + 2 * GH * GV + RANK
FF = 4096
EPS = 1e-6
GATE = 1.0 / 16.0
NEG = -1e30
BIG = 3e38
PANEL = 256
NMOD = 1 + NSEQ
CHUNKS = [(0, 384), (384, 384), (768, 320)]
SUB = 32
ROW_Q, ROW_K, ROW_V = 0, SB, 2 * SB
ROW_QG = 3 * SB
ROW_KG = ROW_QG + GH * GK
ROW_VG = ROW_KG + GH * GK
ROW_RG = ROW_VG + GH * GV
ROW_A = ROW_RG + GH * GV
LAST = IN_W - P
VEC_B = 2 * KD + 3
SH1, SC1, GA1, SH2, SC2, GA2 = range(6)


class Program:

    def __init__(self, nc, io, ctx):
        self.nc, self.io, self.ctx = nc, io, ctx
        self.bank = [ctx.enter_context(nc.psum_tensor(f"bank{i}", [P, 512], F32)) for i in range(8)]
        self.ident = self.sb("ident", [P, P])
        self.ident16 = self.sb("ident16", [P, P], BF16)
        self.causal16 = self.sb("causal16", [P, P], BF16)
        self.modT = self.sb("modT", [P, 6 * KD, NMOD])
        self.vecT = self.sb("vecT", [P, VEC_B + 6 * KD])
        self.cT = self.sb("cT", [P, KD, NMOD])
        self.mul1 = self.sb("mul1", [P, KD, NMOD])
        self.mul2 = self.sb("mul2", [P, KD, NMOD])
        self.sample_o = self.sb("sample_o", [P, 4, NSEQ, NEW])
        self.eps = self.sb("eps", [P, 1])
        self.projT = nc.dram_tensor("projT", [IN_W, T], F32, kind="Internal").ap()
        self.vgnat = nc.dram_tensor("vgnat", [T, GH * GV], F32, kind="Internal").ap()

    def sb(self, name, shape, dt=F32, ctx=None):
        return (ctx or self.ctx).enter_context(self.nc.sbuf_tensor(name, shape, dt))

    def sem(self, name):
        return self.nc.alloc_semaphore(name=name)

    @contextmanager
    def part(self):
        before = self.nc.snapshot_sems()
        yield
        self.nc.clear_and_free_semaphores(self.nc.allocated_since(before))
        self.nc.all_engine_barrier()

    def mod(self, part, kc, row=0):
        return self.modT[:, part * KD + kc, row:row + 1]


def seq_row(a, n=NSEQ, w=NEW):
    return a.rearrange("p (s o) -> p s o", o=1).to_broadcast([P, n, w])


def by_seq(a):
    return a.rearrange("p (s t) -> p s t", s=NSEQ)


def condition(pe, g, bank, w, k0, n):
    for k in range(k0, k0 + n):
        last = pe.matmul(bank[0:NMOD, :], g.cT[:, k, :], w[:, k - k0, :], start=(k == 0), stop=(k == KD - 1))
    return last


def turn_rows(pe, g, bank, c0, rows):
    for m in range(4):
        last = pe.transpose(bank[:, c0 + m * NMOD:c0 + (m + 1) * NMOD], rows[:, m * P:(m + 1) * P], g.ident[0:NMOD, 0:NMOD])
    return last


def add_bias(dve, g, bank, c0, tile, n):
    bias = g.vecT[:, VEC_B + tile:VEC_B + tile + n].rearrange("p (m o) -> p m o", o=1).to_broadcast([P, n, NMOD])
    src = bank[:, c0:c0 + n * NMOD].rearrange("p (m r) -> p m r", m=n)
    return dve.tensor_tensor(g.modT[:, tile:tile + n, :], src, bias, ALU.add)


def scale_gain(dve, g, mul, part, at):
    gain = g.vecT[:, at:at + KD].rearrange("p (k o) -> p k o", o=1).to_broadcast([P, KD, NMOD])
    return dve.scalar_tensor_tensor(out=mul[:], in0=g.modT[:, part * KD:(part + 1) * KD, :], scalar=1.0, in1=gain,
                                    op0=ALU.add, op1=ALU.mult)


def stage_start(g):
    nc, io = g.nc, g.io
    hT_hi, hT_lo = g.op_hi, g.op_lo
    GROUPS = [(0, 4), (4, 4), (8, 1)]
    xp = io["x_prompt"][0]
    xs = io["x_sample"].rearrange("s t d -> (s t) d")
    NCH = 2 * D // 512
    with ExitStack() as ctx:
        sb = lambda *a: g.sb(*a, ctx=ctx)
        c_in = sb("ada_c", [NMOD, D])
        cx = sb("ada_cx", [P, KD, NMOD])
        w = [sb(f"ada_w{i}", [P, KD, 512]) for i in range(NCH)]
        rows = [sb(f"ada_rows{i}", [NMOD, 512]) for i in range(2)]
        vec = sb("ada_vec", [VEC_B + 6 * KD, P])
        x = [sb(f"n1_x{i}", [P, D]) for i in range(9)]
        sq = sb("n1_sq", [P, D])
        ss = sb("n1_ss", [P, 9])
        tmp = [sb(f"n1_tmp{i}", [P, 512]) for i in range(3)]
        s_cin = g.sem("ada_c_loaded")
        s_vec = g.sem("ada_vectors_loaded")
        s_w = [g.sem(f"ada_w{i}_loaded") for i in range(NCH)]
        s_const = g.sem("ada_const")
        s_eps = g.sem("eps_set")
        s_cT = g.sem("ada_c_transposed")
        s_cx = g.sem("ada_cx_copied")
        s_e = g.sem("ada_exp")
        s_silu = g.sem("ada_silu")
        s_vT = g.sem("ada_vectors_transposed")
        s_mm = g.sem("ada_chunk_summed")
        s_row = g.sem("ada_rows_copied")
        s_rT = g.sem("ada_rows_transposed")
        s_mod = g.sem("ada_mod_done")
        s_x = [g.sem(f"n1_x{i}_loaded") for i in range(9)]
        s_ss = g.sem("n1_sumsq")
        s_ln = g.sem("n1_ln")
        s_rstd = g.sem("n1_rstd")
        s_xn = g.sem("n1_normed")
        s_tr = g.sem("n1_transposed")
        s_tmp = g.sem("n1_modulated")
        s_dtmp = g.sem("n1_sample_steps")
        s_hi = g.sem("n1_hi")
        s_lo = g.sem("n1_lo")
        steps = [(gi, t0, n, k) for gi, (t0, n) in enumerate(GROUPS) for k in range(KD)]
        NB, NPR = 4, 2 * KD
        with nc.Block() as block:
            @block.sync
            def _(sp):
                sp.dma_start(c_in[0:1, :], io["c_prompt"]).then_inc(s_cin, 16)
                sp.dma_start(c_in[1:NMOD, :], io["c_sample"]).then_inc(s_cin, 16)
                for i in range(9):
                    if i % 2 == 0 and i // 2 < NCH:
                        cols = slice(i // 2 * 512, i // 2 * 512 + 512)
                        sp.dma_start(w[i // 2][:], io["w_ada"][0][:, cols].rearrange("(k p) c -> p k c", p=P)).then_inc(s_w[i // 2], 16)
                    src = xp[i * P:(i + 1) * P, :] if i < 8 else xs
                    sp.dma_start(x[i][0:src.shape[0], :], src).then_inc(s_x[i], 16)

            @block.gpsimd
            def _(pool):
                pool.memset(g.ident[:], 0.0).then_inc(s_const, 1)
                pool.memset(g.causal16[:], NEG).then_inc(s_const, 1)
                pool.wait_ge(s_const, 2)
                pool.affine_select(out=g.ident[:], in_=g.ident[:], compare_op=ALU.not_equal, fill=1.0,
                                   base=0, pattern=[[-1, P]], channel_multiplier=1).then_inc(s_const, 1)
                pool.affine_select(out=g.causal16[:], in_=g.causal16[:], compare_op=ALU.is_ge, fill=0.0,
                                   base=0, pattern=[[1, P]], channel_multiplier=-1).then_inc(s_const, 1)
                pool.wait_ge(s_const, 4)
                pool.tensor_copy(g.ident16[:], g.ident[:]).then_inc(s_const, 1)

            @block.scalar
            def _(act):
                at = 0
                for name, n in (("g_mix", KD), ("g_ffn", KD), ("b_gla_gate", 2), ("g_gla_out", 1), ("b_ada", 6 * KD)):
                    act.dma_start(vec[at:at + n, :], io[name].rearrange("a (k p) -> (a k) p", p=P)).then_inc(s_vec, 16)
                    at += n
                act.preload_act_table_set("natural_log_exp_and_others")
                act.wait_ge(s_cx, 1)
                act.activation(g.cT[:], cx[:], ACT.Exp, scale=-1.0).then_inc(s_e, 1)
                act.wait_ge(s_eps, 1)
                for i in range(9):
                    n = P if i < 8 else TS
                    act.wait_ge(s_x[i], 16)
                    act.activation(sq[0:n, :], x[i][0:n, :], ACT.Square, accum_out=ss[0:n, i:i + 1]).then_inc(s_ss, 1)
                    act.wait_ge(s_ss, i + 1)
                    act.activation(ss[0:n, i:i + 1], ss[0:n, i:i + 1], ACT.Ln, scale=1.0 / D, bias=g.eps[0:n, :]).then_inc(s_ln, 1)
                    act.wait_ge(s_ln, i + 1)
                    act.activation(ss[0:n, i:i + 1], ss[0:n, i:i + 1], ACT.Exp, scale=-0.5).then_inc(s_rstd, 1)
                act.wait_ge(s_mod, 2)
                for j, (gi, t0, n, k) in enumerate(steps[:NPR]):
                    act.wait_ge(s_tr, j + 1)
                    if j >= 3:
                        act.wait_ge(s_lo, j - 2)
                    for out, done in ((hT_hi[:, k, t0 * P:t0 * P + 512], s_hi), (tmp[j % 3][:], s_tmp)):
                        act.activation(out, g.bank[j % NB][:], ACT.Identity, scale=g.mul1[:, k, 0:1], bias=g.mod(SH1, k)).then_inc(done, 1)

            @block.vector
            def _(dve):
                dve.memset(g.eps[:], EPS).then_inc(s_eps, 1)
                dve.wait_ge(s_cT, 1)
                dve.tensor_copy(cx[:].rearrange("p k r -> p (k r)"), g.bank[7][:, 0:KD * NMOD]).then_inc(s_cx, 1)
                dve.wait_ge(s_e, 1)
                dve.tensor_scalar(g.cT[:], g.cT[:], 1.0, None, ALU.add).then_inc(s_silu, 1)
                dve.wait_ge(s_silu, 1)
                dve.reciprocal(g.cT[:], g.cT[:]).then_inc(s_silu, 1)
                dve.wait_ge(s_silu, 2)
                dve.tensor_tensor(g.cT[:], cx[:], g.cT[:], ALU.mult).then_inc(s_silu, 1)
                dve.wait_ge(s_vT, 1)
                dve.tensor_copy(g.vecT[:], g.bank[6][:, 0:VEC_B + 6 * KD]).then_inc(s_mod, 1)
                for i in range(9):
                    n = P if i < 8 else TS
                    dve.wait_ge(s_rstd, i + 1)
                    dve.tensor_scalar(x[i][0:n, :], x[i][0:n, :], ss[0:n, i:i + 1], None, ALU.mult).then_inc(s_xn, 1)
                    if i % 2 == 0 and i >= 2:
                        j = i // 2 - 1
                        dve.wait_ge(s_mm, j + 1)
                        if j >= 2:
                            dve.wait_ge(s_rT, j - 1)
                        dve.tensor_copy(rows[j % 2][:], g.bank[4 + j % 2][0:NMOD, :]).then_inc(s_row, 1)
                dve.wait_ge(s_rT, NCH)
                dve.wait_ge(s_mod, 1)
                add_bias(dve, g, g.bank[7], 0, 0, 2 * KD).then_inc(s_silu, 1)
                dve.wait_ge(s_silu, 4)
                scale_gain(dve, g, g.mul1, SC1, 0).then_inc(s_mod, 1)
                for j, (gi, t0, n, k) in enumerate(steps):
                    t = tmp[j % 3]
                    if n > 1:
                        dve.wait_ge(s_hi, j + 1)
                        dve.wait_ge(s_tmp, j + 1)
                        dve.tensor_tensor(hT_lo[:, k, t0 * P:t0 * P + 512], t[:], hT_hi[:, k, t0 * P:t0 * P + 512],
                                          ALU.subtract).then_inc(s_lo, 1)
                    else:
                        done = 3 * (j - NPR)
                        if j == NPR:
                            dve.wait_ge(s_mod, 2)
                        dve.wait_ge(s_tr, j + 1)
                        dve.wait_ge(s_lo, j - 2)
                        dve.tensor_tensor(by_seq(t[:, 0:TS]), by_seq(g.bank[j % NB][:, 0:TS]), seq_row(g.mul1[:, k, 1:NMOD]),
                                          ALU.mult).then_inc(s_dtmp, 1)
                        dve.wait_ge(s_dtmp, done + 1)
                        dve.tensor_tensor(by_seq(t[:, 0:TS]), by_seq(t[:, 0:TS]), seq_row(g.modT[:, SH1 * KD + k, 1:NMOD]),
                                          ALU.add).then_inc(s_dtmp, 1)
                        dve.wait_ge(s_dtmp, done + 2)
                        dve.tensor_copy(hT_hi[:, k, TP:T], t[:, 0:TS]).then_inc(s_dtmp, 1)
                        dve.wait_ge(s_dtmp, done + 3)
                        dve.tensor_tensor(hT_lo[:, k, TP:T], t[:, 0:TS], hT_hi[:, k, TP:T], ALU.subtract).then_inc(s_lo, 1)

            @block.tensor
            def _(pe):
                pe.wait_ge(s_cin, 32)
                pe.wait_ge(s_const, 5)
                for k in range(KD):
                    last = pe.transpose(g.bank[7][:, k * NMOD:(k + 1) * NMOD], c_in[:, k * P:(k + 1) * P], g.ident[0:NMOD, 0:NMOD])
                last.then_inc(s_cT, 1)
                pe.wait_ge(s_vec, 5 * 16)
                nv = VEC_B + 6 * KD
                pe.transpose(g.bank[6][:, 0:nv], vec[:], g.ident[0:nv, 0:nv]).then_inc(s_vT, 1)
                pe.wait_ge(s_silu, 3)

                def chunk(i):
                    pe.wait_ge(s_w[i], 16)
                    if i >= 2:
                        pe.wait_ge(s_row, i - 1)
                    condition(pe, g, g.bank[4 + i % 2], w[i], 0, KD).then_inc(s_mm, 1)

                def turn_chunk(i):
                    pe.wait_ge(s_row, i + 1)
                    turn_rows(pe, g, g.bank[7], 4 * i * NMOD, rows[i % 2]).then_inc(s_rT, 1)

                def turn(j):
                    gi, t0, n, k = steps[j]
                    pe.wait_ge(s_xn, t0 + n)
                    if j >= NB:
                        pe.wait_ge(s_lo, j - NB + 1)
                    for i in range(n):
                        m = P if n > 1 else TS
                        last = pe.transpose(g.bank[j % NB][:, i * P:i * P + m], x[t0 + i][0:m, k * P:(k + 1) * P],
                                            g.ident[0:m, 0:m])
                    last.then_inc(s_tr, 1)

                chunk(0)
                for i in range(1, NCH):
                    chunk(i)
                    turn_chunk(i - 1)
                turn_chunk(NCH - 1)
                for j in range(NB):
                    turn(j)
                for j in range(NB, len(steps)):
                    turn(j)


class Panels:

    def __init__(self, g, ctx, tag):
        self.raw = [g.sb(f"{tag}_raw{i}", [P, KD, PANEL], ctx=ctx) for i in range(2)]
        self.hi = [g.sb(f"{tag}_hi{i}", [P, KD, PANEL], F32R, ctx=ctx) for i in range(2)]
        self.lo = [g.sb(f"{tag}_lo{i}", [P, KD, PANEL], F32R, ctx=ctx) for i in range(2)]
        self.loaded = [g.sem(f"{tag}_raw{i}_loaded") for i in range(2)]
        self.hi_done = g.sem(f"{tag}_hi_done")
        self.lo_done = g.sem(f"{tag}_lo_done")


def three_products(pe, out, w_hi, w_lo, x_hi, x_lo, k, nk):
    pe.matmul(out, w_hi, x_hi, start=(k == 0), stop=False)
    pe.matmul(out, w_hi, x_lo, start=False, stop=False)
    return pe.matmul(out, w_lo, x_hi, start=False, stop=(k == nk - 1))


def stage_project_in(g, hT_hi, hT_lo):
    nc, io = g.nc, g.io
    w_in = io["w_in"][0]
    NP = ROW_QG // PANEL
    assert NP % 2 == 0
    with ExitStack() as ctx:
        w = Panels(g, ctx, "in")
        stg = [g.sb(f"in_stage{i}", [P, T], ctx=ctx) for i in range(4)]
        s_mm = g.sem("in_group_summed")
        s_aev = g.sem("in_act_evacuated")
        s_dev = g.sem("in_dve_evacuated")
        s_out = [g.sem(f"in_stage{i}_stored") for i in range(4)]
        last_w = slice(0, P)
        with nc.Block() as block:
            @block.sync
            def _(sp):
                def load(s, cols, n):
                    src = w_in[:, cols].rearrange("(k p) c -> p k c", p=P)
                    sp.dma_start(w.raw[s][:, :, 0:n], src).then_inc(w.loaded[s], 16)

                with sp.Fori(0, NP // 2) as n:
                    for s in range(2):
                        sp.wait_ge(w.lo_done, n * 2 + s + 1)
                        load(s, bass.ds((n * 2 + s) * PANEL, PANEL), PANEL)
                sp.wait_ge(w.lo_done, NP + 1)
                load(0, slice(LAST, IN_W), P)

            @block.gpsimd
            def _(pool):
                pool.sem_inc(w.lo_done, 2)
                with pool.Fori(0, NP // 2) as n:
                    for s in range(2):
                        pool.wait_ge(w.hi_done, n * 2 + s + 1)
                        pool.tensor_tensor(w.lo[s][:], w.raw[s][:], w.hi[s][:], ALU.subtract).then_inc(w.lo_done, 1)
                pool.wait_ge(w.hi_done, NP + 1)
                pool.tensor_tensor(w.lo[0][:, :, last_w], w.raw[0][:, :, last_w], w.hi[0][:, :, last_w],
                                   ALU.subtract).then_inc(w.lo_done, 1)

            @block.tensor
            def _(pe):
                pe.sem_inc(s_mm, 12)

                def groups(s, n, tiles):
                    for m in range(tiles):
                        for c, (t0, tw) in enumerate(CHUNKS):
                            gi = m * 3 + c
                            pe.wait_ge(s_dev if gi % 2 else s_aev, n * 6 + s * 3 + gi // 2 + 1)
                            for k in range(KD):
                                cols = slice(m * P, (m + 1) * P)
                                last = three_products(pe, g.bank[gi][:, 0:tw], w.hi[s][:, k, cols], w.lo[s][:, k, cols],
                                                      hT_hi[:, k, t0:t0 + tw], hT_lo[:, k, t0:t0 + tw], k, KD)
                            last.then_inc(s_mm, 1)

                with pe.Fori(0, NP // 2) as n:
                    for s in range(2):
                        pe.wait_ge(w.lo_done, 2 + n * 2 + s + 1)
                        groups(s, n, 2)
                pe.wait_ge(w.lo_done, 2 + NP + 1)
                groups(0, NP // 2, 1)

            def evacuate(eng, copy, mine, s_ev, prime):
                if prime:
                    eng.sem_inc(s_ev, 3)

                def groups(s, n, tiles):
                    for gi in range(3 * tiles):
                        if gi % 2 != mine:
                            continue
                        m, c = divmod(gi, 3)
                        t0, tw = CHUNKS[c]
                        st = 2 * s + m
                        eng.wait_ge(s_mm, 12 + n * 12 + s * 6 + gi + 1)
                        eng.wait_ge(s_out[st], n * 16 + 16)
                        copy(stg[st][:, t0:t0 + tw], g.bank[gi][:, 0:tw]).then_inc(s_ev, 1)

                with eng.Fori(0, NP // 2) as n:
                    for s in range(2):
                        groups(s, n, 2)
                groups(0, NP // 2, 1)

            @block.vector
            def _(dve):
                evacuate(dve, dve.tensor_copy, 1, s_dev, True)

            @block.scalar
            def _(act):
                for i in range(4):
                    act.sem_inc(s_out[i], 16)
                act.sem_inc(s_aev, 3)

                def groups(s, n, tiles):
                    for gi in range(3 * tiles):
                        m, c = divmod(gi, 3)
                        t0, tw = CHUNKS[c]
                        st = 2 * s + m
                        if gi % 2 == 0:
                            act.wait_ge(s_mm, 12 + n * 12 + s * 6 + gi + 1)
                            act.wait_ge(s_out[st], n * 16 + 16)
                            act.copy(stg[st][:, t0:t0 + tw], g.bank[gi][:, 0:tw]).then_inc(s_aev, 1)
                        if c == 2:
                            act.wait_ge(s_aev, 3 + n * 6 + s * 3 + (gi // 2 + 1))
                            act.wait_ge(s_dev, 3 + n * 6 + s * 3 + (gi + 1) // 2)
                            if tiles == 2:
                                dst, src = g.projT[bass.ds((n * 4 + st) * P, P), :], stg[st][:]
                            else:
                                dst, src = g.projT[ROW_A:IN_W, :], stg[st][P - RANK:P, :]
                            act.dma_start(dst, src).then_inc(s_out[st], 16)

                def round_hi(s, n, cols):
                    act.wait_ge(w.loaded[s], n * 16 + 16)
                    act.wait_ge(s_mm, n * 12 + s * 6 + 6)
                    act.copy(w.hi[s][:, :, cols], w.raw[s][:, :, cols]).then_inc(w.hi_done, 1)

                round_hi(0, 0, slice(0, PANEL))
                with act.Fori(0, NP // 2 - 1) as n:
                    round_hi(1, n, slice(0, PANEL))
                    groups(0, n, 2)
                    round_hi(0, n + 1, slice(0, PANEL))
                    groups(1, n, 2)
                round_hi(1, NP // 2 - 1, slice(0, PANEL))
                groups(0, NP // 2 - 1, 2)
                round_hi(0, NP // 2, last_w)
                groups(1, NP // 2 - 1, 2)
                groups(0, NP // 2, 1)
                act.wait_ge(s_out[0], 16 * (NP // 2 + 2))
                for i in range(1, 4):
                    act.wait_ge(s_out[i], 16 * (NP // 2 + 1))


def stage_natural(g):
    nc, io = g.nc, g.io
    kinds = [(ROW_K, "k"), (ROW_V, "v"), (ROW_VG, "vg")]
    steps = [(a, tt) for a in range(3) for tt in range(NT + 1)]
    NB = 6
    with ExitStack() as ctx:
        src = [g.sb(f"nat_src{i}", [P, 4, T], ctx=ctx) for i in range(3)]
        knat = g.sb("nat_k", [P, NT + 1, SB], ctx=ctx)
        vgn = g.sb("nat_vg", [P, NT + 1, GH * GV], ctx=ctx)
        dst = [knat, g.vnat, vgn]
        stores = [(io[n + "_prompt"].rearrange("l b (n p) h d -> p (l b n) (h d)", p=P),
                   io[n + "_sample"].rearrange("l s t h d -> (l s t) (h d)")) for n in ("k", "v")]
        stores += [(g.vgnat[0:TP].rearrange("(n p) c -> p n c", p=P), g.vgnat[TP:T])]
        s_src = [g.sem(f"nat_src{i}_loaded") for i in range(3)]
        s_tr = g.sem("nat_transposed")
        s_act = g.sem("nat_act_copied")
        s_dve = g.sem("nat_dve_copied")
        s_out = g.sem("nat_stored")
        s_oh = g.sem("nat_sample_hi")
        with nc.Block() as block:
            @block.sync
            def _(sp):
                for a, (row, _) in enumerate(kinds):
                    sp.dma_start(src[a][:], g.projT[row:row + SB, :].rearrange("(m p) t -> p m t", p=P)).then_inc(s_src[a], 16)
                for a, outs in enumerate(stores):
                    n = (a + 1) * (NT + 1)
                    sp.wait_ge(s_act, (n + 1) // 2)
                    sp.wait_ge(s_dve, n // 2)
                    sp.dma_start(outs[0], dst[a][:, 0:NT, :]).then_inc(s_out, 16)
                    sp.dma_start(outs[1], dst[a][0:TS, NT, :]).then_inc(s_out, 16)
                sp.wait_ge(s_out, 6 * 16)

            @block.tensor
            def _(pe):
                for j, (a, tt) in enumerate(steps):
                    m = P if tt < NT else TS
                    if tt == 0:
                        pe.wait_ge(s_src[a], 16)
                    if j >= NB:
                        pe.wait_ge(s_dve if j % 2 else s_act, (j - NB) // 2 + 1)
                    for f in range(4):
                        last = pe.transpose(g.bank[j % NB][0:m, f * P:(f + 1) * P], src[a][:, f, tt * P:tt * P + m], g.ident[:])
                    last.then_inc(s_tr, 1)

            def copies(eng, copy, s_done, mine):
                for j, (a, tt) in enumerate(steps):
                    if j % 2 == mine:
                        m = P if tt < NT else TS
                        eng.wait_ge(s_tr, j + 1)
                        copy(dst[a][0:m, tt, :], g.bank[j % NB][0:m, :]).then_inc(s_done, 1)

            @block.scalar
            def _(act):
                copies(act, act.copy, s_act, 0)

            @block.vector
            def _(dve):
                copies(dve, dve.tensor_copy, s_dve, 1)
                o = g.sample_o[:].rearrange("d p s q -> d p (s q)")
                dve.tensor_copy(g.op_hi[:, 0:4, TP:T], o).then_inc(s_oh, 1)
                dve.wait_ge(s_oh, 1)
                dve.tensor_tensor(g.op_lo[:, 0:4, TP:T], o, g.op_hi[:, 0:4, TP:T], ALU.subtract)


def at_least(eng, sem, value):
    if not isinstance(value, int) or value > 0:
        eng.wait_ge(sem, value)


def stage_project_gla_and_sample_attention(g):
    nc, io = g.nc, g.io
    w_in = io["w_in"][0]
    NTILE = (ROW_A - ROW_QG) // P
    PER = NTILE // (NSEQ // 2)
    assert PER == 3 and NTILE % PER == 0
    DENSE = [[[(0, 0), (0, 1)], [(0, 2), (1, 0)]], [[(1, 1), (1, 2)], [(2, 0), (2, 1), (2, 2)]]]
    NCOL = HEADS * NEW
    with ExitStack() as ctx:
        sb = lambda *a: g.sb(*a, ctx=ctx)
        kpg = [sb(f"sa_k{i}", [P, NPAGE, SB]) for i in range(2)]
        vpg = sb("sa_v", [P, NPAGE, SB])
        kT = sb("sa_kT", [P, 4, 4, P])
        raw = [sb(f"pg_raw{i}", [P, KD, P]) for i in range(PER)]
        whi = [sb(f"pg_hi{i}", [P, KD, P], F32R) for i in range(PER)]
        wlo = [sb(f"pg_lo{i}", [P, KD, P], F32R) for i in range(PER)]
        stg = [sb(f"pg_stage{i}", [P, T]) for i in range(PER)]
        vnewT = sb("sa_vnewT", [P, 4, TS])
        vnew = sb("sa_vnew", [TS, SB])
        qnew = sb("sa_qnew", [P, 4, TS])
        knew = sb("sa_knew", [P, 4, TS])
        qbd = sb("sa_qbd", [P, 4, NSEQ, 2, NEW])
        table = ctx.enter_context(nc.sbuf_tensor("sa_table", [1, NSEQ * NPAGE], mybir.dt.int32))
        bsb = sb("sa_bsb", [1, HEADS])
        brow = sb("sa_brow", [1, NPAGE, HEADS, NEW])
        ones = sb("sa_ones", [1, P])
        negtri = sb("sa_negtri", [P, P])
        negone = sb("sa_negone", [P, P])
        mask16 = sb("sa_mask16", [TS, NSEQ, HEADS, NEW], BF16)
        spn = sb("sa_spn", [P, NSEQ, NCOL])
        wn = sb("sa_wn", [TS, NSEQ, NCOL])
        a = sb("sa_a", [P, 512])
        sp_ = sb("sa_sp", [P, NPAGE, NCOL])
        r = sb("sa_r", [P, NPAGE, NCOL])
        w = [sb(f"sa_w{i}", [P, 512]) for i in range(2)]
        o = g.sample_o
        s_in = g.sem("sa_inputs_loaded")
        s_tab = g.sem("sa_table_loaded")
        s_k = [g.sem(f"sa_k{i}_loaded") for i in range(2)]
        s_v = g.sem("sa_v_loaded")
        s_vn = g.sem("sa_new_v_transposed")
        s_raw = [g.sem(f"pg_raw{i}_loaded") for i in range(PER)]
        s_hi = g.sem("pg_hi_done")
        s_lo = g.sem("pg_lo_done")
        s_mm = g.sem("pg_chunk_summed")
        s_ev = g.sem("pg_chunk_evacuated")
        s_st = [g.sem(f"pg_stage{i}_stored") for i in range(PER)]
        s_c = g.sem("sa_constants")
        s_cd = g.sem("sa_dve_constants")
        s_kt = g.sem("sa_k_transposed")
        s_kta = g.sem("sa_kT_act_copied")
        s_ktd = g.sem("sa_kT_dve_copied")
        s_qk = g.sem("sa_scored")
        s_zn = g.sem("sa_new_scored")
        s_act = g.sem("sa_act_chain")
        s_sp = g.sem("sa_softplus")
        s_r = g.sem("sa_later_pages_summed")
        s_sum = g.sem("sa_stay_subtracted")
        s_w = g.sem("sa_weights")
        s_pv = g.sem("sa_v_multiplied")
        s_o = g.sem("sa_out")
        O, ZN = g.bank[6], g.bank[7]
        Z = [g.bank[4], g.bank[5]]
        TB = g.bank[0:2]
        DB = [g.bank[2], g.bank[3], g.bank[7]]

        def load_pages(eng, cache, pages, s, sem):
            pool_rows = cache[0].rearrange("n p h d -> n p (h d)")
            for j in range(NPAGE):
                page = eng.value_load(table[0:1, bass.ds(s * NPAGE + j, 1)], min_val=0, max_val=pool_rows.shape[0] - 1)
                eng.dma_start(pages[:, j, :], pool_rows[bass.ds(page, 1)].rearrange("o p d -> (o p) d")).then_inc(sem, 16)

        def pairs(body):
            def on(eng):
                body(0, True)
                with eng.Fori(1, NSEQ // 2 - 1) as n:
                    body(n, True)
                body(NSEQ // 2 - 1, False)
            return on

        with nc.Block() as block:
            @block.sync
            def _(sp):
                sp.dma_start(table[:], io["page_table"].rearrange("s (o n) -> o (s n)", o=1)).then_inc(s_tab, 16)
                for t, row in ((qnew, ROW_Q), (knew, ROW_K), (vnewT, ROW_V)):
                    sp.dma_start(t[:], g.projT[row:row + SB, TP:T].rearrange("(m p) t -> p m t", p=P)).then_inc(s_in, 16)
                sp.dma_start(bsb[:], io["b_sb"]).then_inc(s_in, 16)
                sp.wait_ge(s_tab, 16)

                def k_pages(s, slot):
                    at_least(sp, s_kt, (s - 2) * NPAGE + NPAGE)
                    load_pages(sp, io["cache_k"], kpg[slot], s, s_k[slot])

                def weights(i, m):
                    at_least(sp, s_lo, i - PER + 1)
                    sp.dma_start(raw[m][:], w_in[:, bass.ds(ROW_QG + i * P, P)].rearrange("(k p) c -> p k c", p=P)).then_inc(s_raw[m], 16)

                def body(n, more):
                    k_pages(2 * n + 1, 1)
                    if more:
                        for m in range(PER):
                            weights(PER * (n + 1) + m, m)
                        k_pages(2 * n + 2, 0)

                for m in range(PER):
                    weights(m, m)
                k_pages(0, 0)
                pairs(body)(sp)

            @block.gpsimd
            def _(pool):
                pool.memset(qbd[:], 0.0).then_inc(s_c, 1)
                pool.memset(spn[:], 0.0).then_inc(s_c, 1)
                pool.memset(ones[:], 1.0).then_inc(s_c, 1)
                pool.memset(negone[:], -1.0).then_inc(s_c, 1)
                pool.memset(negtri[:], -1.0).then_inc(s_c, 1)
                pool.memset(mask16[:], 0.0).then_inc(s_c, 1)
                pool.wait_ge(s_c, 6)
                pool.affine_select(out=negtri[:], in_=negtri[:], compare_op=ALU.is_ge, fill=0.0, base=0,
                                   pattern=[[-1, P]], channel_multiplier=1).then_inc(s_c, 1)
                pool.affine_select(out=mask16[:], in_=mask16[:], compare_op=ALU.is_ge, fill=NEG, base=0,
                                   pattern=[[-NEW, NSEQ], [0, HEADS], [0, NEW]], channel_multiplier=1).then_inc(s_c, 1)
                pool.wait_ge(s_c, 8)
                pool.affine_select(out=mask16[:], in_=mask16[:], compare_op=ALU.is_gt, fill=NEG, base=0,
                                   pattern=[[NEW, NSEQ], [0, HEADS], [1, NEW]], channel_multiplier=-1).then_inc(s_c, 1)
                pool.wait_ge(s_tab, 16)

                def v_pages(s):
                    at_least(pool, s_pv, s)
                    load_pages(pool, io["cache_v"], vpg, s, s_v)

                def low(n, m):
                    pool.wait_ge(s_hi, PER * n + m + 1)
                    pool.tensor_tensor(wlo[m][:], raw[m][:], whi[m][:], ALU.subtract).then_inc(s_lo, 1)

                def body(n, more):
                    low(n, 2)
                    v_pages(2 * n)
                    if more:
                        low(n + 1, 0)
                    v_pages(2 * n + 1)
                    if more:
                        low(n + 1, 1)

                low(0, 0)
                low(0, 1)
                pairs(body)(pool)

            @block.tensor
            def _(pe):
                pe.wait_ge(s_in, 64)
                for m in range(4):
                    last = pe.transpose(O[0:TS, m * P:(m + 1) * P], vnewT[:, m, :], g.ident[:])
                last.then_inc(s_vn, 1)
                pe.wait_ge(s_c, 9)
                pe.wait_ge(s_cd, 4)
                bias = brow[:].rearrange("o j h q -> o (j h q)")
                pe.matmul(ZN[0:TS, :], ones[:, 0:TS], bias, start=True, stop=False, skip_group_check=True)
                zn = ZN[0:TS, :].rearrange("k (s p c) -> k p s c", s=NSEQ, p=4)
                for p in range(4):
                    pe.matmul(zn[:, p], knew[:, p, :], qbd[:, p].rearrange("k s h q -> k s (h q)"),
                              start=False, stop=False, skip_group_check=True)
                pe.matmul(ZN[0:TS, :], g.ident16[0:TS, 0:TS], mask16[:].rearrange("p s h q -> p (s h q)"),
                          start=False, stop=True, skip_group_check=True).then_inc(s_zn, 1)
                pe.wait_ge(s_sp, 1)
                pe.matmul(ZN[0:TS, :], negtri[0:TS, 0:TS], spn[0:TS].rearrange("k s c -> k (s c)"),
                          start=False, stop=True, skip_group_check=True).then_inc(s_zn, 1)
                pe.wait_ge(s_w, 1)
                ov = O[:].rearrange("d (s p c) -> d p s c", s=NSEQ, p=4)
                wv = wn[:].rearrange("k s (p c) -> k p s c", p=4)
                for p in range(4):
                    pe.matmul(ov[:, p], vnew[:, p * P:(p + 1) * P], wv[:, p],
                              start=(p == 0), stop=False, skip_group_check=True)

                def score(n, slot, between):
                    s = 2 * n + slot
                    at_least(pe, s_w, s)
                    pe.wait_ge(s_k[slot], n * 128 + 128)
                    pe.matmul(Z[slot][:], ones[:], bias, start=True, stop=False, skip_group_check=True)
                    for j in range(NPAGE + 1):
                        if j < NPAGE:
                            at_least(pe, s_ktd if j % 2 else s_kta, s * 4 + j // 2)
                            for p in range(4):
                                last = pe.transpose(TB[j % 2][:, p * P:(p + 1) * P], kpg[slot][:, j, p * P:(p + 1) * P], g.ident[:])
                            last.then_inc(s_kt, 1)
                            pieces(between, 2)
                        if j > 0:
                            i = j - 1
                            pe.wait_ge(s_ktd if i % 2 else s_kta, s * 4 + i // 2 + 1)
                            for p in range(4):
                                c = i * NCOL + p * 16
                                q = qbd[:, p].rearrange("k s h q -> k (s h q)")
                                last = pe.matmul(Z[slot][:, c:c + 16], kT[:, i % 4, p, :], q[:, bass.ds(s * 16, 16)],
                                                 start=False, stop=(i == NPAGE - 1), skip_group_check=True)
                            last.then_inc(s_qk, 1)

                def subtract(s, slot):
                    pe.wait_ge(s_r, s * 8 + 8)
                    pe.matmul(Z[slot][:], negtri[:], sp_[:].rearrange("k j c -> k (j c)"), start=False, stop=False, skip_group_check=True)
                    pe.matmul(Z[slot][:], negone[:], r[:].rearrange("k j c -> k (j c)"), start=False, stop=True,
                              skip_group_check=True).then_inc(s_sum, 1)

                def values(s, slot, between):
                    pe.wait_ge(s_w, s + 2)
                    pe.wait_ge(s_v, s * 128 + 128)
                    for j in range(NPAGE):
                        for p in range(4):
                            c = j * NCOL + p * 16
                            last = pe.matmul(O[:, bass.ds(s * NCOL + p * 16, 16)], vpg[:, j, p * P:(p + 1) * P],
                                             w[slot][:, c:c + 16], start=False, stop=(j == NPAGE - 1), skip_group_check=True)
                        pieces(between, 3)
                    last.then_inc(s_pv, 1)

                def pieces(of, count):
                    for _ in range(count):
                        next(of, None)

                def dense(n, chunks):
                    for m, c in chunks:
                        i = PER * n + m
                        t0, tw = CHUNKS[c]
                        if c == 0:
                            pe.wait_ge(s_lo, i + 1)
                        at_least(pe, s_ev, 3 * i + c - 2)
                        for k in range(KD):
                            last = three_products(pe, DB[c][:, 0:tw], whi[m][:, k, :], wlo[m][:, k, :],
                                                  g.op_hi[:, k, t0:t0 + tw], g.op_lo[:, k, t0:t0 + tw], k, KD)
                            if k == KD - 1:
                                last.then_inc(s_mm, 1)
                            yield

                def body(n, more):
                    for slot in range(2):
                        s = 2 * n + slot
                        score(n, slot, dense(n, DENSE[slot][0]))
                        chunks = dense(n, DENSE[slot][1])
                        if not isinstance(s, int) or s > 0:
                            values(s - 1, 1 - slot, chunks)
                        pieces(chunks, 3 * KD)
                        subtract(s, slot)

                pairs(body)(pe)
                values(NSEQ - 1, 1, iter(()))

            @block.scalar
            def _(act):
                def chain(z, out, i):
                    act.activation(out, z, ACT.Abs).then_inc(s_act, 1)
                    act.wait_ge(s_act, i * 3 + 1)
                    act.activation(out, out, ACT.Exp, scale=-1.0).then_inc(s_act, 1)
                    act.wait_ge(s_act, i * 3 + 2)
                    act.activation(out, out, ACT.Ln, bias=1.0).then_inc(s_act, 1)

                act.wait_ge(s_zn, 1)
                chain(ZN[0:TS, :], a[0:TS, :], 0)
                act.wait_ge(s_zn, 2)
                act.activation(wn[:].rearrange("k s c -> k (s c)"), ZN[0:TS, :], ACT.Exp).then_inc(s_w, 1)

                def stay(s, slot):
                    for j in range(0, NPAGE, 2):
                        act.wait_ge(s_kt, s * NPAGE + j + 1)
                        at_least(act, s_qk, s * NPAGE + j - 3)
                        act.copy(kT[:, j % 4].rearrange("k p c -> k (p c)"), TB[0][:]).then_inc(s_kta, 1)
                    act.wait_ge(s_qk, s * NPAGE + NPAGE)
                    act.wait_ge(s_sp, s + 1)
                    chain(Z[slot][:], a[:], s + 1)

                def weights(s, slot):
                    at_least(act, s_pv, s - 1)
                    act.wait_ge(s_sum, s + 1)
                    act.activation(w[slot][:], Z[slot][:], ACT.Exp).then_inc(s_w, 1)

                def high(n, m):
                    i = PER * n + m
                    act.wait_ge(s_raw[m], n * 16 + 16)
                    at_least(act, s_mm, 3 * (i - PER) + 3)
                    act.copy(whi[m][:], raw[m][:]).then_inc(s_hi, 1)

                def store(n, m):
                    act.wait_ge(s_ev, 3 * (PER * n + m) + 3)
                    act.dma_start(g.projT[bass.ds(ROW_QG + (PER * n + m) * P, P), :], stg[m][:]).then_inc(s_st[m], 16)

                def body(n, more):
                    stay(2 * n, 0)
                    high(n, 2)
                    weights(2 * n, 0)
                    store(n, 0)
                    stay(2 * n + 1, 1)
                    if more:
                        high(n + 1, 0)
                    weights(2 * n + 1, 1)
                    if more:
                        high(n + 1, 1)
                    store(n, 1)
                    store(n, 2)

                high(0, 0)
                high(0, 1)
                pairs(body)(act)
                for m in range(PER):
                    act.wait_ge(s_st[m], 16 * (NSEQ // 2))

            @block.vector
            def _(dve):
                dve.wait_ge(s_vn, 1)
                dve.tensor_copy(vnew[:], O[0:TS, :]).then_inc(s_cd, 1)
                dve.wait_ge(s_in, 64)
                dve.wait_ge(s_c, 2)
                b = bsb[:].rearrange("o (j h q) -> o j h q", j=1, q=1).to_broadcast([1, NPAGE, HEADS, NEW])
                dve.tensor_copy(brow[:], b).then_inc(s_cd, 1)
                for h in range(2):
                    rows = slice(h * HD, (h + 1) * HD)
                    src = qnew[rows].rearrange("k p (s q) -> k p s q", s=NSEQ)
                    dve.tensor_scalar(qbd[rows, :, :, h, :], src, HD ** -0.5, None, ALU.mult).then_inc(s_cd, 1)
                dve.wait_ge(s_act, 3)
                dve.scalar_tensor_tensor(out=spn[0:TS].rearrange("k s c -> k (s c)"), in0=ZN[0:TS, :], scalar=0.0,
                                         in1=a[0:TS, :], op0=ALU.max, op1=ALU.add).then_inc(s_sp, 1)

                def step(s, slot):
                    for j in range(1, NPAGE, 2):
                        dve.wait_ge(s_kt, s * NPAGE + j + 1)
                        at_least(dve, s_qk, s * NPAGE + j - 3)
                        dve.tensor_copy(kT[:, j % 4].rearrange("k p c -> k (p c)"), TB[1][:]).then_inc(s_ktd, 1)
                    dve.wait_ge(s_act, (s + 1) * 3 + 3)
                    at_least(dve, s_sum, s)
                    dve.scalar_tensor_tensor(out=sp_[:].rearrange("k j c -> k (j c)"), in0=Z[slot][:], scalar=0.0,
                                             in1=a[:], op0=ALU.max, op1=ALU.add).then_inc(s_sp, 1)
                    spn_s = spn[:].rearrange("k s c -> k (s c)")[:, bass.ds(s * NCOL, NCOL)]
                    dve.tensor_copy(r[:, NPAGE - 1, :], spn_s).then_inc(s_r, 1)
                    dve.wait_ge(s_sp, s + 2)
                    for j in range(NPAGE - 2, -1, -1):
                        dve.wait_ge(s_r, s * 8 + NPAGE - 1 - j)
                        dve.tensor_tensor(r[:, j, :], r[:, j + 1, :], sp_[:, j + 1, :], ALU.add).then_inc(s_r, 1)

                def evacuate(n, chunks):
                    for m, c in chunks:
                        t0, tw = CHUNKS[c]
                        dve.wait_ge(s_mm, 3 * (PER * n + m) + c + 1)
                        at_least(dve, s_st[m], n * 16)
                        dve.tensor_copy(stg[m][:, t0:t0 + tw], DB[c][:, 0:tw]).then_inc(s_ev, 1)

                def body(n, more):
                    for slot in range(2):
                        step(2 * n + slot, slot)
                        evacuate(n, DENSE[slot][0])
                        evacuate(n, DENSE[slot][1])

                pairs(body)(dve)
                dve.wait_ge(s_pv, NSEQ)
                for h in range(2):
                    rows = slice(h * HD, (h + 1) * HD)
                    src = O[rows, :].rearrange("d (s p h q) -> d p s h q", s=NSEQ, p=4, h=2)[:, :, :, h, :]
                    dve.tensor_copy(o[rows], src).then_inc(s_o, 1)


def stage_prompt_attention(g):
    nc, io = g.nc, g.io
    HALF = slice(0, HD), slice(HD, P)
    TILES = 4
    steps = []
    for i in range(NT):
        c, w = i // TILES, (i + 1) * P
        if w > 512:
            steps.append((c, i, 512, w - 512))
        steps.append((c, i, 0, min(w, 512)))
    NS, NU = len(steps), 3 * TILES
    NZ = 4
    with ExitStack() as ctx:
        sb = lambda *a: g.sb(*a, ctx=ctx)
        qraw = [sb(f"pa_qraw{i}", [P, TP]) for i in range(2)]
        kraw = [sb(f"pa_kraw{i}", [P, TP]) for i in range(2)]
        qh = sb("pa_qh", [P, TP], F32R)
        qa = [sb(f"pa_qa{i}", [P, TP], F32R) for i in range(2)]
        qb = [sb(f"pa_qb{i}", [P, TP], F32R) for i in range(2)]
        ka = [sb(f"pa_ka{i}", [P, TP], F32R) for i in range(2)]
        kb = [sb(f"pa_kb{i}", [P, TP], F32R) for i in range(2)]
        vhl = [sb(f"pa_vhl{i}", [P, NT, P], F32R) for i in range(2)]
        bq = sb("pa_bias", [P, HEADS])
        bh = sb("pa_bias_hi", [P, HEADS], F32R)
        a = [sb(f"pa_a{i}", [P, 512]) for i in range(NZ)]
        s = [sb(f"pa_s{i}", [P, 512]) for i in range(NZ)]
        w = [sb(f"pa_w{c}", [P, TILES, 512 * (c + 1)]) for c in range(2)]
        wth = [sb(f"pa_wth{i}", [P, 512], F32R) for i in range(2)]
        wtl = [sb(f"pa_wtl{i}", [P, 512], F32R) for i in range(2)]
        ot = [sb(f"pa_ot{i}", [P, 512]) for i in range(2)]
        s_in = [g.sem(f"pa_qk{i}_loaded") for i in range(2)]
        s_b = g.sem("pa_bias_loaded")
        s_bd = g.sem("pa_bias_split")
        s_c = g.sem("pa_constants")
        s_pra = g.sem("pa_act_prepared")
        s_prp = g.sem("pa_pool_prepared")
        s_prd = g.sem("pa_dve_prepared")
        s_z = g.sem("pa_scored")
        s_a = g.sem("pa_act_chain")
        s_sp = g.sem("pa_softplus")
        s_sc = g.sem("pa_scanned")
        s_x = g.sem("pa_log_weight")
        s_w = g.sem("pa_weight")
        s_tp = g.sem("pa_transposed")
        s_hi = g.sem("pa_wT_hi")
        s_lo = g.sem("pa_wT_lo")
        s_pv = g.sem("pa_v_multiplied")
        s_oa = g.sem("pa_out_half")
        s_o = g.sem("pa_out_summed")
        s_oh = g.sem("pa_out_hi")
        Z, TB, O = g.bank[0:4], g.bank[4:6], g.bank[6:8]

        NG = 4
        group_steps = [[[k] for k in range(TILES)], [[TILES + 2 * k, TILES + 2 * k + 1] for k in range(NG)]]
        group_blocks = [[[(1, 0), (1, 1)], [(1, 2)], [(1, 3)], [(1, 4)]],
                        [[(1, 5), (1, 6)], [(1, 7), (0, 0)], [(0, 1), (0, 2)], [(0, 3)]]]
        last_step = [group_steps[c][-1][-1] for c in range(2)]

        def heads(eng, group, prep, finish):
            def before(n, slot):
                return (n, 0) if slot else (n - 1, 1)

            def head(n, slot, first, more):
                for c in range(2):
                    for k in range(NG):
                        group((n, slot), c, k, blocks(n, slot, c, k, first), True)
                        if not first and k == 1 + c:
                            finish(*before(n, slot), c)
                        if more and c:
                            prep(2 * n + slot + 1, 1 - slot, k)

            def blocks(n, slot, c, k, first):
                return [(*((n, slot) if half == 0 else before(n, slot)), half, j) for half, j in group_blocks[c][k]
                        if half == 0 or not first]

            for k in range(NG):
                prep(0, 0, k)
            head(0, 0, True, True)
            head(0, 1, False, True)
            with eng.Fori(1, HEADS // 2 - 1) as n:
                head(n, 0, False, True)
                head(n, 1, False, True)
            n = HEADS // 2 - 1
            head(n, 0, False, True)
            head(n, 1, False, False)
            for c, k in ((0, 0), (0, 1), (0, 2), (0, 3), (1, 0), (1, 1)):
                group((n + 1, 0), c, k, [b for b in blocks(n + 1, 0, c, k, False) if b[2] == 1], False)
                if (c, k) == (0, 1):
                    finish(n, 1, 0)
            finish(n, 1, 1)

        def nothing(*_):
            pass

        with nc.Block() as block:
            @block.sync
            def _(sp):
                sp.dma_start(bq[:], io["b_sb"].to_broadcast([P, HEADS])).then_inc(s_b, 16)

                def load(h, slot, k):
                    if k > 0:
                        return
                    at_least(sp, s_prp, 3 * (h - 2) + 3)
                    at_least(sp, s_pra, 4 * (h - 2) + 4)
                    for raw, row in ((qraw, ROW_Q), (kraw, ROW_K)):
                        for half in HALF:
                            sp.dma_start(raw[slot][half, :], g.projT[bass.ds(h * HD + row, HD), 0:TP]).then_inc(s_in[slot], 16)

                heads(sp, nothing, load, nothing)

            @block.gpsimd
            def _(pool):
                for i in range(2):
                    pool.memset(kb[i][HALF[1], :].bitcast(F32), 1.0 / 32).then_inc(s_c, 1)

                def prep(h, slot, k):
                    if k > 0:
                        return
                    lo, hi = HALF
                    pool.wait_ge(s_pra, 4 * h + 2)
                    pool.tensor_tensor(kb[slot][lo, :], kraw[slot][lo, :], ka[slot][lo, :], ALU.subtract).then_inc(s_prp, 1)
                    pool.tensor_scalar(qraw[slot][hi, :], qraw[slot][hi, :], HD ** -0.5, 0.0, ALU.mult, ALU.add).then_inc(s_prp, 1)
                    pool.wait_ge(s_prp, 3 * h + 2)
                    pool.tensor_tensor(qa[slot][hi, :], qraw[slot][hi, :], qh[hi, :], ALU.subtract).then_inc(s_prp, 1)

                heads(pool, nothing, prep, nothing)

            @block.tensor
            def _(pe):
                pe.wait_ge(s_c, 2)

                def score(n, slot, t):
                    h = 2 * n + slot
                    _, i, k0, kw = steps[t]
                    z = Z[t % NZ][:, 0:kw]
                    q = slice(i * P, (i + 1) * P)
                    if t == 0:
                        pe.wait_ge(s_pra, 4 * h + 4)
                        pe.wait_ge(s_prp, 3 * h + 3)
                        pe.wait_ge(s_prd, 3 * h + 3)
                    at_least(pe, s_x, h * NS + t - NZ + 1)
                    diagonal = k0 + kw == (i + 1) * P
                    pe.matmul(z, qa[slot][:, q], ka[slot][:, k0:k0 + kw], start=True, stop=False)
                    last = pe.matmul(z, qb[slot][:, q], kb[slot][:, k0:k0 + kw], start=False, stop=not diagonal)
                    if diagonal:
                        last = pe.matmul(z[:, kw - P:kw], g.ident16[:], g.causal16[:], start=False, stop=True)
                    last.then_inc(s_z, 1)

                def transpose(n, slot, c, j):
                    h, u = 2 * n + slot, c * TILES + j
                    if j == 0:
                        pe.wait_ge(s_w, h * NS + last_step[c] + 1)
                    at_least(pe, s_lo, h * NU + u - 1)
                    for i in range(max(0, j - c * TILES), TILES):
                        last = pe.transpose(TB[u % 2][:, i * P:(i + 1) * P], w[c][:, i, j * P:(j + 1) * P], g.ident[:])
                    last.then_inc(s_tp, 1)

                def multiply(n, slot, c, j):
                    h, u = 2 * n + slot, c * TILES + j
                    cols = slice(max(0, j - c * TILES) * P, 512)
                    if j == 0:
                        at_least(pe, s_o, 2 * h + c - 1)
                    pe.wait_ge(s_lo, h * NU + u + 1)
                    pe.matmul(O[c][:, cols], vhl[slot][:, j, :], wth[u % 2][:, cols], start=(j == 0), stop=False)
                    pe.matmul(O[c][:, cols], vhl[slot][:, j, :], wtl[u % 2][:, cols], start=False,
                              stop=(j == TILES * (c + 1) - 1)).then_inc(s_pv, 1)

                def group(head, c, k, blocks, scores):
                    if scores:
                        for t in group_steps[c][k]:
                            score(*head, t)
                    for n, slot, half, j in blocks:
                        transpose(n, slot, half, j)
                        if j > 0:
                            multiply(n, slot, half, j - 1)
                            if half == 1 and j == 2 * TILES - 1 and not scores:
                                multiply(n, slot, half, j)
                        elif half == 1:
                            multiply(n, slot, 0, TILES - 1)
                        elif slot:
                            multiply(n, 0, 1, 2 * TILES - 1)
                        elif not isinstance(n, int) or n > 0:
                            multiply(n - 1, 1, 1, 2 * TILES - 1)

                heads(pe, group, nothing, nothing)

            @block.scalar
            def _(act):
                def prep(h, slot, k):
                    lo, hi = HALF
                    if k == 0:
                        act.wait_ge(s_in[slot], (h - slot + 2) * 32)
                        at_least(act, s_z, (h - 2) * NS + NS)
                        at_least(act, s_prp, 3 * h)
                        act.activation(qh[hi, :], qraw[slot][hi, :], ACT.Copy, scale=HD ** -0.5).then_inc(s_pra, 1)
                        act.copy(ka[slot][:], kraw[slot][:]).then_inc(s_pra, 1)
                    if k == 1:
                        act.activation(qa[slot][lo, :], qraw[slot][lo, :], ACT.Copy, scale=HD ** -0.5).then_inc(s_pra, 1)
                        act.activation(qb[slot][lo, :], qraw[slot][lo, :], ACT.Copy, scale=HD ** -0.5).then_inc(s_pra, 1)

                def weights(n, slot, c, k):
                    h = 2 * n + slot
                    for t in group_steps[c][k]:
                        _, i, k0, kw = steps[t]
                        act.wait_ge(s_x, h * NS + t + 1)
                        at_least(act, s_tp, (h - 1) * NU + c * TILES + i + 1)
                        act.activation(w[c][:, i % TILES, k0:k0 + kw], a[t % NZ][:, 0:kw], ACT.Exp).then_inc(s_w, 1)

                def high(n, slot, c, j):
                    h, u = 2 * n + slot, c * TILES + j
                    cols = slice(max(0, j - c * TILES) * P, 512)
                    act.wait_ge(s_tp, h * NU + u + 1)
                    at_least(act, s_pv, h * NU + u - 1)
                    act.copy(wth[u % 2][:, cols], TB[u % 2][:, cols]).then_inc(s_hi, 1)

                def group(head, c, k, blocks, scores):
                    n, slot = head
                    h = 2 * n + slot
                    ts = group_steps[c][k]
                    m, base = len(ts), (h * NS + ts[0]) * 3
                    if c == 0 and k == 0 and blocks:
                        weights(*blocks[0][:2], 1, NG - 1)
                    if scores:
                        for t in ts:
                            at_least(act, s_w, h * NS + t - NZ + 1)
                            act.wait_ge(s_z, h * NS + t + 1)
                            act.activation(a[t % NZ][:, 0:steps[t][3]], Z[t % NZ][:, 0:steps[t][3]], ACT.Abs).then_inc(s_a, 1)
                    if blocks:
                        high(*blocks[0])
                    if scores:
                        for x, t in enumerate(ts):
                            out = a[t % NZ][:, 0:steps[t][3]]
                            act.wait_ge(s_a, base + x + 1)
                            act.activation(out, out, ACT.Exp, scale=-1.0).then_inc(s_a, 1)
                    if len(blocks) > 1:
                        high(*blocks[1])
                    if scores:
                        for x, t in enumerate(ts):
                            out = a[t % NZ][:, 0:steps[t][3]]
                            act.wait_ge(s_a, base + m + x + 1)
                            act.activation(out, out, ACT.Ln, bias=1.0).then_inc(s_a, 1)
                        if k > 0:
                            weights(n, slot, c, k - 1)
                        elif c == 1:
                            weights(n, slot, 0, NG - 1)

                def finish(n, slot, c):
                    h = 2 * n + slot
                    act.wait_ge(s_pv, h * NU + c * TILES + TILES * (c + 1))
                    at_least(act, s_oh, 2 * h + c - 1)
                    act.copy(ot[c][HALF[slot], :], O[c][HALF[1 - slot], :]).then_inc(s_oa, 1)

                heads(act, group, prep, finish)

            @block.vector
            def _(dve):
                dve.wait_ge(s_b, 16)
                dve.tensor_copy(bh[:], bq[:]).then_inc(s_bd, 1)
                dve.wait_ge(s_bd, 1)
                lo_rows = slice(96, P)
                dve.tensor_tensor(bq[lo_rows], bq[lo_rows], bh[lo_rows].bitcast(F32), ALU.subtract).then_inc(s_bd, 1)
                dve.wait_ge(s_bd, 2)

                def prep(h, slot, k):
                    v = g.vnat[:, 0:NT, bass.ds(h * HD, HD)]
                    if k == 0:
                        at_least(dve, s_z, (h - 2) * NS + NS)
                        b = bq[HALF[1], bass.ds(h, 1)].to_broadcast([HD, TP])
                        dve.tensor_scalar(qb[slot][HALF[1], :], b, 1.0, None, ALU.mult).then_inc(s_prd, 1)
                    elif k == 2:
                        at_least(dve, s_pv, (h - 2) * NU + NU)
                        dve.tensor_scalar(vhl[slot][:, :, 0:HD], v, 1.0, None, ALU.mult).then_inc(s_prd, 1)
                    elif k == 3:
                        dve.wait_ge(s_prd, 3 * h + 2)
                        dve.tensor_tensor(vhl[slot][:, :, HD:P], v, vhl[slot][:, :, 0:HD], ALU.subtract).then_inc(s_prd, 1)

                def low(n, slot, c, j):
                    h, u = 2 * n + slot, c * TILES + j
                    cols = slice(max(0, j - c * TILES) * P, 512)
                    dve.wait_ge(s_hi, h * NU + u + 1)
                    dve.tensor_tensor(wtl[u % 2][:, cols], TB[u % 2][:, cols], wth[u % 2][:, cols], ALU.subtract).then_inc(s_lo, 1)

                def group(head, c, k, blocks, scores):
                    n, slot = head
                    h = 2 * n + slot
                    ts = group_steps[c][k] if scores else []
                    part = lambda b, t: b[t % NZ][:, 0:steps[t][3]]
                    if blocks:
                        low(*blocks[0])
                    for x, t in enumerate(ts):
                        dve.wait_ge(s_a, (h * NS + ts[0]) * 3 + 2 * len(ts) + x + 1)
                        dve.scalar_tensor_tensor(out=part(a, t), in0=part(Z, t), scalar=0.0, in1=part(a, t), op0=ALU.max,
                                                 op1=ALU.add).then_inc(s_sp, 1)
                    if len(blocks) > 1:
                        low(*blocks[1])
                    for t in ts:
                        _, i, k0, kw = steps[t]
                        dve.wait_ge(s_sp, h * NS + t + 1)
                        later = 0.0
                        if i >= TILES and k0 == 0:
                            dve.wait_ge(s_sc, h * NS + t)
                            later = s[(t - 1) % NZ][:, 0:1]
                        dve.tensor_tensor_scan(part(s, t)[:, ::-1], part(a, t)[:, ::-1], part(a, t)[:, ::-1], later, ALU.add,
                                               ALU.max).then_inc(s_sc, 1)
                    for t in ts:
                        dve.wait_ge(s_sc, h * NS + t + 1)
                        dve.tensor_tensor(part(a, t), part(Z, t), part(s, t), ALU.subtract).then_inc(s_x, 1)

                def finish(n, slot, c):
                    rows, G = HALF[slot], 2 * (2 * n + slot) + c
                    dve.wait_ge(s_oa, G + 1)
                    dve.tensor_tensor(ot[c][rows, :], ot[c][rows, :], O[c][rows, :], ALU.add).then_inc(s_o, 1)
                    hi, lo = (m[rows, bass.ds(n, 1), c * 512:(c + 1) * 512].rearrange("d o t -> d (o t)") for m in (g.op_hi, g.op_lo))
                    dve.wait_ge(s_o, G + 1)
                    dve.tensor_scalar(hi, ot[c][rows, :], 1.0, None, ALU.mult).then_inc(s_oh, 1)
                    dve.wait_ge(s_oh, G + 1)
                    dve.tensor_tensor(lo, ot[c][rows, :], hi, ALU.subtract)

                heads(dve, group, prep, finish)


def stage_gla(g):
    nc, io = g.nc, g.io
    NSUB = P // SUB
    MID = SUB // 2 - 1
    QS = GK ** -0.5
    HALF = slice(0, GK), slice(GK, P)
    with ExitStack() as ctx:
        sb = lambda *a: g.sb(*a, ctx=ctx)
        q = sb("gl_q", [P, 2, T])
        k = sb("gl_k", [P, 2, T])
        rg = [sb(f"gl_r{i}", [P, GH, P]) for i in range(3)]
        sr = [sb(f"gl_silu{i}", [P, GH, P]) for i in range(2)]
        v = [sb(f"gl_v{i}", [P, GH * GV]) for i in range(3)]
        al = sb("gl_alow", [RANK, T])
        wg = sb("gl_wgate", [RANK, GH * GK])
        negb = sb("gl_negb", [P, 2])
        bc = sb("gl_bc", [P, 2, T])
        nx = sb("gl_nx", [P, 2, T])
        kend = sb("gl_kend", [P, 2, T])
        reset = kend[:, 0, :]
        eb = [sb(f"gl_eb{i}", [P, 2, P]) for i in range(2)]
        qdec = [sb(f"gl_qdec{i}", [P, 2, P]) for i in range(2)]
        qi = [sb(f"gl_qi{i}", [P, 2, 2, P]) for i in range(2)]
        dec = sb("gl_dec", [P, 2, NT + NSEQ])
        ki = [sb(f"gl_ki{i}", [P, 2, NSUB, P]) for i in range(2)]
        kn = [sb(f"gl_kn{i}", [P, 2 * P]) for i in range(2)]
        pt = [sb(f"gl_pt{i}", [P, GH, P]) for i in range(2)]
        st = sb("gl_state", [P, GH, GV])
        on = [sb(f"gl_on{i}", [P, GH, GV]) for i in range(2)]
        fin = [sb(f"gl_fin{i}", [P, GH, P]) for i in range(2)]
        sq = sb("gl_sq", [P, GH, GV])
        rs = sb("gl_rstd", [P, NT + 1, GH])
        tri = sb("gl_tri", [P, P])
        tri8 = sb("gl_tri8", [TS, TS])
        rowm = sb("gl_rowmask", [TS, NSEQ])
        colm = sb("gl_colmask", [P, NSEQ, TS])
        kinv = sb("gl_kinv", [P, 2, TS])
        qs = sb("gl_qs", [P, 2, 2, TS])
        qm = sb("gl_qm", [P, 2, NSEQ, TS])
        kem = [sb(f"gl_kem{i}", [TS, 2 * P]) for i in range(2)]
        s0 = sb("gl_s0", [P, NSEQ, GH, GV])
        wa = [sb(f"ada2_w{i}", [P, 2, 512]) for i in range(2)]
        arow = sb("ada2_rows", [NMOD, 512])
        NADA = 4 * D // 512
        s_wa = [g.sem(f"ada2_w{i}_loaded") for i in range(2)]
        s_am = g.sem("ada2_quarter_summed")
        s_ar = g.sem("ada2_rows_copied")
        s_at = g.sem("ada2_rows_transposed")
        s_ae = g.sem("ada2_mod_done")
        s_gin = g.sem("gl_gate_inputs_loaded")
        s_k = g.sem("gl_k_loaded")
        s_q = g.sem("gl_q_loaded")
        s_r = [g.sem(f"gl_r{i}_loaded") for i in range(3)]
        s_s0 = g.sem("gl_s0_loaded")
        s_c = g.sem("gl_constants")
        s_z = g.sem("gl_zeroed")
        s_nb = g.sem("gl_negb_done")
        s_gate = g.sem("gl_gate_product")
        s_a = g.sem("gl_act_pre")
        s_d = g.sem("gl_dve_pre")
        s_E = g.sem("gl_ki_exp")
        s_D = g.sem("gl_ki_diff")
        s_ki = g.sem("gl_ki_done")
        s_kt = g.sem("gl_kend_transposed")
        s_kn = g.sem("gl_kn_copied")
        s_sc = g.sem("gl_scored")
        s_cl = g.sem("gl_clamped")
        s_pt = g.sem("gl_masked")
        s_oo = g.sem("gl_o")
        s_ds = g.sem("gl_ds")
        s_st = g.sem("gl_state_updated")
        s_sq = g.sem("gl_squares")
        s_rl = g.sem("gl_rstd_ln")
        s_rs = g.sem("gl_rstd_done")
        s_on = g.sem("gl_on_done")
        s_ot = g.sem("gl_on_transposed")
        s_fin = g.sem("gl_fin_done")
        s_fh = g.sem("gl_fin_hi")
        s_fl = g.sem("gl_fin_lo")
        s_out = g.sem("gl_stored")
        s_v = [g.sem(f"gl_v{i}_loaded") for i in range(3)]
        s_eb = g.sem("gl_exp_bc")
        s_qd = g.sem("gl_qdec_done")
        s_se = g.sem("gl_silu_act")
        s_sd = g.sem("gl_silu_exponent")
        s_sm = g.sem("gl_silu_done")
        s_km = g.sem("gl_kem_done")
        s_x = g.sem("gl_sample_dve")
        s_xp = g.sem("gl_sample_pe")
        KT, SC, OB, DS, OT, ADA = g.bank[0], g.bank[1:3], g.bank[3:5], g.bank[5], g.bank[6], g.bank[7]
        N9 = NT + 1

        def tile(i):
            return slice(i * P, i * P + (P if i < NT else TS))

        with nc.Block() as block:
            @block.sync
            def _(sp):
                sp.dma_start(al[:], g.projT[ROW_A:IN_W, :]).then_inc(s_gin, 16)
                sp.dma_start(wg[:], io["w_gla_gate"][0]).then_inc(s_gin, 16)
                sp.dma_start(k[:], g.projT[ROW_KG:ROW_VG, :].rearrange("(m p) t -> p m t", p=P)).then_inc(s_k, 16)
                sp.dma_start(q[:], g.projT[ROW_QG:ROW_KG, :].rearrange("(m p) t -> p m t", p=P)).then_inc(s_q, 16)
                for i in range(2):
                    sp.dma_start(v[i][:], g.vgnat[tile(i)]).then_inc(s_v[i], 16)

                def load_r(i):
                    if i >= 3:
                        sp.wait_ge(s_fin, i - 2)
                    w = P if i < NT else TS
                    sp.dma_start(rg[i % 3][:, :, 0:w], g.projT[ROW_RG:ROW_A, tile(i)].rearrange("(m p) t -> p m t", p=P)).then_inc(s_r[i % 3], 16)

                def weights(i):
                    if i >= 2:
                        sp.wait_ge(s_am, i - 1)
                    chunk, m = divmod(i, 4)
                    part = io["w_ada"][0][m * 2 * P:(m + 1) * 2 * P, 2 * D + chunk * 512:2 * D + (chunk + 1) * 512]
                    sp.dma_start(wa[i % 2][:], part.rearrange("(k p) c -> p k c", p=P)).then_inc(s_wa[i % 2], 16)

                for i in range(2):
                    load_r(i)
                    weights(i)
                sp.wait_ge(s_z, 4)
                s0d = io["state_gla"][0].rearrange("s (m h) k v -> h m k s v", h=2)
                for h in range(2):
                    for m in range(2):
                        sp.dma_start(s0[HALF[h], :, 2 * m + h, :], s0d[h, m]).then_inc(s_s0, 16)
                for i in range(2, N9):
                    if i >= 3:
                        sp.wait_ge(s_ds, i - 2)
                        sp.wait_ge(s_oo, i - 2)
                    sp.dma_start(v[i % 3][0:P if i < NT else TS, :], g.vgnat[tile(i)]).then_inc(s_v[i % 3], 16)
                    for t in range(4):
                        weights(4 * (i - 2) + 2 + t)
                    load_r(i)
                for t in range(4 * NADA - 2, 4 * NADA):
                    weights(t)
                sp.wait_ge(s_st, 4 * NT)
                outp = io["state_prompt"][0, 0].rearrange("(m h) k v -> h m k v", h=2)
                for h in range(2):
                    for m in range(2):
                        sp.dma_start(outp[h, m], st[HALF[h], 2 * m + h, :]).then_inc(s_out, 16)
                sp.wait_ge(s_x, 1 + 4 * NSEQ)
                outs = io["state_sample"][0].rearrange("s (m h) k v -> h m k s v", h=2)
                for h in range(2):
                    for m in range(2):
                        sp.dma_start(outs[h, m], s0[HALF[h], :, 2 * m + h, :]).then_inc(s_out, 16)
                sp.wait_ge(s_out, 8 * 16)

            @block.gpsimd
            def _(pool):
                pool.memset(st[:], 0.0).then_inc(s_z, 1)
                pool.memset(qi[0][:], 0.0).then_inc(s_z, 1)
                pool.memset(qi[1][:], 0.0).then_inc(s_z, 1)
                pool.memset(s0[:], 0.0).then_inc(s_z, 1)
                pool.memset(qs[:], 0.0).then_inc(s_z, 1)
                pool.memset(reset, 1.0).then_inc(s_c, 1)
                pool.memset(tri[:], 1.0).then_inc(s_c, 1)
                pool.memset(tri8[:], 1.0).then_inc(s_c, 1)
                pool.memset(rowm[:], 1.0).then_inc(s_c, 1)
                pool.memset(colm[:], 1.0).then_inc(s_c, 1)
                pool.wait_ge(s_c, 5)
                pool.memset(reset[:, 0:TP:P], 0.0).then_inc(s_c, 1)
                pool.memset(reset[:, TP:T:NEW], 0.0).then_inc(s_c, 1)

                def keep(out, pattern, base, mult):
                    pool.affine_select(out=out, in_=out, compare_op=ALU.is_ge, fill=0.0, base=base,
                                       pattern=pattern, channel_multiplier=mult).then_inc(s_c, 1)

                keep(tri[:], [[1, P]], 0, -1)
                t8 = tri8[:].rearrange("k (s q) -> k s q", s=NSEQ)
                keep(t8, [[NEW, NSEQ], [1, NEW]], 0, -1)
                keep(rowm[:], [[-NEW, NSEQ]], 0, 1)
                keep(colm[:], [[-NEW, NSEQ], [1, TS]], 0, 0)
                pool.wait_ge(s_c, 11)
                keep(t8, [[-NEW, NSEQ], [0, NEW]], 0, 1)
                keep(rowm[:], [[NEW, NSEQ]], NEW - 1, -1)
                keep(colm[:], [[NEW, NSEQ], [-1, TS]], NEW - 1, 0)
                for i in range(N9):
                    w = P if i < NT else TS
                    pool.wait_ge(s_fh, i + 1)
                    pool.tensor_tensor(g.op_lo[:, GH:2 * GH, tile(i)], fin[i % 2][:, :, 0:w],
                                       g.op_hi[:, GH:2 * GH, tile(i)], ALU.subtract).then_inc(s_fl, 1)

            @block.scalar
            def _(act):
                act.wait_ge(s_nb, 1)
                n = 0
                for m in range(2):
                    for c, (t0, tw) in enumerate(CHUNKS):
                        act.wait_ge(s_gate, 3 * m + c + 1)
                        act.activation(nx[:, m, t0:t0 + tw], g.bank[3 * m + c][:, 0:tw], ACT.Identity, scale=-1.0,
                                       bias=negb[:, m:m + 1]).then_inc(s_a, 1)
                act.wait_ge(s_a, 6)
                act.activation(bc[:], nx[:], ACT.Abs).then_inc(s_a, 1)
                act.wait_ge(s_a, 7)
                act.activation(bc[:], bc[:], ACT.Exp, scale=-1.0).then_inc(s_a, 1)
                act.wait_ge(s_a, 8)
                act.activation(bc[:], bc[:], ACT.Ln, bias=1.0).then_inc(s_a, 1)
                act.wait_ge(s_d, 3)
                act.activation(dec[:, :, 0:NT], bc[:, :, P - 1:TP:P], ACT.Exp, scale=-GATE)
                act.activation(dec[:, :, NT:], bc[:, :, TP + NEW - 1:T:NEW], ACT.Exp, scale=-GATE).then_inc(s_a, 1)
                act.wait_ge(s_d, 5)
                act.activation(kend[:], kend[:], ACT.Exp, scale=GATE).then_inc(s_a, 1)
                act.wait_ge(s_d, 7)
                act.activation(nx[:, :, 0:TP], nx[:, :, 0:TP], ACT.Exp, scale=-GATE).then_inc(s_a, 1)
                act.activation(kinv[:], bc[:, :, TP:T], ACT.Exp, scale=GATE).then_inc(s_a, 1)
                act.activation(nx[:, :, TP:T], bc[:, :, TP:T], ACT.Exp, scale=-GATE).then_inc(s_a, 1)

                def key_exps(i):
                    if i >= 2:
                        act.wait_ge(s_qd, 3 * (i - 1))
                    act.activation(eb[i % 2][:], bc[:, :, tile(i)], ACT.Exp, scale=-GATE).then_inc(s_eb, 1)
                    for m in range(2):
                        act.wait_ge(s_D, 2 * i + m + 1)
                        act.activation(ki[i % 2][:, m], ki[i % 2][:, m], ACT.Exp, scale=GATE).then_inc(s_E, 1)

                def copy_kn(i):
                    rows = P if i < NT else TS
                    act.wait_ge(s_kt, i + 1)
                    if 2 <= i < NT:
                        act.wait_ge(s_ds, i - 1)
                    act.copy(kn[i % 2][0:rows], KT[0:rows, 0:2 * P]).then_inc(s_kn, 1)

                def norms(i):
                    rows = P if i < NT else TS
                    act.wait_ge(s_oo, i + 1)
                    for h in range(GH):
                        act.activation(sq[0:rows, h], OB[i % 2][0:rows, h * GV:(h + 1) * GV], ACT.Square,
                                       accum_out=rs[0:rows, i, h:h + 1]).then_inc(s_sq, 1)
                    act.wait_ge(s_sq, GH * (i + 1))
                    act.activation(rs[0:rows, i], rs[0:rows, i], ACT.Ln, scale=1.0 / GV, bias=g.eps[0:rows, :]).then_inc(s_rl, 1)
                    act.wait_ge(s_rl, i + 1)
                    act.activation(rs[0:rows, i], rs[0:rows, i], ACT.Exp, scale=-0.5).then_inc(s_rs, 1)

                def gate_ln(i):
                    x = sr[i % 2][:, :, 0:P if i < NT else TS]
                    act.wait_ge(s_r[i % 3], 16 * (i // 3 + 1))
                    if i >= 2:
                        act.wait_ge(s_fin, i - 1)
                    act.activation(x, rg[i % 3][:, :, 0:x.shape[2]], ACT.Abs).then_inc(s_se, 1)
                    act.wait_ge(s_se, 4 * i + 1)
                    act.activation(x, x, ACT.Exp, scale=-1.0).then_inc(s_se, 1)
                    act.wait_ge(s_se, 4 * i + 2)
                    act.activation(x, x, ACT.Ln, bias=1.0).then_inc(s_se, 1)

                def gate_exp(i):
                    x = sr[i % 2][:, :, 0:P if i < NT else TS]
                    act.wait_ge(s_sd, i + 1)
                    act.activation(x, x, ACT.Exp).then_inc(s_se, 1)

                def fin_hi(i):
                    w = P if i < NT else TS
                    act.wait_ge(s_fin, i + 1)
                    act.copy(g.op_hi[:, GH:2 * GH, tile(i)], fin[i % 2][:, :, 0:w]).then_inc(s_fh, 1)

                key_exps(0)
                copy_kn(0)
                for i in range(N9):
                    if i + 1 < NT:
                        key_exps(i + 1)
                    if i + 1 < N9:
                        copy_kn(i + 1)
                    gate_ln(i)
                    norms(i)
                    gate_exp(i)
                    if i > 0:
                        fin_hi(i - 1)
                fin_hi(N9 - 1)

            @block.vector
            def _(dve):
                nd = [0]

                def pre(ins):
                    nd[0] += 1
                    ins.then_inc(s_d, 1)

                dve.tensor_scalar(negb[:], g.vecT[:, 16:18], -1.0, None, ALU.mult).then_inc(s_nb, 1)
                dve.wait_ge(s_a, 9)
                dve.wait_ge(s_c, 7)
                pre(dve.scalar_tensor_tensor(out=nx[:].rearrange("k m t -> k (m t)"), in0=nx[:].rearrange("k m t -> k (m t)"),
                                             scalar=0.0, in1=bc[:].rearrange("k m t -> k (m t)"), op0=ALU.max, op1=ALU.add))
                dve.wait_ge(s_d, 1)
                for m in range(2):
                    pre(dve.tensor_tensor_scan(bc[:, m, :], reset, nx[:, m, :], 0.0, ALU.mult, ALU.add))
                dve.wait_ge(s_d, 3)
                for n, w, t0 in ((NT, P, 0), (NSEQ, NEW, TP)):
                    b = bc[:, :, t0:t0 + n * w].rearrange("k m (n w) -> k m n w", w=w)
                    pre(dve.tensor_tensor(kend[:, :, t0:t0 + n * w].rearrange("k m (n w) -> k m n w", w=w), b,
                                          b[:, :, :, w - 1:w].to_broadcast([P, 2, n, w]), ALU.subtract))
                dve.wait_ge(s_q, 16)
                dve.wait_ge(s_k, 16)
                for m in range(2):
                    b = bc[:, m, 0:TP].rearrange("k (n w) -> k n w", w=SUB)
                    pre(dve.tensor_tensor(nx[:, m, 0:TP].rearrange("k (n w) -> k n w", w=SUB), b,
                                          b[:, :, MID:MID + 1].to_broadcast([P, TP // SUB, SUB]), ALU.subtract))
                dve.wait_ge(s_a, 11)
                pre(dve.tensor_tensor(kend[:], kend[:], k[:], ALU.mult))
                dve.wait_ge(s_a, 14)
                dve.wait_ge(s_z, 5)
                pre(dve.scalar_tensor_tensor(out=kinv[:], in0=kinv[:], scalar=BIG, in1=k[:, :, TP:T], op0=ALU.min, op1=ALU.mult))
                for h in range(2):
                    pre(dve.scalar_tensor_tensor(out=qs[HALF[h], :, h, :], in0=nx[HALF[h], :, TP:T], scalar=QS,
                                                 in1=q[HALF[h], :, TP:T], op0=ALU.mult, op1=ALU.mult))
                dve.wait_ge(s_d, 11)
                dve.scalar_tensor_tensor(out=nx[:, :, TP:T], in0=nx[:, :, TP:T], scalar=QS, in1=q[:, :, TP:T],
                                         op0=ALU.mult, op1=ALU.mult).then_inc(s_x, 1)
                dve.wait_ge(s_x, 1)
                dve.wait_ge(s_c, 14)
                for m in range(2):
                    pre(dve.tensor_tensor(qm[:, m], nx[:, m, TP:T].rearrange("k (o t) -> k o t", o=1).to_broadcast([P, NSEQ, TS]),
                                          colm[:], ALU.mult))

                def keys(i):
                    b = bc[:, :, tile(i)]
                    mid = b.rearrange("k m (n w) -> k m n w", w=SUB)[:, :, :, MID:MID + 1]
                    if i >= 2:
                        dve.wait_ge(s_sc, i - 1)
                    for m in range(2):
                        dve.tensor_tensor(ki[i % 2][:, m], b[:, m:m + 1, :].to_broadcast([P, NSUB, P]),
                                          mid[:, m].to_broadcast([P, NSUB, P]), ALU.subtract).then_inc(s_D, 1)
                    for m in range(2):
                        dve.wait_ge(s_E, 2 * i + m + 1)
                        dve.scalar_tensor_tensor(out=ki[i % 2][:, m], in0=ki[i % 2][:, m], scalar=BIG,
                                                 in1=k[:, m:m + 1, tile(i)].to_broadcast([P, NSUB, P]),
                                                 op0=ALU.min, op1=ALU.mult).then_inc(s_ki, 1)
                    if i >= 2:
                        dve.wait_ge(s_oo, i - 1)
                    dve.wait_ge(s_eb, i + 1)
                    dve.scalar_tensor_tensor(out=qdec[i % 2][:], in0=eb[i % 2][:], scalar=QS, in1=q[:, :, tile(i)],
                                             op0=ALU.mult, op1=ALU.mult).then_inc(s_qd, 1)
                    for h in range(2):
                        dve.scalar_tensor_tensor(out=qi[i % 2][HALF[h], :, h, :], in0=nx[HALF[h], :, tile(i)], scalar=QS,
                                                 in1=q[HALF[h], :, tile(i)], op0=ALU.mult, op1=ALU.mult).then_inc(s_qd, 1)

                def scores(i):
                    rows = P if i < NT else TS
                    s = SC[i % 2][0:rows].rearrange("k (h t) -> k h t", h=GH)[:, :, 0:rows]
                    p = pt[i % 2][0:rows, :, 0:rows]
                    dve.wait_ge(s_sc, i + 1)
                    if i >= 2:
                        dve.wait_ge(s_oo, i - 1)
                    dve.tensor_scalar(p, s, BIG, -BIG, ALU.min, ALU.max).then_inc(s_cl, 1)
                    dve.wait_ge(s_cl, i + 1)
                    mask = (tri if i < NT else tri8)[:].rearrange("k (o t) -> k o t", o=1).to_broadcast([rows, GH, rows])
                    dve.tensor_tensor(p, p, mask, ALU.mult).then_inc(s_pt, 1)

                def normed(i):
                    rows = P if i < NT else TS
                    dve.wait_ge(s_rs, i + 1)
                    if i >= 2:
                        dve.wait_ge(s_ot, i - 1)
                    dve.tensor_tensor(on[i % 2][0:rows], OB[i % 2][0:rows].rearrange("t (h v) -> t h v", h=GH),
                                      rs[0:rows, i].rearrange("t (h o) -> t h o", o=1).to_broadcast([rows, GH, GV]),
                                      ALU.mult).then_inc(s_on, 1)

                def gate_exponent(i):
                    w = P if i < NT else TS
                    x = sr[i % 2][:, :, 0:w]
                    dve.wait_ge(s_se, 4 * i + 3)
                    dve.scalar_tensor_tensor(out=x, in0=rg[i % 3][:, :, 0:w], scalar=0.0, in1=x, op0=ALU.min,
                                             op1=ALU.subtract).then_inc(s_sd, 1)

                def gated(i):
                    w = P if i < NT else TS
                    dve.wait_ge(s_ot, i + 1)
                    if i >= 2:
                        dve.wait_ge(s_fl, i - 1)
                    x = sr[i % 2][:, :, 0:w]
                    dve.wait_ge(s_se, 4 * i + 4)
                    dve.tensor_tensor(x, x, rg[i % 3][:, :, 0:w], ALU.mult).then_inc(s_sm, 1)
                    dve.wait_ge(s_sm, i + 1)
                    dve.scalar_tensor_tensor(out=fin[i % 2][:, :, 0:w], in0=OT[:].rearrange("v (h t) -> v h t", h=GH)[:, :, 0:w],
                                             scalar=g.vecT[:, 18:19], in1=x, op0=ALU.mult,
                                             op1=ALU.mult).then_inc(s_fin, 1)

                def state(i):
                    dve.wait_ge(s_ds, i + 1)
                    for h in range(GH):
                        r = HALF[h % 2]
                        dve.scalar_tensor_tensor(out=st[r, h, :], in0=st[r, h, :], scalar=dec[r, h // 2, i:i + 1],
                                                 in1=DS[r, h * GV:(h + 1) * GV], op0=ALU.mult, op1=ALU.add).then_inc(s_st, 1)

                keys(0)
                for i in range(N9):
                    if i + 1 < NT:
                        keys(i + 1)
                    if i > 0:
                        dve.wait_ge(s_am, 4 * i)
                        if i > 1:
                            dve.wait_ge(s_at, i - 1)
                        dve.tensor_copy(arow[:], ADA[0:NMOD, :]).then_inc(s_ar, 1)
                    scores(i)
                    gate_exponent(i)
                    if i > 0:
                        normed(i - 1)
                        dve.wait_ge(s_at, i)
                        add_bias(dve, g, ADA, 0, 2 * KD + 4 * (i - 1), 4).then_inc(s_ae, 1)
                    if i < NT:
                        if i > 0:
                            dve.wait_ge(s_st, 4 * i)
                        state(i)
                    if i > 0:
                        gated(i - 1)
                normed(NT)
                gated(NT)
                dve.wait_ge(s_ae, NADA)
                scale_gain(dve, g, g.mul2, SC2, KD)
                dve.wait_ge(s_kn, N9)
                dve.wait_ge(s_s0, 64)
                dve.wait_ge(s_oo, N9)
                for s in range(NSEQ + 1):
                    if s < NSEQ:
                        if s >= 2:
                            dve.wait_ge(s_xp, s - 1)
                        dve.tensor_scalar(kem[s % 2][:], kn[NT % 2][0:TS], rowm[:, s:s + 1], None, ALU.mult).then_inc(s_km, 1)
                    if s == 0:
                        continue
                    dve.wait_ge(s_xp, s)
                    for h in range(GH):
                        r = HALF[h % 2]
                        dve.scalar_tensor_tensor(out=s0[r, s - 1, h, :], in0=s0[r, s - 1, h, :], scalar=dec[r, h // 2, NT + s - 1:NT + s],
                                                 in1=g.bank[s - 1][r, h * GV:(h + 1) * GV], op0=ALU.mult, op1=ALU.add).then_inc(s_x, 1)

            @block.tensor
            def _(pe):
                pe.wait_ge(s_gin, 32)
                for m in range(2):
                    for c, (t0, tw) in enumerate(CHUNKS):
                        pe.matmul(g.bank[3 * m + c][:, 0:tw], wg[:, m * P:(m + 1) * P], al[:, t0:t0 + tw],
                                  start=True, stop=True).then_inc(s_gate, 1)

                def turn_keys(i):
                    rows = P if i < NT else TS
                    if i > 0:
                        pe.wait_ge(s_kn, i)
                    for m in range(2):
                        last = pe.transpose(KT[0:rows, m * P:(m + 1) * P], kend[:, m, tile(i)], g.ident[:])
                    last.then_inc(s_kt, 1)

                def score(i):
                    if i >= 2:
                        pe.wait_ge(s_pt, i - 1)
                    if i < NT:
                        pe.wait_ge(s_qd, 3 * i + 3)
                        out = SC[i % 2][:].rearrange("k (m h t) -> k m h t", m=2, h=2)
                        for m in range(2):
                            for n in range(NSUB):
                                c = slice(n * SUB, (n + 1) * SUB)
                                last = pe.matmul(out[:, m, :, n * SUB:(n + 1) * SUB], ki[i % 2][:, m, n, :], qi[i % 2][:, m, :, c],
                                                 start=True, stop=True)
                    else:
                        out = SC[i % 2][0:TS].rearrange("k (m h t) -> k m h t", m=2, h=2)
                        for m in range(2):
                            last = pe.matmul(out[:, m, :, 0:TS], kinv[:, m, :], qs[:, m], start=True, stop=True)
                    last.then_inc(s_sc, 1)

                def output(i):
                    rows = P if i < NT else TS
                    o = OB[i % 2][0:rows, :]
                    if i >= 2:
                        pe.wait_ge(s_on, i - 1)
                    pe.wait_ge(s_pt, i + 1)
                    pe.wait_ge(s_v[i % 3], 16 * (i // 3 + 1))
                    for h in range(GH):
                        last = pe.matmul(o[:, h * GV:(h + 1) * GV], pt[i % 2][0:rows, h, 0:rows], v[i % 3][0:rows, h * GV:(h + 1) * GV],
                                         start=(h == 0), stop=False, skip_group_check=True)
                    if i < NT:
                        if i > 0:
                            pe.wait_ge(s_st, 4 * i)
                        for m in range(2):
                            last = pe.matmul(o[:, 2 * m * GV:(2 * m + 2) * GV], qdec[i % 2][:, m, :], st[:, 2 * m:2 * m + 2, :],
                                             start=False, stop=True, skip_group_check=True)
                    else:
                        pe.wait_ge(s_s0, 64)
                        for m in range(2):
                            for s in range(NSEQ):
                                last = pe.matmul(o[:, 2 * m * GV:(2 * m + 2) * GV], qm[:, m, s, :], s0[:, s, 2 * m:2 * m + 2, :],
                                                 start=False, stop=(s == NSEQ - 1), skip_group_check=True)
                    last.then_inc(s_oo, 1)

                def outer(i):
                    pe.wait_ge(s_kn, i + 1)
                    if i > 0:
                        pe.wait_ge(s_st, 4 * i)
                    for m in range(2):
                        last = pe.matmul(DS[:, 2 * m * GV:(2 * m + 2) * GV], kn[i % 2][:, m * P:(m + 1) * P],
                                         v[i % 3][:, 2 * m * GV:(2 * m + 2) * GV], start=True, stop=True)
                    last.then_inc(s_ds, 1)

                def turn_out(i):
                    rows = P if i < NT else TS
                    pe.wait_ge(s_on, i + 1)
                    if i >= 1:
                        pe.wait_ge(s_fin, i)
                    for h in range(GH):
                        last = pe.transpose(OT[:, h * P:h * P + rows], on[i % 2][0:rows, h, :], g.ident[0:rows, 0:rows])
                    last.then_inc(s_ot, 1)

                pe.wait_ge(s_d, 13)
                turn_keys(0)
                score(0)

                assert NADA == N9 - 1
                for i in range(N9):
                    if i + 1 < N9:
                        turn_keys(i + 1)
                        score(i + 1)
                    if i > 0:
                        pe.wait_ge(s_ar, i)
                        turn_rows(pe, g, ADA, 0, arow).then_inc(s_at, 1)
                    output(i)
                    if i < NT:
                        outer(i)
                    if i > 0:
                        turn_out(i - 1)
                    if i < NADA:
                        for m in range(4):
                            t = 4 * i + m
                            pe.wait_ge(s_wa[t % 2], 16 * (t // 2 + 1))
                            if m == 0 and i > 0:
                                pe.wait_ge(s_ae, i)
                            condition(pe, g, ADA, wa[t % 2], 2 * m, 2).then_inc(s_am, 1)
                turn_out(NT)
                pe.wait_ge(s_fin, N9)
                for s in range(NSEQ):
                    pe.wait_ge(s_km, s + 1)
                    for m in range(2):
                        last = pe.matmul(g.bank[s][:, 2 * m * GV:(2 * m + 2) * GV], kem[s % 2][:, m * P:(m + 1) * P],
                                         v[NT % 3][0:TS, 2 * m * GV:(2 * m + 2) * GV], start=True, stop=True)
                    last.then_inc(s_xp, 1)


def stage_project_out_and_norm(g):
    nc, io = g.nc, g.io
    w_out = io["w_out"][0]
    xp = io["x_prompt"][0]
    xs = io["x_sample"].rearrange("s t d -> (s t) d")
    NP = D // PANEL
    WIN = [(0, 512), (512, 512)]
    with ExitStack() as ctx:
        w = Panels(g, ctx, "out")
        x = [g.sb(f"out_x{i}", [P, D], ctx=ctx) for i in range(9)]
        tmp = [g.sb(f"out_tmp{i}", [P, TS], ctx=ctx) for i in range(2)]
        sq = [g.sb(f"out_sq{i}", [P, CHUNKS[0][1]], ctx=ctx) for i in range(2)]
        ones = g.sb("out_ones", [P, P], ctx=ctx)
        rb = g.sb("out_rstd", [P, T], ctx=ctx)
        xn = [x[i][:, 0:512] for i in range(2)]
        mod = [x[2 + i][:, 0:512] for i in range(3)]
        xsn = x[5][:, 0:512].rearrange("p (k t) -> p k t", k=KD)
        s_x = [g.sem(f"out_x{i}_loaded") for i in range(9)]
        s_c = g.sem("out_ones_set")
        s_xt = g.sem("out_x_transposed")
        s_xc = g.sem("out_x_copied")
        s_mm = g.sem("out_group_summed")
        s_ev = g.sem("out_added")
        s_tm = g.sem("out_sample_scaled")
        s_sq = g.sem("out_squared")
        s_ss = g.sem("out_squares_summed")
        s_ln = g.sem("n2_ln")
        s_rb = g.sem("n2_rstd_done")
        s_xn = g.sem("n2_normed")
        s_md = g.sem("n2_modulated")
        s_hi = g.sem("n2_hi")
        s_lop = g.sem("n2_pool_lo")
        s_lod = g.sem("n2_dve_lo")
        s_sn = g.sem("n2_sample_steps")
        turns = [None] + [(k, t0) for k in range(KD) for t0 in (0, 4)]
        groups = [(k, c) for k in range(KD) for c in range(3)]
        pieces = [(k, t0, tw) for t0, tw in WIN for k in range(KD)]
        with nc.Block() as block:
            @block.sync
            def _(sp):
                def panel(p):
                    sp.dma_start(w.raw[p % 2][:], w_out[:, p * PANEL:(p + 1) * PANEL].rearrange("(k p) c -> p k c", p=P)).then_inc(w.loaded[p % 2], 16)
                panel(0)
                sp.dma_start(x[8][0:TS], xs).then_inc(s_x[8], 16)
                for i in range(8):
                    sp.dma_start(x[i][:], xp[i * P:(i + 1) * P]).then_inc(s_x[i], 16)
                panel(1)
                for p in range(2, NP):
                    sp.wait_ge(w.lo_done, p - 1)
                    panel(p)

            @block.gpsimd
            def _(pool):
                pool.memset(ones[:], 1.0).then_inc(s_c, 1)
                for p in range(NP):
                    pool.wait_ge(w.hi_done, p + 1)
                    pool.tensor_tensor(w.lo[p % 2][:], w.raw[p % 2][:], w.hi[p % 2][:], ALU.subtract).then_inc(w.lo_done, 1)
                for j, (k, t0, tw) in enumerate(pieces):
                    if j % 2 == 0:
                        pool.wait_ge(s_hi, j + 1)
                        pool.wait_ge(s_md, j + 1)
                        pool.tensor_tensor(g.op_lo[:, k, t0:t0 + tw], mod[j % 3], g.op_hi[:, k, t0:t0 + tw], ALU.subtract).then_inc(s_lop, 1)

            @block.scalar
            def _(act):
                def round_hi(p):
                    act.wait_ge(w.loaded[p % 2], 16 * (p // 2 + 1))
                    if p >= 2:
                        act.wait_ge(s_mm, 6 * (p - 1))
                    act.copy(w.hi[p % 2][:], w.raw[p % 2][:]).then_inc(w.hi_done, 1)

                def copy_turn(j):
                    act.wait_ge(s_xt, j + 1)
                    b = g.bank[3 + j % 2]
                    if j == 0:
                        act.copy(g.x1T[:, :, TP:T], b[:].rearrange("p (k t) -> p k t", k=KD)).then_inc(s_xc, 1)
                    else:
                        k, t0 = turns[j]
                        act.copy(g.x1T[:, k, t0 * P:(t0 + 4) * P], b[:]).then_inc(s_xc, 1)

                round_hi(0)
                for j in range(5):
                    copy_turn(j)
                round_hi(1)
                for k in range(KD):
                    for c, (t0, tw) in enumerate(CHUNKS):
                        j = 3 * k + c
                        act.wait_ge(s_ev, j + 1)
                        if j >= 2:
                            act.wait_ge(s_ss, j - 1)
                        act.activation(sq[j % 2][:, 0:tw], g.x1T[:, k, t0:t0 + tw], ACT.Square).then_inc(s_sq, 1)
                    if k + 2 < KD:
                        copy_turn(2 * k + 5)
                        copy_turn(2 * k + 6)
                    if k % 2 and k // 2 + 2 < NP:
                        round_hi(k // 2 + 2)
                for c, (t0, tw) in enumerate(CHUNKS):
                    act.wait_ge(s_ss, 3 * (KD - 1) + c + 1)
                    act.activation(rb[:, t0:t0 + tw], g.bank[5 + c][:, 0:tw], ACT.Ln, scale=1.0 / D, bias=g.eps[:]).then_inc(s_ln, 1)
                for c, (t0, tw) in enumerate(CHUNKS):
                    act.wait_ge(s_ln, c + 1)
                    act.activation(rb[:, t0:t0 + tw], rb[:, t0:t0 + tw], ACT.Exp, scale=-0.5).then_inc(s_rb, 1)
                for j, (k, t0, tw) in enumerate(pieces):
                    act.wait_ge(s_xn, j + 1)
                    if j >= 3:
                        act.wait_ge(s_lop if (j - 3) % 2 == 0 else s_lod, (j - 3) // 2 + 1)
                    for out, done in ((g.op_hi[:, k, t0:t0 + tw], s_hi), (mod[j % 3], s_md)):
                        act.activation(out, xn[j % 2], ACT.Identity, scale=g.mul2[:, k, 0:1], bias=g.mod(SH2, k)).then_inc(done, 1)

            @block.vector
            def _(dve):
                for j, (kc, c) in enumerate(groups):
                    t0, tw = CHUNKS[c]
                    pw = min(tw, TP - t0)
                    b = g.bank[c]
                    dve.wait_ge(s_mm, j + 1)
                    if c == 0:
                        dve.wait_ge(s_xc, 2 * kc + 3)
                    if c == 2:
                        t = tmp[kc % 2]
                        dve.tensor_tensor(by_seq(t[:]), by_seq(b[:, pw:tw]), seq_row(g.modT[:, GA1 * KD + kc, 1:NMOD]), ALU.mult).then_inc(s_tm, 1)
                        dve.wait_ge(s_tm, kc + 1)
                        dve.tensor_tensor(g.x1T[:, kc, TP:T], g.x1T[:, kc, TP:T], t[:], ALU.add)
                    out = g.x1T[:, kc, t0:t0 + pw]
                    dve.scalar_tensor_tensor(out=out, in0=b[:, 0:pw], scalar=g.mod(GA1, kc), in1=out, op0=ALU.mult,
                                             op1=ALU.add).then_inc(s_ev, 1)

                def low(j):
                    k, t0, tw = pieces[j]
                    dve.wait_ge(s_hi, j + 1)
                    dve.wait_ge(s_md, j + 1)
                    dve.tensor_tensor(g.op_lo[:, k, t0:t0 + tw], mod[j % 3], g.op_hi[:, k, t0:t0 + tw], ALU.subtract).then_inc(s_lod, 1)

                for j, (k, t0, tw) in enumerate(pieces):
                    if j % KD == 0:
                        dve.wait_ge(s_rb, 3 if t0 else 2)
                    if j >= 2:
                        dve.wait_ge(s_hi, j - 1)
                        dve.wait_ge(s_md, j - 1)
                    dve.tensor_tensor(xn[j % 2], g.x1T[:, k, t0:t0 + tw], rb[:, t0:t0 + tw], ALU.mult).then_inc(s_xn, 1)
                    if j >= 2 and (j - 2) % 2:
                        low(j - 2)
                low(len(pieces) - 1)
                rows = lambda a: a.rearrange("p k (s o) -> p k s o", o=1).to_broadcast([P, KD, NSEQ, NEW])
                seqs = xsn.rearrange("p k (s t) -> p k s t", s=NSEQ)
                hi, lo = g.op_hi[:, :, TP:T], g.op_lo[:, :, TP:T]
                rstd = rb[:, TP:T].rearrange("p (o t) -> p o t", o=1).to_broadcast([P, KD, TS])
                dve.tensor_tensor(xsn, g.x1T[:, :, TP:T], rstd, ALU.mult).then_inc(s_sn, 1)
                dve.wait_ge(s_sn, 1)
                dve.tensor_tensor(seqs, seqs, rows(g.mul2[:, :, 1:NMOD]), ALU.mult).then_inc(s_sn, 1)
                dve.wait_ge(s_sn, 2)
                dve.tensor_tensor(seqs, seqs, rows(g.modT[:, SH2 * KD:(SH2 + 1) * KD, 1:NMOD]), ALU.add).then_inc(s_sn, 1)
                dve.wait_ge(s_sn, 3)
                dve.tensor_copy(hi, xsn).then_inc(s_sn, 1)
                dve.wait_ge(s_sn, 4)
                dve.tensor_tensor(lo, xsn, hi, ALU.subtract)

            @block.tensor
            def _(pe):
                def turn(j):
                    b = g.bank[3 + j % 2]
                    if j >= 2:
                        pe.wait_ge(s_xc, j - 1)
                    if j == 0:
                        pe.wait_ge(s_x[8], 16)
                        for k in range(KD):
                            last = pe.transpose(b[:, k * TS:(k + 1) * TS], x[8][0:TS, k * P:(k + 1) * P], g.ident[0:TS, 0:TS])
                    else:
                        k, t0 = turns[j]
                        for i in range(4):
                            if k == 0:
                                pe.wait_ge(s_x[t0 + i], 16)
                            last = pe.transpose(b[:, i * P:(i + 1) * P], x[t0 + i][:, k * P:(k + 1) * P], g.ident[:])
                    last.then_inc(s_xt, 1)

                def sum_squares(j):
                    k, c = groups[j]
                    tw = CHUNKS[c][1]
                    pe.wait_ge(s_sq, j + 1)
                    pe.matmul(g.bank[5 + c][:, 0:tw], ones[:], sq[j % 2][:, 0:tw], start=(k == 0), stop=(k == KD - 1)).then_inc(s_ss, 1)

                for j in range(5):
                    turn(j)
                pe.wait_ge(s_c, 1)
                for j, (kc, c) in enumerate(groups):
                    p, m = divmod(kc, 2)
                    t0, tw = CHUNKS[c]
                    if j % 6 == 0:
                        pe.wait_ge(w.lo_done, p + 1)
                    if j >= 3:
                        pe.wait_ge(s_ev, j - 2)
                    for k in range(KD):
                        cols = slice(m * P, (m + 1) * P)
                        last = three_products(pe, g.bank[c][:, 0:tw], w.hi[p % 2][:, k, cols], w.lo[p % 2][:, k, cols],
                                              g.op_hi[:, k, t0:t0 + tw], g.op_lo[:, k, t0:t0 + tw], k, KD)
                    last.then_inc(s_mm, 1)
                    if j >= 2:
                        sum_squares(j - 2)
                    if c == 2 and kc + 2 < KD:
                        turn(2 * kc + 5)
                        turn(2 * kc + 6)
                sum_squares(len(groups) - 2)
                sum_squares(len(groups) - 1)


def stage_mlp(g, h_hi, h_lo):
    nc, io = g.nc, g.io
    w_up, w_down = io["w_up"][0], io["w_down"][0]
    FB = 512
    NG = FF // FB
    KF = FB // P
    NUP, NDN = 3 * KF, 3 * KD
    NGR = NUP + NDN
    NBANK = 6
    with ExitStack() as ctx:
        w = Panels(g, ctx, "mlp")
        a_hi = g.sb("mlp_a_hi", [P, KF, T], F32R, ctx=ctx)
        a_lo = g.sb("mlp_a_lo", [P, KF, T], F32R, ctx=ctx)
        r = [g.sb(f"mlp_relu{i}", [P, 384], ctx=ctx) for i in range(3)]
        q = [g.sb(f"mlp_sq{i}", [P, 384], ctx=ctx) for i in range(3)]
        tmp = [g.sb(f"mlp_tmp{i}", [P, TS], ctx=ctx) for i in range(2)]
        s_mm = g.sem("mlp_group_summed")
        s_re = g.sem("mlp_relu_done")
        s_sq = g.sem("mlp_squared")
        s_ah = g.sem("mlp_a_hi_done")
        s_al = g.sem("mlp_a_lo_done")
        s_dn = g.sem("mlp_added")
        s_tm = g.sem("mlp_sample_scaled")

        def down_view(t):
            return t[:].rearrange("p k c -> p (k c)").rearrange("p (k c) -> p k c", k=KF)

        def up_groups(u):
            return [(u * NUP // 2 + m * 3 + c, 2 * u + m, c) for m in range(2) for c in range(3)]

        def slot_free(q_):
            return [NUP + NDN // 2 - NGR, 0, NUP // 2, NUP][q_]

        with nc.Block() as block:
            @block.sync
            def _(sp):
                with sp.Fori(0, NG) as n:
                    for p in range(4):
                        s = p % 2
                        sp.wait_ge(w.lo_done, n * 4 + p + 1)
                        if p < 2:
                            src = w_up[:, bass.ds(n * FB + p * PANEL, PANEL)].rearrange("(k p) c -> p k c", p=P)
                            sp.dma_start(w.raw[s][:], src).then_inc(w.loaded[s], 16)
                        else:
                            src = w_down[bass.ds(n * FB, FB), (p - 2) * 512:(p - 1) * 512].rearrange("(k p) c -> p k c", p=P)
                            sp.dma_start(down_view(w.raw[s]), src).then_inc(w.loaded[s], 16)

            def blocks(eng, split, work):
                def block_(n, more):
                    for p in range(4):
                        if p < 3:
                            split(n, p + 1)
                        elif more:
                            split(n + 1, 0)
                        work(n, p)
                split(0, 0)
                with eng.Fori(0, NG - 1) as n:
                    block_(n, True)
                block_(NG - 1, False)

            @block.gpsimd
            def _(pool):
                pool.sem_inc(w.lo_done, 2)

                def split(n, p):
                    s = p % 2
                    pool.wait_ge(w.hi_done, n * 4 + p + 1)
                    pool.tensor_tensor(w.lo[s][:], w.raw[s][:], w.hi[s][:], ALU.subtract).then_inc(w.lo_done, 1)

                def work(n, p):
                    if p < 2:
                        for i, m, c in up_groups(p):
                            t0, tw = CHUNKS[c]
                            pool.wait_ge(s_ah, n * NUP + i + 1)
                            pool.tensor_tensor(a_lo[:, m, t0:t0 + tw], q[i % 3][:, 0:tw], a_hi[:, m, t0:t0 + tw],
                                               ALU.subtract).then_inc(s_al, 1)

                blocks(pool, split, work)

            @block.scalar
            def _(act):
                act.sem_inc(s_al, 3)

                def split(n, p):
                    s = p % 2
                    act.wait_ge(w.loaded[s], (n * 2 + p // 2) * 16 + 16)
                    act.wait_ge(s_mm, n * NGR + (NGR + slot_free(p)))
                    act.copy(w.hi[s][:], w.raw[s][:]).then_inc(w.hi_done, 1)

                def work(n, p):
                    if p < 2:
                        def hi(i, m, c):
                            t0, tw = CHUNKS[c]
                            act.wait_ge(s_sq, n * NUP + i + 1)
                            act.copy(a_hi[:, m, t0:t0 + tw], q[i % 3][:, 0:tw]).then_inc(s_ah, 1)
                        before = None
                        for i, m, c in up_groups(p):
                            tw = CHUNKS[c][1]
                            act.wait_ge(s_mm, NGR + n * NGR + i + 1)
                            act.wait_ge(s_al, n * NUP + i + 1)
                            act.activation(r[i % 3][:, 0:tw], g.bank[i % NBANK][:, 0:tw], ACT.Relu).then_inc(s_re, 1)
                            if before:
                                hi(*before)
                            before = (i, m, c)
                        hi(*before)

                blocks(act, split, work)

            @block.vector
            def _(dve):
                dve.sem_inc(s_dn, NDN)
                dve.sem_inc(s_tm, 2)
                with dve.Fori(0, NG) as n:
                    for i in range(NUP):
                        tw = CHUNKS[i % 3][1]
                        dve.wait_ge(s_re, n * NUP + i + 1)
                        dve.tensor_tensor(q[i % 3][:, 0:tw], r[i % 3][:, 0:tw], r[i % 3][:, 0:tw], ALU.mult).then_inc(s_sq, 1)
                    for i in range(NDN):
                        kc, c = divmod(i, 3)
                        t0, tw = CHUNKS[c]
                        pw = min(tw, TP - t0)
                        b = g.bank[(NUP + i) % NBANK]
                        dve.wait_ge(s_mm, NGR + n * NGR + NUP + i + 1)
                        dve.wait_ge(s_dn, n * NDN + i + 1)
                        if c == 2:
                            t = tmp[kc % 2]
                            dve.tensor_tensor(by_seq(t[:]), by_seq(b[:, pw:tw]), seq_row(g.modT[:, GA2 * KD + kc, 1:NMOD]),
                                              ALU.mult).then_inc(s_tm, 1)
                            dve.wait_ge(s_tm, n * KD + kc + 3)
                            dve.tensor_tensor(g.x1T[:, kc, TP:T], g.x1T[:, kc, TP:T], t[:], ALU.add)
                        out = g.x1T[:, kc, t0:t0 + pw]
                        dve.scalar_tensor_tensor(out=out, in0=b[:, 0:pw], scalar=g.mod(GA2, kc), in1=out, op0=ALU.mult,
                                                 op1=ALU.add).then_inc(s_dn, 1)

            @block.tensor
            def _(pe):
                pe.sem_inc(s_mm, NGR)
                with pe.Fori(0, NG) as n:
                    def bank_free(i):
                        p = i - NBANK
                        if p < 0:
                            pe.wait_ge(s_dn, n * NDN + NDN + p + 1)
                        elif p < NUP:
                            pe.wait_ge(s_re, n * NUP + p + 1)
                        else:
                            pe.wait_ge(s_dn, n * NDN + NDN + p - NUP + 1)

                    for u in range(2):
                        pe.wait_ge(w.lo_done, n * 4 + u + 3)
                        for i, m, c in up_groups(u):
                            t0, tw = CHUNKS[c]
                            bank_free(i)
                            cols = slice((m % 2) * P, (m % 2 + 1) * P)
                            for k in range(KD):
                                last = three_products(pe, g.bank[i % NBANK][:, 0:tw], w.hi[u][:, k, cols], w.lo[u][:, k, cols],
                                                      h_hi[:, k, t0:t0 + tw], h_lo[:, k, t0:t0 + tw], k, KD)
                            last.then_inc(s_mm, 1)
                    for d in range(2):
                        pe.wait_ge(w.lo_done, n * 4 + d + 5)
                        hi, lo = down_view(w.hi[d]), down_view(w.lo[d])
                        for j in range(NDN // 2):
                            m, c = divmod(j, 3)
                            i = NUP + d * NDN // 2 + j
                            t0, tw = CHUNKS[c]
                            bank_free(i)
                            cols = slice(m * P, (m + 1) * P)
                            for k in range(KF):
                                if d == 0 and j < 3:
                                    pe.wait_ge(s_al, 3 + n * NUP + 3 * k + c + 1)
                                last = three_products(pe, g.bank[i % NBANK][:, 0:tw], hi[:, k, cols], lo[:, k, cols],
                                                      a_hi[:, k, t0:t0 + tw], a_lo[:, k, t0:t0 + tw], k, KF)
                            last.then_inc(s_mm, 1)


def stage_final(g):
    nc, io = g.nc, g.io
    N9 = NT + 1
    yp = io["y_prompt"][0]
    ys = io["y_sample"].rearrange("s t d -> (s t) d")
    with ExitStack() as ctx:
        sb = lambda *a: g.sb(*a, ctx=ctx)
        gain = sb("fin_gain", [P, D])
        sq = [sb(f"fin_sq{i}", [P, D]) for i in range(2)]
        ss = sb("fin_ss", [P, N9, 2])
        rs = sb("fin_rstd", [P, N9])
        y = [sb(f"fin_y{i}", [P, D]) for i in range(3)]
        s_g = g.sem("fin_gain_loaded")
        s_tr = g.sem("fin_turned")
        s_sq = g.sem("fin_squared")
        s_su = g.sem("fin_summed")
        s_ln = g.sem("fin_ln")
        s_rs = g.sem("fin_rstd_done")
        s_y = g.sem("fin_y_done")
        s_out = [g.sem(f"fin_y{i}_stored") for i in range(3)]
        with nc.Block() as block:
            @block.sync
            def _(sp):
                sp.dma_start(gain[:], io["g_final"].rearrange("(o d) -> o d", o=1).to_broadcast([P, D])).then_inc(s_g, 16)
                for i in range(N9):
                    w = P if i < NT else TS
                    sp.wait_ge(s_y, 2 * i + 2)
                    sp.dma_start(yp[i * P:(i + 1) * P] if i < NT else ys, y[i % 3][0:w]).then_inc(s_out[i % 3], 16)
                for i in range(3):
                    sp.wait_ge(s_out[i], 16 * 3)

            @block.tensor
            def _(pe):
                for i in range(N9):
                    w = P if i < NT else TS
                    for half in range(2):
                        if i >= 4:
                            pe.wait_ge(s_y, 2 * (i - 4) + half + 1)
                        for k in range(4):
                            last = pe.transpose(g.bank[(2 * i + half) % 8][0:w, k * P:(k + 1) * P],
                                                g.x1T[:, half * 4 + k, i * P:i * P + w], g.ident[:])
                        last.then_inc(s_tr, 1)

            @block.scalar
            def _(act):
                for i in range(N9):
                    w = P if i < NT else TS
                    for half in range(2):
                        act.wait_ge(s_tr, 2 * i + half + 1)
                        if i >= 2:
                            act.wait_ge(s_sq, 2 * (i - 2) + half + 1)
                        act.activation(sq[i % 2][0:w, half * 512:half * 512 + 512], g.bank[(2 * i + half) % 8][0:w], ACT.Square,
                                       accum_out=ss[0:w, i, half:half + 1]).then_inc(s_sq, 1)
                    act.wait_ge(s_su, i + 1)
                    act.activation(rs[0:w, i:i + 1], rs[0:w, i:i + 1], ACT.Ln, scale=1.0 / D, bias=g.eps[0:w]).then_inc(s_ln, 1)
                    act.wait_ge(s_ln, i + 1)
                    act.activation(rs[0:w, i:i + 1], rs[0:w, i:i + 1], ACT.Exp, scale=-0.5).then_inc(s_rs, 1)

            @block.vector
            def _(dve):
                dve.wait_ge(s_g, 16)
                for i in range(N9):
                    w = P if i < NT else TS
                    dve.wait_ge(s_sq, 2 * i + 2)
                    dve.tensor_tensor(rs[0:w, i:i + 1], ss[0:w, i, 0:1], ss[0:w, i, 1:2], ALU.add).then_inc(s_su, 1)
                    dve.wait_ge(s_rs, i + 1)
                    if i >= 3:
                        dve.wait_ge(s_out[i % 3], 16 * (i // 3))
                    for half in range(2):
                        cols = slice(half * 512, half * 512 + 512)
                        dve.scalar_tensor_tensor(out=y[i % 3][0:w, cols], in0=g.bank[(2 * i + half) % 8][0:w], scalar=rs[0:w, i:i + 1],
                                                 in1=gain[0:w, cols], op0=ALU.mult, op1=ALU.mult).then_inc(s_y, 1)


def build(nc, io):
    with ExitStack() as ctx:
        g = Program(nc, io, ctx)
        g.op_hi = g.sb("op_hi", [P, KD, T], F32R)
        g.op_lo = g.sb("op_lo", [P, KD, T], F32R)
        stage_start(g)
        stage_project_in(g, g.op_hi, g.op_lo)
        with g.part():
            stage_project_gla_and_sample_attention(g)
        with ExitStack() as c:
            g.vnat = g.sb("vnat", [P, NT + 1, SB], ctx=c)
            with g.part():
                stage_natural(g)
                stage_prompt_attention(g)
        with g.part():
            stage_gla(g)
        g.x1T = g.sb("x1T", [P, KD, T])
        stage_project_out_and_norm(g)
        stage_mlp(g, g.op_hi, g.op_lo)
        stage_final(g)


OUTS = [("y_prompt", (1, TP, D)), ("y_sample", (NSEQ, NEW, D)),
        ("k_prompt", (1, 1, TP, HEADS, HD)), ("v_prompt", (1, 1, TP, HEADS, HD)),
        ("state_prompt", (1, 1, GH, GK, GV)),
        ("k_sample", (1, NSEQ, NEW, HEADS, HD)), ("v_sample", (1, NSEQ, NEW, HEADS, HD)),
        ("state_sample", (1, NSEQ, GH, GK, GV))]

INS = ["x_prompt", "x_sample", "c_prompt", "c_sample", "cache_k", "cache_v", "state_gla", "page_table", "w_ada", "b_ada",
       "g_mix", "w_in", "b_sb", "w_gla_gate", "b_gla_gate", "g_gla_out", "w_out", "g_ffn", "w_up", "w_down", "g_final"]


def kernel(**inputs):
    import numpy as np
    from concourse import bacc
    from concourse.bass_utils import run_bass_kernel_spmd

    nc = bacc.Bacc("TRN2", target_bir_lowering=False, num_devices=1)
    arrays, io = {}, {}
    for name in INS:
        a = np.ascontiguousarray(inputs[name])
        arrays[f"in_{name}"] = a
        io[name] = nc.dram_tensor(f"in_{name}", a.shape, mybir.dt.from_np(a.dtype), kind="ExternalInput").ap()
    for name, shape in OUTS:
        io[name] = nc.dram_tensor(name, shape, F32, kind="ExternalOutput").ap()
    build(nc, io)
    r = run_bass_kernel_spmd(nc, [arrays], core_ids=[0])
    return tuple(r.results[0][name] for name, _ in OUTS)
```

```python
from contextlib import ExitStack, contextmanager

import concourse.bass as bass
from concourse import mybir

F32 = mybir.dt.float32
F32R = mybir.dt.float32r
BF16 = mybir.dt.bfloat16
ALU = mybir.AluOpType
ACT = mybir.ActivationFunctionType

P = 128
D = 1024
KD = D // P
TP = 1024
NSEQ, NEW = 8, 8
TS = NSEQ * NEW
T = TP + TS
NT = TP // P
PAGE = 128
NPAGE = 8
HEADS, HD = 8, 64
SB = HEADS * HD
GH, GK, GV = 4, 64, 128
RANK = 16
IN_W = 3 * SB + 2 * GH * GK + 2 * GH * GV + RANK
FF = 4096
EPS = 1e-6
GATE = 1.0 / 16.0
NEG = -1e30
BIG = 3e38
PANEL = 256
NMOD = 1 + NSEQ
CHUNKS = [(0, 384), (384, 384), (768, 320)]
SUB = 32
ROW_Q, ROW_K, ROW_V = 0, SB, 2 * SB
ROW_QG = 3 * SB
ROW_KG = ROW_QG + GH * GK
ROW_VG = ROW_KG + GH * GK
ROW_RG = ROW_VG + GH * GV
ROW_A = ROW_RG + GH * GV
LAST = IN_W - P
VEC_B = 2 * KD + 3
SH1, SC1, GA1, SH2, SC2, GA2 = range(6)


class Program:

    def __init__(self, nc, io, ctx):
        self.nc, self.io, self.ctx = nc, io, ctx
        self.bank = [ctx.enter_context(nc.psum_tensor(f"bank{i}", [P, 512], F32)) for i in range(8)]
        self.ident = self.sb("ident", [P, P])
        self.ident16 = self.sb("ident16", [P, P], BF16)
        self.causal16 = self.sb("causal16", [P, P], BF16)
        self.modT = self.sb("modT", [P, 6 * KD, NMOD])
        self.vecT = self.sb("vecT", [P, VEC_B + 6 * KD])
        self.cT = self.sb("cT", [P, KD, NMOD])
        self.mul1 = self.sb("mul1", [P, KD, NMOD])
        self.mul2 = self.sb("mul2", [P, KD, NMOD])
        self.sample_o = self.sb("sample_o", [P, 4, NSEQ, NEW])
        self.eps = self.sb("eps", [P, 1])
        self.projT = nc.dram_tensor("projT", [IN_W, T], F32, kind="Internal").ap()
        self.vgnat = nc.dram_tensor("vgnat", [T, GH * GV], F32, kind="Internal").ap()

    def sb(self, name, shape, dt=F32, ctx=None):
        return (ctx or self.ctx).enter_context(self.nc.sbuf_tensor(name, shape, dt))

    def sem(self, name):
        return self.nc.alloc_semaphore(name=name)

    @contextmanager
    def part(self):
        before = self.nc.snapshot_sems()
        yield
        self.nc.clear_and_free_semaphores(self.nc.allocated_since(before))
        self.nc.all_engine_barrier()

    def mod(self, part, kc, row=0):
        return self.modT[:, part * KD + kc, row:row + 1]


def seq_row(a, n=NSEQ, w=NEW):
    return a.rearrange("p (s o) -> p s o", o=1).to_broadcast([P, n, w])


def by_seq(a):
    return a.rearrange("p (s t) -> p s t", s=NSEQ)


def at_least(eng, sem, value):
    if not isinstance(value, int) or value > 0:
        eng.wait_ge(sem, value)


class Panels:

    def __init__(self, g, ctx, tag, buffers=None):
        self.raw = buffers.raw if buffers else [g.sb(f"{tag}_raw{i}", [P, KD, PANEL], ctx=ctx) for i in range(2)]
        self.hi = buffers.hi if buffers else [g.sb(f"{tag}_hi{i}", [P, KD, PANEL], F32R, ctx=ctx) for i in range(2)]
        self.lo = buffers.lo if buffers else [g.sb(f"{tag}_lo{i}", [P, KD, PANEL], F32R, ctx=ctx) for i in range(2)]
        self.loaded = [g.sem(f"{tag}_raw{i}_loaded") for i in range(2)]
        self.hi_done = g.sem(f"{tag}_hi_done")
        self.lo_done = g.sem(f"{tag}_lo_done")

    def load(self, dma, src, cols, s):
        dma.dma_start(self.raw[s][:], src[:, cols].rearrange("(k p) c -> p k c", p=P)).then_inc(self.loaded[s], 16)

    def first_hi(self, act):
        act.wait_ge(self.loaded[0], 16)
        act.copy(self.hi[0][:], self.raw[0][:]).then_inc(self.hi_done, 1)

    def first_lo(self, pool):
        pool.wait_ge(self.hi_done, 1)
        pool.tensor_tensor(self.lo[0][:], self.raw[0][:], self.hi[0][:], ALU.subtract).then_inc(self.lo_done, 1)


def condition(pe, g, bank, w, k0, n):
    for k in range(k0, k0 + n):
        last = pe.matmul(bank[0:NMOD, :], g.cT[:, k, :], w[:, k - k0, :], start=(k == 0), stop=(k == KD - 1))
    return last


def turn_rows(pe, g, bank, c0, rows):
    for m in range(4):
        last = pe.transpose(bank[:, c0 + m * NMOD:c0 + (m + 1) * NMOD], rows[:, m * P:(m + 1) * P], g.ident[0:NMOD, 0:NMOD])
    return last


def add_bias(dve, g, bank, c0, tile, n):
    bias = g.vecT[:, VEC_B + tile:VEC_B + tile + n].rearrange("p (m o) -> p m o", o=1).to_broadcast([P, n, NMOD])
    src = bank[:, c0:c0 + n * NMOD].rearrange("p (m r) -> p m r", m=n)
    return dve.tensor_tensor(g.modT[:, tile:tile + n, :], src, bias, ALU.add)


def scale_gain(dve, g, mul, part, at):
    gain = g.vecT[:, at:at + KD].rearrange("p (k o) -> p k o", o=1).to_broadcast([P, KD, NMOD])
    return dve.scalar_tensor_tensor(out=mul[:], in0=g.modT[:, part * KD:(part + 1) * KD, :], scalar=1.0, in1=gain,
                                    op0=ALU.add, op1=ALU.mult)


def stage_start(g, w_in):
    nc, io = g.nc, g.io
    hT_hi, hT_lo = g.op_hi, g.op_lo
    GROUPS = [(0, 4), (4, 4), (8, 1)]
    xp = io["x_prompt"][0]
    xs = io["x_sample"].rearrange("s t d -> (s t) d")
    NCH = 2 * D // 512
    with ExitStack() as ctx:
        sb = lambda *a: g.sb(*a, ctx=ctx)
        c_in = sb("ada_c", [NMOD, D])
        cx = sb("ada_cx", [P, KD, NMOD])
        w = [sb(f"ada_w{i}", [P, KD, 512]) for i in range(2)]
        rows = [sb(f"ada_rows{i}", [NMOD, 512]) for i in range(2)]
        vec = sb("ada_vec", [VEC_B + 6 * KD, P])
        x = [sb(f"n1_x{i}", [P, D]) for i in range(9)]
        sq = sb("n1_sq", [P, D])
        ss = sb("n1_ss", [P, 9])
        tmp = [sb(f"n1_tmp{i}", [P, 512]) for i in range(3)]
        s_cin = g.sem("ada_c_loaded")
        s_vec = g.sem("ada_vectors_loaded")
        s_w = [g.sem(f"ada_w{i}_loaded") for i in range(2)]
        s_const = g.sem("ada_const")
        s_eps = g.sem("eps_set")
        s_cT = g.sem("ada_c_transposed")
        s_cx = g.sem("ada_cx_copied")
        s_e = g.sem("ada_exp")
        s_silu = g.sem("ada_silu")
        s_vT = g.sem("ada_vectors_transposed")
        s_mm = g.sem("ada_chunk_summed")
        s_row = g.sem("ada_rows_copied")
        s_rT = g.sem("ada_rows_transposed")
        s_mod = g.sem("ada_mod_done")
        s_x = [g.sem(f"n1_x{i}_loaded") for i in range(9)]
        s_ss = g.sem("n1_sumsq")
        s_ln = g.sem("n1_ln")
        s_rstd = g.sem("n1_rstd")
        s_xn = g.sem("n1_normed")
        s_tr = g.sem("n1_transposed")
        s_tmp = g.sem("n1_modulated")
        s_dtmp = g.sem("n1_sample_steps")
        s_hi = g.sem("n1_hi")
        s_lo = g.sem("n1_lo")
        steps = [(gi, t0, n, k) for gi, (t0, n) in enumerate(GROUPS) for k in range(KD)]
        NB, NPR = 4, 2 * KD
        with nc.Block() as block:
            @block.sync
            def _(sp):
                sp.dma_start(c_in[0:1, :], io["c_prompt"]).then_inc(s_cin, 16)
                sp.dma_start(c_in[1:NMOD, :], io["c_sample"]).then_inc(s_cin, 16)
                def chunk(i):
                    if i >= 2:
                        sp.wait_ge(s_mm, i - 1)
                    cols = slice(i * 512, i * 512 + 512)
                    sp.dma_start(w[i % 2][:], io["w_ada"][0][:, cols].rearrange("(k p) c -> p k c", p=P)).then_inc(s_w[i % 2], 16)

                for i in range(9):
                    if i in (0, 2):
                        chunk(i // 2)
                    src = xp[i * P:(i + 1) * P, :] if i < 8 else xs
                    sp.dma_start(x[i][0:src.shape[0], :], src).then_inc(s_x[i], 16)
                for i in range(2, NCH):
                    chunk(i)
                for p in range(2):
                    w_in.load(sp, io["w_in"][0], slice(p * PANEL, (p + 1) * PANEL), p)

            @block.gpsimd
            def _(pool):
                pool.memset(g.ident[:], 0.0).then_inc(s_const, 1)
                pool.memset(g.causal16[:], NEG).then_inc(s_const, 1)
                pool.wait_ge(s_const, 2)
                pool.affine_select(out=g.ident[:], in_=g.ident[:], compare_op=ALU.not_equal, fill=1.0,
                                   base=0, pattern=[[-1, P]], channel_multiplier=1).then_inc(s_const, 1)
                pool.affine_select(out=g.causal16[:], in_=g.causal16[:], compare_op=ALU.is_ge, fill=0.0,
                                   base=0, pattern=[[1, P]], channel_multiplier=-1).then_inc(s_const, 1)
                pool.wait_ge(s_const, 4)
                pool.tensor_copy(g.ident16[:], g.ident[:]).then_inc(s_const, 1)
                w_in.first_lo(pool)

            @block.scalar
            def _(act):
                at = 0
                for name, n in (("g_mix", KD), ("g_ffn", KD), ("b_gla_gate", 2), ("g_gla_out", 1), ("b_ada", 6 * KD)):
                    act.dma_start(vec[at:at + n, :], io[name].rearrange("a (k p) -> (a k) p", p=P)).then_inc(s_vec, 16)
                    at += n
                act.preload_act_table_set("natural_log_exp_and_others")
                act.wait_ge(s_cx, 1)
                act.activation(g.cT[:], cx[:], ACT.Exp, scale=-1.0).then_inc(s_e, 1)
                act.wait_ge(s_eps, 1)
                for i in range(9):
                    n = P if i < 8 else TS
                    act.wait_ge(s_x[i], 16)
                    act.activation(sq[0:n, :], x[i][0:n, :], ACT.Square, accum_out=ss[0:n, i:i + 1]).then_inc(s_ss, 1)
                    act.wait_ge(s_ss, i + 1)
                    act.activation(ss[0:n, i:i + 1], ss[0:n, i:i + 1], ACT.Ln, scale=1.0 / D, bias=g.eps[0:n, :]).then_inc(s_ln, 1)
                    act.wait_ge(s_ln, i + 1)
                    act.activation(ss[0:n, i:i + 1], ss[0:n, i:i + 1], ACT.Exp, scale=-0.5).then_inc(s_rstd, 1)
                w_in.first_hi(act)
                act.wait_ge(s_mod, 2)
                for j, (gi, t0, n, k) in enumerate(steps[:NPR]):
                    act.wait_ge(s_tr, j + 1)
                    if j >= 3:
                        act.wait_ge(s_lo, j - 2)
                    for out, done in ((hT_hi[:, k, t0 * P:t0 * P + 512], s_hi), (tmp[j % 3][:], s_tmp)):
                        act.activation(out, g.bank[j % NB][:], ACT.Identity, scale=g.mul1[:, k, 0:1], bias=g.mod(SH1, k)).then_inc(done, 1)

            @block.vector
            def _(dve):
                dve.memset(g.eps[:], EPS).then_inc(s_eps, 1)
                dve.wait_ge(s_cT, 1)
                dve.tensor_copy(cx[:].rearrange("p k r -> p (k r)"), g.bank[7][:, 0:KD * NMOD]).then_inc(s_cx, 1)
                dve.wait_ge(s_e, 1)
                dve.tensor_scalar(g.cT[:], g.cT[:], 1.0, None, ALU.add).then_inc(s_silu, 1)
                dve.wait_ge(s_silu, 1)
                dve.reciprocal(g.cT[:], g.cT[:]).then_inc(s_silu, 1)
                dve.wait_ge(s_silu, 2)
                dve.tensor_tensor(g.cT[:], cx[:], g.cT[:], ALU.mult).then_inc(s_silu, 1)
                dve.wait_ge(s_vT, 1)
                dve.tensor_copy(g.vecT[:], g.bank[6][:, 0:VEC_B + 6 * KD]).then_inc(s_mod, 1)
                for i in range(9):
                    n = P if i < 8 else TS
                    dve.wait_ge(s_rstd, i + 1)
                    dve.tensor_scalar(x[i][0:n, :], x[i][0:n, :], ss[0:n, i:i + 1], None, ALU.mult).then_inc(s_xn, 1)
                    if i % 2 == 0 and i >= 2:
                        j = i // 2 - 1
                        dve.wait_ge(s_mm, j + 1)
                        if j >= 2:
                            dve.wait_ge(s_rT, j - 1)
                        dve.tensor_copy(rows[j % 2][:], g.bank[4 + j % 2][0:NMOD, :]).then_inc(s_row, 1)
                dve.wait_ge(s_rT, NCH)
                dve.wait_ge(s_mod, 1)
                add_bias(dve, g, g.bank[7], 0, 0, 2 * KD).then_inc(s_silu, 1)
                dve.wait_ge(s_silu, 4)
                scale_gain(dve, g, g.mul1, SC1, 0).then_inc(s_mod, 1)
                for j, (gi, t0, n, k) in enumerate(steps):
                    t = tmp[j % 3]
                    if n > 1:
                        dve.wait_ge(s_hi, j + 1)
                        dve.wait_ge(s_tmp, j + 1)
                        dve.tensor_tensor(hT_lo[:, k, t0 * P:t0 * P + 512], t[:], hT_hi[:, k, t0 * P:t0 * P + 512],
                                          ALU.subtract).then_inc(s_lo, 1)
                    else:
                        done = 3 * (j - NPR)
                        if j == NPR:
                            dve.wait_ge(s_mod, 2)
                        dve.wait_ge(s_tr, j + 1)
                        dve.wait_ge(s_lo, j - 2)
                        dve.tensor_tensor(by_seq(t[:, 0:TS]), by_seq(g.bank[j % NB][:, 0:TS]), seq_row(g.mul1[:, k, 1:NMOD]),
                                          ALU.mult).then_inc(s_dtmp, 1)
                        dve.wait_ge(s_dtmp, done + 1)
                        dve.tensor_tensor(by_seq(t[:, 0:TS]), by_seq(t[:, 0:TS]), seq_row(g.modT[:, SH1 * KD + k, 1:NMOD]),
                                          ALU.add).then_inc(s_dtmp, 1)
                        dve.wait_ge(s_dtmp, done + 2)
                        dve.tensor_copy(hT_hi[:, k, TP:T], t[:, 0:TS]).then_inc(s_dtmp, 1)
                        dve.wait_ge(s_dtmp, done + 3)
                        dve.tensor_tensor(hT_lo[:, k, TP:T], t[:, 0:TS], hT_hi[:, k, TP:T], ALU.subtract).then_inc(s_lo, 1)

            @block.tensor
            def _(pe):
                pe.wait_ge(s_cin, 32)
                pe.wait_ge(s_const, 5)
                for k in range(KD):
                    last = pe.transpose(g.bank[7][:, k * NMOD:(k + 1) * NMOD], c_in[:, k * P:(k + 1) * P], g.ident[0:NMOD, 0:NMOD])
                last.then_inc(s_cT, 1)
                pe.wait_ge(s_vec, 5 * 16)
                nv = VEC_B + 6 * KD
                pe.transpose(g.bank[6][:, 0:nv], vec[:], g.ident[0:nv, 0:nv]).then_inc(s_vT, 1)
                pe.wait_ge(s_silu, 3)

                def chunk(i):
                    pe.wait_ge(s_w[i % 2], 16 * (i // 2 + 1))
                    if i >= 2:
                        pe.wait_ge(s_row, i - 1)
                    condition(pe, g, g.bank[4 + i % 2], w[i % 2], 0, KD).then_inc(s_mm, 1)

                def turn_chunk(i):
                    pe.wait_ge(s_row, i + 1)
                    turn_rows(pe, g, g.bank[7], 4 * i * NMOD, rows[i % 2]).then_inc(s_rT, 1)

                def turn(j):
                    gi, t0, n, k = steps[j]
                    pe.wait_ge(s_xn, t0 + n)
                    if j >= NB:
                        pe.wait_ge(s_lo, j - NB + 1)
                    for i in range(n):
                        m = P if n > 1 else TS
                        last = pe.transpose(g.bank[j % NB][:, i * P:i * P + m], x[t0 + i][0:m, k * P:(k + 1) * P],
                                            g.ident[0:m, 0:m])
                    last.then_inc(s_tr, 1)

                chunk(0)
                for i in range(1, NCH):
                    chunk(i)
                    turn_chunk(i - 1)
                turn_chunk(NCH - 1)
                for j in range(NB):
                    turn(j)
                for j in range(NB, len(steps)):
                    turn(j)


def three_products(pe, out, w_hi, w_lo, x_hi, x_lo, k, nk):
    pe.matmul(out, w_hi, x_hi, start=(k == 0), stop=False)
    pe.matmul(out, w_hi, x_lo, start=False, stop=False)
    return pe.matmul(out, w_lo, x_hi, start=False, stop=(k == nk - 1))


def stage_project_in(g, w, hT_hi, hT_lo):
    nc, io = g.nc, g.io
    w_in = io["w_in"][0]
    NP = ROW_QG // PANEL
    assert NP % 2 == 0
    with ExitStack() as ctx:
        stg = [g.sb(f"in_stage{i}", [P, T], ctx=ctx) for i in range(4)]
        s_mm = g.sem("in_group_summed")
        s_aev = g.sem("in_act_evacuated")
        s_dev = g.sem("in_dve_evacuated")
        s_out = [g.sem(f"in_stage{i}_stored") for i in range(4)]
        last_w = slice(0, P)
        with nc.Block() as block:
            @block.sync
            def _(sp):
                with sp.Fori(0, NP // 2 - 1) as n:
                    for s in range(2):
                        sp.wait_ge(w.lo_done, n * 2 + s + 1)
                        w.load(sp, w_in, bass.ds((n * 2 + 2 + s) * PANEL, PANEL), s)
                sp.wait_ge(w.lo_done, NP - 1)
                sp.dma_start(w.raw[0][:, :, last_w], w_in[:, LAST:IN_W].rearrange("(k p) c -> p k c", p=P)).then_inc(w.loaded[0], 16)

            @block.gpsimd
            def _(pool):
                def low(i, s):
                    pool.wait_ge(w.hi_done, i + 1)
                    pool.tensor_tensor(w.lo[s][:], w.raw[s][:], w.hi[s][:], ALU.subtract).then_inc(w.lo_done, 1)

                with pool.Fori(0, NP // 2 - 1) as n:
                    low(n * 2 + 1, 1)
                    low(n * 2 + 2, 0)
                low(NP - 1, 1)
                pool.wait_ge(w.hi_done, NP + 1)
                pool.tensor_tensor(w.lo[0][:, :, last_w], w.raw[0][:, :, last_w], w.hi[0][:, :, last_w],
                                   ALU.subtract).then_inc(w.lo_done, 1)

            @block.tensor
            def _(pe):
                pe.sem_inc(s_mm, 12)

                def groups(s, n, tiles):
                    for m in range(tiles):
                        for c, (t0, tw) in enumerate(CHUNKS):
                            gi = m * 3 + c
                            pe.wait_ge(s_dev if gi % 2 else s_aev, n * 6 + s * 3 + gi // 2 + 1)
                            for k in range(KD):
                                cols = slice(m * P, (m + 1) * P)
                                last = three_products(pe, g.bank[gi][:, 0:tw], w.hi[s][:, k, cols], w.lo[s][:, k, cols],
                                                      hT_hi[:, k, t0:t0 + tw], hT_lo[:, k, t0:t0 + tw], k, KD)
                            last.then_inc(s_mm, 1)

                with pe.Fori(0, NP // 2) as n:
                    for s in range(2):
                        pe.wait_ge(w.lo_done, n * 2 + s + 1)
                        groups(s, n, 2)
                pe.wait_ge(w.lo_done, NP + 1)
                groups(0, NP // 2, 1)

            def evacuate(eng, copy, mine, s_ev, prime):
                if prime:
                    eng.sem_inc(s_ev, 3)

                def groups(s, n, tiles):
                    for gi in range(3 * tiles):
                        if gi % 2 != mine:
                            continue
                        m, c = divmod(gi, 3)
                        t0, tw = CHUNKS[c]
                        st = 2 * s + m
                        eng.wait_ge(s_mm, 12 + n * 12 + s * 6 + gi + 1)
                        eng.wait_ge(s_out[st], n * 16 + 16)
                        copy(stg[st][:, t0:t0 + tw], g.bank[gi][:, 0:tw]).then_inc(s_ev, 1)

                with eng.Fori(0, NP // 2) as n:
                    for s in range(2):
                        groups(s, n, 2)
                groups(0, NP // 2, 1)

            @block.vector
            def _(dve):
                evacuate(dve, dve.tensor_copy, 1, s_dev, True)

            @block.scalar
            def _(act):
                for i in range(4):
                    act.sem_inc(s_out[i], 16)
                act.sem_inc(s_aev, 3)

                def groups(s, n, tiles):
                    for gi in range(3 * tiles):
                        m, c = divmod(gi, 3)
                        t0, tw = CHUNKS[c]
                        st = 2 * s + m
                        if gi % 2 == 0:
                            act.wait_ge(s_mm, 12 + n * 12 + s * 6 + gi + 1)
                            act.wait_ge(s_out[st], n * 16 + 16)
                            act.copy(stg[st][:, t0:t0 + tw], g.bank[gi][:, 0:tw]).then_inc(s_aev, 1)
                        if c == 2:
                            act.wait_ge(s_aev, 3 + n * 6 + s * 3 + (gi // 2 + 1))
                            act.wait_ge(s_dev, 3 + n * 6 + s * 3 + (gi + 1) // 2)
                            if tiles == 2:
                                dst, src = g.projT[bass.ds((n * 4 + st) * P, P), :], stg[st][:]
                            else:
                                dst, src = g.projT[ROW_A:IN_W, :], stg[st][P - RANK:P, :]
                            act.dma_start(dst, src).then_inc(s_out[st], 16)

                def round_hi(s, n, cols):
                    act.wait_ge(w.loaded[s], n * 16 + 16)
                    act.wait_ge(s_mm, n * 12 + s * 6 + 6)
                    act.copy(w.hi[s][:, :, cols], w.raw[s][:, :, cols]).then_inc(w.hi_done, 1)

                with act.Fori(0, NP // 2 - 1) as n:
                    round_hi(1, n, slice(0, PANEL))
                    groups(0, n, 2)
                    round_hi(0, n + 1, slice(0, PANEL))
                    groups(1, n, 2)
                round_hi(1, NP // 2 - 1, slice(0, PANEL))
                groups(0, NP // 2 - 1, 2)
                round_hi(0, NP // 2, last_w)
                groups(1, NP // 2 - 1, 2)
                groups(0, NP // 2, 1)
                act.wait_ge(s_out[0], 16 * (NP // 2 + 2))
                for i in range(1, 4):
                    act.wait_ge(s_out[i], 16 * (NP // 2 + 1))


class HeadOperands:

    LO, HI = slice(0, HD), slice(HD, P)

    def __init__(self, g, ctx):
        sb = lambda *a: g.sb(*a, ctx=ctx)
        self.g = g
        self.qraw = [sb(f"pa_qraw{i}", [P, TP]) for i in range(2)]
        self.kraw = [sb(f"pa_kraw{i}", [P, TP]) for i in range(2)]
        self.qh = sb("pa_qh", [P, TP], F32R)
        self.qa, self.qb, self.ka, self.kb = ([sb(f"pa_{n}{i}", [P, TP], F32R) for i in range(2)] for n in ("qa", "qb", "ka", "kb"))
        self.bq = sb("pa_bias", [P, HEADS])
        self.bh = sb("pa_bias_hi", [P, HEADS], F32R)
        self.loaded = [g.sem(f"pa_qk{i}_loaded") for i in range(2)]
        self.s_b = g.sem("pa_bias_loaded")
        self.s_bd = g.sem("pa_bias_split")
        self.kb_set = g.sem("pa_kb_constants")
        self.act_done = g.sem("pa_act_prepared")
        self.pool_done = g.sem("pa_pool_prepared")
        self.qb_done = g.sem("pa_bias_spread")

    def load_bias(self, sp):
        sp.dma_start(self.bq[:], self.g.io["b_sb"].to_broadcast([P, HEADS])).then_inc(self.s_b, 16)

    def load(self, sp, h, slot):
        at_least(sp, self.pool_done, 3 * (h - 2) + 3)
        at_least(sp, self.act_done, 4 * (h - 2) + 4)
        for raw, row in ((self.qraw, ROW_Q), (self.kraw, ROW_K)):
            for half in (self.LO, self.HI):
                sp.dma_start(raw[slot][half, :], self.g.projT[bass.ds(h * HD + row, HD), 0:TP]).then_inc(self.loaded[slot], 16)

    def set_kb(self, pool):
        for i in range(2):
            pool.memset(self.kb[i][self.HI, :].bitcast(F32), 1.0 / 32).then_inc(self.kb_set, 1)

    def pool_part(self, pool, h, slot):
        lo, hi = self.LO, self.HI
        pool.wait_ge(self.act_done, 4 * h + 2)
        pool.tensor_tensor(self.kb[slot][lo, :], self.kraw[slot][lo, :], self.ka[slot][lo, :], ALU.subtract).then_inc(self.pool_done, 1)
        pool.tensor_scalar(self.qraw[slot][hi, :], self.qraw[slot][hi, :], HD ** -0.5, 0.0, ALU.mult, ALU.add).then_inc(self.pool_done, 1)
        pool.wait_ge(self.pool_done, 3 * h + 2)
        pool.tensor_tensor(self.qa[slot][hi, :], self.qraw[slot][hi, :], self.qh[hi, :], ALU.subtract).then_inc(self.pool_done, 1)

    def act_part(self, act, h, slot, k, scored=None, steps=0):
        lo, hi = self.LO, self.HI
        if k == 0:
            act.wait_ge(self.loaded[slot], (h - slot + 2) * 32)
            at_least(act, scored, (h - 1) * steps)
            at_least(act, self.pool_done, 3 * h)
            act.activation(self.qh[hi, :], self.qraw[slot][hi, :], ACT.Copy, scale=HD ** -0.5).then_inc(self.act_done, 1)
            act.copy(self.ka[slot][:], self.kraw[slot][:]).then_inc(self.act_done, 1)
        if k == 1:
            for q in (self.qa, self.qb):
                act.activation(q[slot][lo, :], self.qraw[slot][lo, :], ACT.Copy, scale=HD ** -0.5).then_inc(self.act_done, 1)

    def split_bias(self, dve):
        dve.wait_ge(self.s_b, 16)
        dve.tensor_copy(self.bh[:], self.bq[:]).then_inc(self.s_bd, 1)
        dve.wait_ge(self.s_bd, 1)
        lo_rows = slice(96, P)
        dve.tensor_tensor(self.bq[lo_rows], self.bq[lo_rows], self.bh[lo_rows].bitcast(F32), ALU.subtract).then_inc(self.s_bd, 1)
        dve.wait_ge(self.s_bd, 2)

    def spread_bias(self, dve, h, slot):
        b = self.bq[self.HI, bass.ds(h, 1)].to_broadcast([HD, TP])
        dve.tensor_scalar(self.qb[slot][self.HI, :], b, 1.0, None, ALU.mult).then_inc(self.qb_done, 1)


def stage_natural(g, heads):
    nc, io = g.nc, g.io
    kinds = [(ROW_K, "k"), (ROW_V, "v"), (ROW_VG, "vg")]
    steps = [(a, tt) for a in range(3) for tt in range(NT + 1)]
    NB = 6
    with ExitStack() as ctx:
        src = [g.sb(f"nat_src{i}", [P, 4, T], ctx=ctx) for i in range(2)]
        assert SB == GH * GV
        knat = g.sb("nat_k", [P, NT + 1, SB], ctx=ctx)
        dst = [knat, g.vnat, knat]
        stores = [(io[n + "_prompt"].rearrange("l b (n p) h d -> p (l b n) (h d)", p=P),
                   io[n + "_sample"].rearrange("l s t h d -> (l s t) (h d)")) for n in ("k", "v")]
        stores += [(g.vgnat[0:TP].rearrange("(n p) c -> p n c", p=P), g.vgnat[TP:T])]
        s_src = [g.sem(f"nat_src{i}_loaded") for i in range(3)]
        s_tr = g.sem("nat_transposed")
        s_act = g.sem("nat_act_copied")
        s_dve = g.sem("nat_dve_copied")
        s_out = [g.sem(f"nat_{n}_stored") for _, n in kinds]
        s_oh = g.sem("nat_sample_hi")
        with nc.Block() as block:
            @block.sync
            def _(sp):
                for a, (row, _) in enumerate(kinds):
                    if a == 2:
                        heads.load_bias(sp)
                        heads.load(sp, 0, 0)
                        sp.wait_ge(s_tr, NT + 1)
                    sp.dma_start(src[a % 2][:], g.projT[row:row + SB, :].rearrange("(m p) t -> p m t", p=P)).then_inc(s_src[a], 16)
                heads.load(sp, 1, 1)
                for a, outs in enumerate(stores):
                    n = (a + 1) * (NT + 1)
                    sp.wait_ge(s_act, (n + 1) // 2)
                    sp.wait_ge(s_dve, n // 2)
                    sp.dma_start(outs[0], dst[a][:, 0:NT, :]).then_inc(s_out[a], 16)
                    sp.dma_start(outs[1], dst[a][0:TS, NT, :]).then_inc(s_out[a], 16)
                for done in s_out:
                    sp.wait_ge(done, 32)

            @block.gpsimd
            def _(pool):
                heads.set_kb(pool)
                heads.pool_part(pool, 0, 0)

            @block.tensor
            def _(pe):
                for j, (a, tt) in enumerate(steps):
                    m = P if tt < NT else TS
                    if tt == 0:
                        pe.wait_ge(s_src[a], 16)
                    if j >= NB:
                        pe.wait_ge(s_dve if j % 2 else s_act, (j - NB) // 2 + 1)
                    for f in range(4):
                        last = pe.transpose(g.bank[j % NB][0:m, f * P:(f + 1) * P], src[a % 2][:, f, tt * P:tt * P + m], g.ident[:])
                    last.then_inc(s_tr, 1)

            def copies(eng, copy, s_done, mine, between):
                for j, (a, tt) in enumerate(steps):
                    between(j)
                    if j % 2 == mine:
                        m = P if tt < NT else TS
                        eng.wait_ge(s_tr, j + 1)
                        if a == 2:
                            eng.wait_ge(s_out[0], 32)
                        copy(dst[a][0:m, tt, :], g.bank[j % NB][0:m, :]).then_inc(s_done, 1)

            @block.scalar
            def _(act):
                def between(j):
                    if j in (12, 16):
                        heads.act_part(act, 0, 0, (j - 12) // 4)

                copies(act, act.copy, s_act, 0, between)

            @block.vector
            def _(dve):
                def between(j):
                    if j == 12:
                        heads.split_bias(dve)
                        heads.spread_bias(dve, 0, 0)

                copies(dve, dve.tensor_copy, s_dve, 1, between)
                o = g.sample_o[:].rearrange("d p s q -> d p (s q)")
                dve.tensor_copy(g.op_hi[:, 0:4, TP:T], o).then_inc(s_oh, 1)
                dve.wait_ge(s_oh, 1)
                dve.tensor_tensor(g.op_lo[:, 0:4, TP:T], o, g.op_hi[:, 0:4, TP:T], ALU.subtract)


def stage_project_gla_and_sample_attention(g):
    nc, io = g.nc, g.io
    w_in = io["w_in"][0]
    NTILE = (ROW_A - ROW_QG) // P
    PER = NTILE // (NSEQ // 2)
    assert PER == 3 and NTILE % PER == 0
    DENSE = [[[(0, 0), (0, 1)], [(0, 2), (1, 0)]], [[(1, 1), (1, 2)], [(2, 0), (2, 1), (2, 2)]]]
    NCOL = HEADS * NEW
    with ExitStack() as ctx:
        sb = lambda *a: g.sb(*a, ctx=ctx)
        kpg = [sb(f"sa_k{i}", [P, NPAGE, SB]) for i in range(2)]
        vpg = sb("sa_v", [P, NPAGE, SB])
        kT = sb("sa_kT", [P, 4, 4, P])
        raw = [sb(f"pg_raw{i}", [P, KD, P]) for i in range(PER)]
        whi = [sb(f"pg_hi{i}", [P, KD, P], F32R) for i in range(PER)]
        wlo = [sb(f"pg_lo{i}", [P, KD, P], F32R) for i in range(PER)]
        stg = [sb(f"pg_stage{i}", [P, T]) for i in range(PER)]
        vnewT = sb("sa_vnewT", [P, 4, TS])
        vnew = sb("sa_vnew", [TS, SB])
        qnew = sb("sa_qnew", [P, 4, TS])
        knew = sb("sa_knew", [P, 4, TS])
        qbd = sb("sa_qbd", [P, 4, NSEQ, 2, NEW])
        table = ctx.enter_context(nc.sbuf_tensor("sa_table", [1, NSEQ * NPAGE], mybir.dt.int32))
        bsb = sb("sa_bsb", [33, HEADS])
        brow = sb("sa_brow", [33, NPAGE, HEADS, NEW], F32R)
        ones = sb("sa_ones", [33, P], F32R)
        negtri = sb("sa_negtri", [P, P])
        negone = sb("sa_negone", [P, P])
        mask16 = sb("sa_mask16", [TS, NSEQ, HEADS, NEW], BF16)
        spn = sb("sa_spn", [P, NSEQ, NCOL])
        wn = sb("sa_wn", [TS, NSEQ, NCOL])
        a = sb("sa_a", [P, 512])
        sp_ = sb("sa_sp", [P, NPAGE, NCOL])
        r = sb("sa_r", [P, NPAGE, NCOL])
        w = [sb(f"sa_w{i}", [P, 512]) for i in range(2)]
        o = g.sample_o
        s_in = g.sem("sa_inputs_loaded")
        s_tab = g.sem("sa_table_loaded")
        s_k = [g.sem(f"sa_k{i}_loaded") for i in range(2)]
        s_v = g.sem("sa_v_loaded")
        s_vn = g.sem("sa_new_v_transposed")
        s_raw = [g.sem(f"pg_raw{i}_loaded") for i in range(PER)]
        s_hi = g.sem("pg_hi_done")
        s_lo = g.sem("pg_lo_done")
        s_mm = g.sem("pg_chunk_summed")
        s_ev = g.sem("pg_chunk_evacuated")
        s_st = [g.sem(f"pg_stage{i}_stored") for i in range(PER)]
        s_c = g.sem("sa_constants")
        s_cd = g.sem("sa_dve_constants")
        s_kt = g.sem("sa_k_transposed")
        s_kta = g.sem("sa_kT_act_copied")
        s_ktd = g.sem("sa_kT_dve_copied")
        s_qk = g.sem("sa_scored")
        s_zn = g.sem("sa_new_scored")
        s_act = g.sem("sa_act_chain")
        s_sp = g.sem("sa_softplus")
        s_r = g.sem("sa_later_pages_summed")
        s_sum = g.sem("sa_stay_subtracted")
        s_w = g.sem("sa_weights")
        s_pv = g.sem("sa_v_multiplied")
        s_o = g.sem("sa_out")
        O, ZN = g.bank[6], g.bank[7]
        Z = [g.bank[4], g.bank[5]]
        TB = g.bank[0:2]
        DB = [g.bank[2], g.bank[3], g.bank[7]]

        def load_pages(eng, cache, pages, s, sem):
            pool_rows = cache[0].rearrange("n p h d -> n p (h d)")
            for j in range(NPAGE):
                page = eng.value_load(table[0:1, bass.ds(s * NPAGE + j, 1)], min_val=0, max_val=pool_rows.shape[0] - 1)
                eng.dma_start(pages[:, j, :], pool_rows[bass.ds(page, 1)].rearrange("o p d -> (o p) d")).then_inc(sem, 16)

        def pairs(body):
            def on(eng):
                body(0, True)
                with eng.Fori(1, NSEQ // 2 - 1) as n:
                    body(n, True)
                body(NSEQ // 2 - 1, False)
            return on

        with nc.Block() as block:
            @block.sync
            def _(sp):
                sp.dma_start(table[:], io["page_table"].rearrange("s (o n) -> o (s n)", o=1)).then_inc(s_tab, 16)
                for t, row in ((qnew, ROW_Q), (knew, ROW_K), (vnewT, ROW_V)):
                    sp.dma_start(t[:], g.projT[row:row + SB, TP:T].rearrange("(m p) t -> p m t", p=P)).then_inc(s_in, 16)
                sp.dma_start(bsb[:], io["b_sb"].to_broadcast([33, HEADS])).then_inc(s_in, 16)
                sp.wait_ge(s_tab, 16)

                def k_pages(s, slot):
                    at_least(sp, s_kt, (s - 2) * NPAGE + NPAGE)
                    load_pages(sp, io["cache_k"], kpg[slot], s, s_k[slot])

                def weights(i, m):
                    at_least(sp, s_lo, i - PER + 1)
                    sp.dma_start(raw[m][:], w_in[:, bass.ds(ROW_QG + i * P, P)].rearrange("(k p) c -> p k c", p=P)).then_inc(s_raw[m], 16)

                def body(n, more):
                    k_pages(2 * n + 1, 1)
                    if more:
                        for m in range(PER):
                            weights(PER * (n + 1) + m, m)
                        k_pages(2 * n + 2, 0)

                for m in range(PER):
                    weights(m, m)
                k_pages(0, 0)
                pairs(body)(sp)

            @block.gpsimd
            def _(pool):
                pool.memset(qbd[:], 0.0).then_inc(s_c, 1)
                pool.memset(spn[:], 0.0).then_inc(s_c, 1)
                pool.memset(ones[:].bitcast(F32), 1.0).then_inc(s_c, 1)
                pool.memset(brow[:].bitcast(F32), 0.0).then_inc(s_c, 1)
                pool.memset(negone[:], -1.0).then_inc(s_c, 1)
                pool.memset(negtri[:], -1.0).then_inc(s_c, 1)
                pool.memset(mask16[:], 0.0).then_inc(s_c, 1)
                pool.wait_ge(s_c, 7)
                pool.affine_select(out=negtri[:], in_=negtri[:], compare_op=ALU.is_ge, fill=0.0, base=0,
                                   pattern=[[-1, P]], channel_multiplier=1).then_inc(s_c, 1)
                pool.affine_select(out=mask16[:], in_=mask16[:], compare_op=ALU.is_ge, fill=NEG, base=0,
                                   pattern=[[-NEW, NSEQ], [0, HEADS], [0, NEW]], channel_multiplier=1).then_inc(s_c, 1)
                pool.wait_ge(s_c, 9)
                pool.affine_select(out=mask16[:], in_=mask16[:], compare_op=ALU.is_gt, fill=NEG, base=0,
                                   pattern=[[NEW, NSEQ], [0, HEADS], [1, NEW]], channel_multiplier=-1).then_inc(s_c, 1)
                pool.wait_ge(s_tab, 16)

                def v_pages(s):
                    at_least(pool, s_pv, s)
                    load_pages(pool, io["cache_v"], vpg, s, s_v)

                def low(n, m):
                    pool.wait_ge(s_hi, PER * n + m + 1)
                    pool.tensor_tensor(wlo[m][:], raw[m][:], whi[m][:], ALU.subtract).then_inc(s_lo, 1)

                def body(n, more):
                    low(n, 2)
                    v_pages(2 * n)
                    if more:
                        low(n + 1, 0)
                    v_pages(2 * n + 1)
                    if more:
                        low(n + 1, 1)

                low(0, 0)
                low(0, 1)
                pairs(body)(pool)

            @block.tensor
            def _(pe):
                pe.wait_ge(s_in, 64)
                for m in range(4):
                    last = pe.transpose(O[0:TS, m * P:(m + 1) * P], vnewT[:, m, :], g.ident[:])
                last.then_inc(s_vn, 1)
                pe.wait_ge(s_c, 10)
                pe.wait_ge(s_cd, 6)
                bias = brow[:].rearrange("o j h q -> o (j h q)")
                pe.matmul(ZN[0:TS, :], ones[:, 0:TS].bitcast(F32), bias.bitcast(F32), start=True, stop=False, skip_group_check=True)
                zn = ZN[0:TS, :].rearrange("k (s p c) -> k p s c", s=NSEQ, p=4)
                for p in range(4):
                    pe.matmul(zn[:, p], knew[:, p, :], qbd[:, p].rearrange("k s h q -> k s (h q)"),
                              start=False, stop=False, skip_group_check=True)
                pe.matmul(ZN[0:TS, :], g.ident16[0:TS, 0:TS], mask16[:].rearrange("p s h q -> p (s h q)"),
                          start=False, stop=True, skip_group_check=True).then_inc(s_zn, 1)
                pe.wait_ge(s_sp, 1)
                pe.matmul(ZN[0:TS, :], negtri[0:TS, 0:TS], spn[0:TS].rearrange("k s c -> k (s c)"),
                          start=False, stop=True, skip_group_check=True).then_inc(s_zn, 1)
                pe.wait_ge(s_w, 1)
                ov = O[:].rearrange("d (s p c) -> d p s c", s=NSEQ, p=4)
                wv = wn[:].rearrange("k s (p c) -> k p s c", p=4)
                for p in range(4):
                    pe.matmul(ov[:, p], vnew[:, p * P:(p + 1) * P], wv[:, p],
                              start=(p == 0), stop=False, skip_group_check=True)

                def score(n, slot, between):
                    s = 2 * n + slot
                    at_least(pe, s_w, s)
                    pe.wait_ge(s_k[slot], n * 128 + 128)
                    pe.matmul(Z[slot][:], ones[:], bias, start=True, stop=False, skip_group_check=True)
                    for j in range(NPAGE + 1):
                        if j < NPAGE:
                            at_least(pe, s_ktd if j % 2 else s_kta, s * 4 + j // 2)
                            for p in range(4):
                                last = pe.transpose(TB[j % 2][:, p * P:(p + 1) * P], kpg[slot][:, j, p * P:(p + 1) * P], g.ident[:])
                            last.then_inc(s_kt, 1)
                            pieces(between, 2)
                        if j > 0:
                            i = j - 1
                            pe.wait_ge(s_ktd if i % 2 else s_kta, s * 4 + i // 2 + 1)
                            for p in range(4):
                                c = i * NCOL + p * 16
                                q = qbd[:, p].rearrange("k s h q -> k (s h q)")
                                last = pe.matmul(Z[slot][:, c:c + 16], kT[:, i % 4, p, :], q[:, bass.ds(s * 16, 16)],
                                                 start=False, stop=(i == NPAGE - 1), skip_group_check=True)
                            last.then_inc(s_qk, 1)

                def subtract(s, slot):
                    pe.wait_ge(s_r, s * 8 + 8)
                    pe.matmul(Z[slot][:], negtri[:], sp_[:].rearrange("k j c -> k (j c)"), start=False, stop=False, skip_group_check=True)
                    pe.matmul(Z[slot][:], negone[:], r[:].rearrange("k j c -> k (j c)"), start=False, stop=True,
                              skip_group_check=True).then_inc(s_sum, 1)

                def values(s, slot, between):
                    pe.wait_ge(s_w, s + 2)
                    pe.wait_ge(s_v, s * 128 + 128)
                    for j in range(NPAGE):
                        for p in range(4):
                            c = j * NCOL + p * 16
                            last = pe.matmul(O[:, bass.ds(s * NCOL + p * 16, 16)], vpg[:, j, p * P:(p + 1) * P],
                                             w[slot][:, c:c + 16], start=False, stop=(j == NPAGE - 1), skip_group_check=True)
                        pieces(between, 3)
                    last.then_inc(s_pv, 1)

                def pieces(of, count):
                    for _ in range(count):
                        next(of, None)

                def dense(n, chunks):
                    for m, c in chunks:
                        i = PER * n + m
                        t0, tw = CHUNKS[c]
                        if c == 0:
                            pe.wait_ge(s_lo, i + 1)
                        at_least(pe, s_ev, 3 * i + c - 2)
                        for k in range(KD):
                            last = three_products(pe, DB[c][:, 0:tw], whi[m][:, k, :], wlo[m][:, k, :],
                                                  g.op_hi[:, k, t0:t0 + tw], g.op_lo[:, k, t0:t0 + tw], k, KD)
                            if k == KD - 1:
                                last.then_inc(s_mm, 1)
                            yield

                def body(n, more):
                    for slot in range(2):
                        s = 2 * n + slot
                        score(n, slot, dense(n, DENSE[slot][0]))
                        chunks = dense(n, DENSE[slot][1])
                        if not isinstance(s, int) or s > 0:
                            values(s - 1, 1 - slot, chunks)
                        pieces(chunks, 3 * KD)
                        subtract(s, slot)

                pairs(body)(pe)
                values(NSEQ - 1, 1, iter(()))

            @block.scalar
            def _(act):
                def chain(z, out, i):
                    act.activation(out, z, ACT.Abs).then_inc(s_act, 1)
                    act.wait_ge(s_act, i * 3 + 1)
                    act.activation(out, out, ACT.Exp, scale=-1.0).then_inc(s_act, 1)
                    act.wait_ge(s_act, i * 3 + 2)
                    act.activation(out, out, ACT.Ln, bias=1.0).then_inc(s_act, 1)

                act.wait_ge(s_zn, 1)
                chain(ZN[0:TS, :], a[0:TS, :], 0)
                act.wait_ge(s_zn, 2)
                act.activation(wn[:].rearrange("k s c -> k (s c)"), ZN[0:TS, :], ACT.Exp).then_inc(s_w, 1)

                def stay(s, slot):
                    for j in range(0, NPAGE, 2):
                        act.wait_ge(s_kt, s * NPAGE + j + 1)
                        at_least(act, s_qk, s * NPAGE + j - 3)
                        act.copy(kT[:, j % 4].rearrange("k p c -> k (p c)"), TB[0][:]).then_inc(s_kta, 1)
                    act.wait_ge(s_qk, s * NPAGE + NPAGE)
                    act.wait_ge(s_sp, s + 1)
                    chain(Z[slot][:], a[:], s + 1)

                def weights(s, slot):
                    at_least(act, s_pv, s - 1)
                    act.wait_ge(s_sum, s + 1)
                    act.activation(w[slot][:], Z[slot][:], ACT.Exp).then_inc(s_w, 1)

                def high(n, m):
                    i = PER * n + m
                    act.wait_ge(s_raw[m], n * 16 + 16)
                    at_least(act, s_mm, 3 * (i - PER) + 3)
                    act.copy(whi[m][:], raw[m][:]).then_inc(s_hi, 1)

                def store(n, m):
                    act.wait_ge(s_ev, 3 * (PER * n + m) + 3)
                    act.dma_start(g.projT[bass.ds(ROW_QG + (PER * n + m) * P, P), :], stg[m][:]).then_inc(s_st[m], 16)

                def body(n, more):
                    stay(2 * n, 0)
                    high(n, 2)
                    weights(2 * n, 0)
                    store(n, 0)
                    stay(2 * n + 1, 1)
                    if more:
                        high(n + 1, 0)
                    weights(2 * n + 1, 1)
                    if more:
                        high(n + 1, 1)
                    store(n, 1)
                    store(n, 2)

                high(0, 0)
                high(0, 1)
                pairs(body)(act)
                for m in range(PER):
                    act.wait_ge(s_st[m], 16 * (NSEQ // 2))

            @block.vector
            def _(dve):
                dve.wait_ge(s_vn, 1)
                dve.tensor_copy(vnew[:], O[0:TS, :]).then_inc(s_cd, 1)
                dve.wait_ge(s_in, 64)
                dve.wait_ge(s_c, 7)
                b = bsb[:].rearrange("o (j h q) -> o j h q", j=1, q=1).to_broadcast([33, NPAGE, HEADS, NEW])
                for row in (slice(0, 1), slice(32, 33)):
                    dve.tensor_copy(brow[row], b[row]).then_inc(s_cd, 1)
                dve.wait_ge(s_cd, 3)
                dve.tensor_tensor(brow[32:33], b[32:33], brow[32:33], ALU.subtract).then_inc(s_cd, 1)
                for h in range(2):
                    rows = slice(h * HD, (h + 1) * HD)
                    src = qnew[rows].rearrange("k p (s q) -> k p s q", s=NSEQ)
                    dve.tensor_scalar(qbd[rows, :, :, h, :], src, HD ** -0.5, None, ALU.mult).then_inc(s_cd, 1)
                dve.wait_ge(s_act, 3)
                dve.scalar_tensor_tensor(out=spn[0:TS].rearrange("k s c -> k (s c)"), in0=ZN[0:TS, :], scalar=0.0,
                                         in1=a[0:TS, :], op0=ALU.max, op1=ALU.add).then_inc(s_sp, 1)

                def step(s, slot):
                    for j in range(1, NPAGE, 2):
                        dve.wait_ge(s_kt, s * NPAGE + j + 1)
                        at_least(dve, s_qk, s * NPAGE + j - 3)
                        dve.tensor_copy(kT[:, j % 4].rearrange("k p c -> k (p c)"), TB[1][:]).then_inc(s_ktd, 1)
                    dve.wait_ge(s_act, (s + 1) * 3 + 3)
                    at_least(dve, s_sum, s)
                    dve.scalar_tensor_tensor(out=sp_[:].rearrange("k j c -> k (j c)"), in0=Z[slot][:], scalar=0.0,
                                             in1=a[:], op0=ALU.max, op1=ALU.add).then_inc(s_sp, 1)
                    spn_s = spn[:].rearrange("k s c -> k (s c)")[:, bass.ds(s * NCOL, NCOL)]
                    dve.tensor_copy(r[:, NPAGE - 1, :], spn_s).then_inc(s_r, 1)
                    dve.wait_ge(s_sp, s + 2)
                    for j in range(NPAGE - 2, -1, -1):
                        dve.wait_ge(s_r, s * 8 + NPAGE - 1 - j)
                        dve.tensor_tensor(r[:, j, :], r[:, j + 1, :], sp_[:, j + 1, :], ALU.add).then_inc(s_r, 1)

                def evacuate(n, chunks):
                    for m, c in chunks:
                        t0, tw = CHUNKS[c]
                        dve.wait_ge(s_mm, 3 * (PER * n + m) + c + 1)
                        at_least(dve, s_st[m], n * 16)
                        dve.tensor_copy(stg[m][:, t0:t0 + tw], DB[c][:, 0:tw]).then_inc(s_ev, 1)

                def body(n, more):
                    for slot in range(2):
                        step(2 * n + slot, slot)
                        evacuate(n, DENSE[slot][0])
                        evacuate(n, DENSE[slot][1])

                pairs(body)(dve)
                dve.wait_ge(s_pv, NSEQ)
                for h in range(2):
                    rows = slice(h * HD, (h + 1) * HD)
                    src = O[rows, :].rearrange("d (s p h q) -> d p s h q", s=NSEQ, p=4, h=2)[:, :, :, h, :]
                    dve.tensor_copy(o[rows], src).then_inc(s_o, 1)


def stage_prompt_attention(g, ops):
    nc, io = g.nc, g.io
    HALF = slice(0, HD), slice(HD, P)
    TILES = 4
    steps = []
    for i in range(NT):
        c, w = i // TILES, (i + 1) * P
        if w > 512:
            steps.append((c, i, 512, w - 512))
        steps.append((c, i, 0, min(w, 512)))
    NS, NU = len(steps), 3 * TILES
    NZ = 4
    with ExitStack() as ctx:
        sb = lambda *a: g.sb(*a, ctx=ctx)
        vhl = [sb(f"pa_vhl{i}", [P, NT, P], F32R) for i in range(2)]
        a = [sb(f"pa_a{i}", [P, 512]) for i in range(NZ)]
        s = [sb(f"pa_s{i}", [P, 512]) for i in range(NZ)]
        w = [sb(f"pa_w{c}", [P, TILES, 512 * (c + 1)]) for c in range(2)]
        wth = [sb(f"pa_wth{i}", [P, 512], F32R) for i in range(2)]
        wtl = [sb(f"pa_wtl{i}", [P, 512], F32R) for i in range(2)]
        ot = [sb(f"pa_ot{i}", [P, 512]) for i in range(2)]
        s_vhl = g.sem("pa_v_split")
        s_z = g.sem("pa_scored")
        s_a = g.sem("pa_act_chain")
        s_sp = g.sem("pa_softplus")
        s_sc = g.sem("pa_scanned")
        s_x = g.sem("pa_log_weight")
        s_w = g.sem("pa_weight")
        s_tp = g.sem("pa_transposed")
        s_hi = g.sem("pa_wT_hi")
        s_lo = g.sem("pa_wT_lo")
        s_pv = g.sem("pa_v_multiplied")
        s_oa = g.sem("pa_out_half")
        s_o = g.sem("pa_out_summed")
        s_oh = g.sem("pa_out_hi")
        Z, TB, O = g.bank[0:4], g.bank[4:6], g.bank[6:8]

        NG = 4
        group_steps = [[[k] for k in range(TILES)], [[TILES + 2 * k, TILES + 2 * k + 1] for k in range(NG)]]
        group_blocks = [[[], [(1, 0), (1, 1)], [(1, 2), (1, 3)], [(1, 4)]],
                        [[(1, 5), (1, 6)], [(1, 7), (0, 0)], [(0, 1), (0, 2)], [(0, 3)]]]
        last_step = [group_steps[c][-1][-1] for c in range(2)]

        def heads(eng, group, prep, finish):
            def before(n, slot):
                return (n, 0) if slot else (n - 1, 1)

            def head(n, slot, first, more):
                for c in range(2):
                    for k in range(NG):
                        group((n, slot), c, k, blocks(n, slot, c, k, first), True, None if first else before(n, slot))
                        if not first and k == 2:
                            finish(*before(n, slot), c)
                        if more and c:
                            prep(2 * n + slot + 1, 1 - slot, k)

            def blocks(n, slot, c, k, first):
                return [(*((n, slot) if half == 0 else before(n, slot)), half, j) for half, j in group_blocks[c][k]
                        if half == 0 or not first]

            for k in range(NG):
                prep(0, 0, k)
            head(0, 0, True, True)
            head(0, 1, False, True)
            with eng.Fori(1, HEADS // 2 - 1) as n:
                head(n, 0, False, True)
                head(n, 1, False, True)
            n = HEADS // 2 - 1
            head(n, 0, False, True)
            head(n, 1, False, False)
            for c, k in ((0, 0), (0, 1), (0, 2), (0, 3), (1, 0), (1, 1)):
                group((n + 1, 0), c, k, [b for b in blocks(n + 1, 0, c, k, False) if b[2] == 1], False, (n, 1))
                if (c, k) == (0, 2):
                    finish(n, 1, 0)
            finish(n, 1, 1)

        def nothing(*_):
            pass

        def made(h):
            return isinstance(h, int) and h == 0

        with nc.Block() as block:
            @block.sync
            def _(sp):
                def load(h, slot, k):
                    if k == 0 and not (isinstance(h, int) and h < 2):
                        ops.load(sp, h, slot)

                heads(sp, nothing, load, nothing)

            @block.gpsimd
            def _(pool):
                def prep(h, slot, k):
                    if k == 0 and not made(h):
                        ops.pool_part(pool, h, slot)

                heads(pool, nothing, prep, nothing)

            @block.tensor
            def _(pe):
                pe.wait_ge(ops.kb_set, 2)

                def score(n, slot, t):
                    h = 2 * n + slot
                    _, i, k0, kw = steps[t]
                    z = Z[t % NZ][:, 0:kw]
                    q = slice(i * P, (i + 1) * P)
                    if t == 0:
                        pe.wait_ge(ops.act_done, 4 * h + 4)
                        pe.wait_ge(ops.pool_done, 3 * h + 3)
                        pe.wait_ge(ops.qb_done, h + 1)
                    at_least(pe, s_x, h * NS + t - NZ + 1)
                    diagonal = k0 + kw == (i + 1) * P
                    pe.matmul(z, ops.qa[slot][:, q], ops.ka[slot][:, k0:k0 + kw], start=True, stop=False)
                    last = pe.matmul(z, ops.qb[slot][:, q], ops.kb[slot][:, k0:k0 + kw], start=False, stop=not diagonal)
                    if diagonal:
                        last = pe.matmul(z[:, kw - P:kw], g.ident16[:], g.causal16[:], start=False, stop=True)
                    last.then_inc(s_z, 1)

                def transpose(n, slot, c, j):
                    h, u = 2 * n + slot, c * TILES + j
                    if j == 0:
                        pe.wait_ge(s_w, h * NS + last_step[c] + 1)
                    at_least(pe, s_lo, h * NU + u - 1)
                    for i in range(max(0, j - c * TILES), TILES):
                        last = pe.transpose(TB[u % 2][:, i * P:(i + 1) * P], w[c][:, i, j * P:(j + 1) * P], g.ident[:])
                    last.then_inc(s_tp, 1)

                def multiply(n, slot, c, j):
                    h, u = 2 * n + slot, c * TILES + j
                    cols = slice(max(0, j - c * TILES) * P, 512)
                    if j == 0:
                        at_least(pe, s_o, 2 * h + c - 1)
                        pe.wait_ge(s_vhl, 2 * h + 2)
                    pe.wait_ge(s_lo, h * NU + u + 1)
                    pe.matmul(O[c][:, cols], vhl[slot][:, j, :], wth[u % 2][:, cols], start=(j == 0), stop=False)
                    pe.matmul(O[c][:, cols], vhl[slot][:, j, :], wtl[u % 2][:, cols], start=False,
                              stop=(j == TILES * (c + 1) - 1)).then_inc(s_pv, 1)

                def group(head, c, k, blocks, scores, prev):
                    if scores:
                        for t in group_steps[c][k]:
                            score(*head, t)
                    for n, slot, half, j in blocks:
                        transpose(n, slot, half, j)
                        if j > 0:
                            multiply(n, slot, half, j - 1)
                            if half == 1 and j == 2 * TILES - 1 and not scores:
                                multiply(n, slot, half, j)
                        elif half == 1:
                            multiply(n, slot, 0, TILES - 1)
                        elif slot:
                            multiply(n, 0, 1, 2 * TILES - 1)
                        elif not isinstance(n, int) or n > 0:
                            multiply(n - 1, 1, 1, 2 * TILES - 1)

                heads(pe, group, nothing, nothing)

            @block.scalar
            def _(act):
                def prep(h, slot, k):
                    if not made(h):
                        ops.act_part(act, h, slot, k, s_z, NS)

                def weights(n, slot, c, k):
                    h = 2 * n + slot
                    for t in group_steps[c][k]:
                        _, i, k0, kw = steps[t]
                        act.wait_ge(s_x, h * NS + t + 1)
                        at_least(act, s_tp, (h - 1) * NU + c * TILES + i + 1)
                        act.activation(w[c][:, i % TILES, k0:k0 + kw], a[t % NZ][:, 0:kw], ACT.Exp).then_inc(s_w, 1)

                def high(n, slot, c, j):
                    h, u = 2 * n + slot, c * TILES + j
                    cols = slice(max(0, j - c * TILES) * P, 512)
                    act.wait_ge(s_tp, h * NU + u + 1)
                    at_least(act, s_pv, h * NU + u - 1)
                    act.copy(wth[u % 2][:, cols], TB[u % 2][:, cols]).then_inc(s_hi, 1)

                def group(head, c, k, blocks, scores, prev):
                    n, slot = head
                    h = 2 * n + slot
                    ts = group_steps[c][k]
                    m, base = len(ts), (h * NS + ts[0]) * 3
                    if scores:
                        for t in ts:
                            at_least(act, s_w, h * NS + t - NZ + 1)
                            act.wait_ge(s_z, h * NS + t + 1)
                            act.activation(a[t % NZ][:, 0:steps[t][3]], Z[t % NZ][:, 0:steps[t][3]], ACT.Abs).then_inc(s_a, 1)
                    if blocks:
                        high(*blocks[0])
                    if scores:
                        for x, t in enumerate(ts):
                            out = a[t % NZ][:, 0:steps[t][3]]
                            act.wait_ge(s_a, base + x + 1)
                            act.activation(out, out, ACT.Exp, scale=-1.0).then_inc(s_a, 1)
                    if len(blocks) > 1:
                        high(*blocks[1])
                    if scores:
                        for x, t in enumerate(ts):
                            out = a[t % NZ][:, 0:steps[t][3]]
                            act.wait_ge(s_a, base + m + x + 1)
                            act.activation(out, out, ACT.Ln, bias=1.0).then_inc(s_a, 1)
                        if k > 0:
                            weights(n, slot, c, k - 1)
                        elif c == 1:
                            weights(n, slot, 0, NG - 1)
                    if c == 0 and k == 0 and prev:
                        weights(*prev, 1, NG - 1)

                def finish(n, slot, c):
                    h = 2 * n + slot
                    act.wait_ge(s_pv, h * NU + c * TILES + TILES * (c + 1))
                    at_least(act, s_oh, 2 * h + c - 1)
                    act.copy(ot[c][HALF[slot], :], O[c][HALF[1 - slot], :]).then_inc(s_oa, 1)

                heads(act, group, prep, finish)

            @block.vector
            def _(dve):
                def prep(h, slot, k):
                    v = g.vnat[:, 0:NT, bass.ds(h * HD, HD)]
                    if k == 0 and not made(h):
                        at_least(dve, s_z, (h - 1) * NS)
                        ops.spread_bias(dve, h, slot)
                    elif k == 2:
                        at_least(dve, s_pv, (h - 2) * NU + NU)
                        dve.tensor_scalar(vhl[slot][:, :, 0:HD], v, 1.0, None, ALU.mult).then_inc(s_vhl, 1)
                    elif k == 3:
                        dve.wait_ge(s_vhl, 2 * h + 1)
                        dve.tensor_tensor(vhl[slot][:, :, HD:P], v, vhl[slot][:, :, 0:HD], ALU.subtract).then_inc(s_vhl, 1)

                def low(n, slot, c, j):
                    h, u = 2 * n + slot, c * TILES + j
                    cols = slice(max(0, j - c * TILES) * P, 512)
                    dve.wait_ge(s_hi, h * NU + u + 1)
                    dve.tensor_tensor(wtl[u % 2][:, cols], TB[u % 2][:, cols], wth[u % 2][:, cols], ALU.subtract).then_inc(s_lo, 1)

                def group(head, c, k, blocks, scores, prev):
                    n, slot = head
                    h = 2 * n + slot
                    ts = group_steps[c][k] if scores else []
                    part = lambda b, t: b[t % NZ][:, 0:steps[t][3]]
                    if blocks:
                        low(*blocks[0])
                    for x, t in enumerate(ts):
                        dve.wait_ge(s_a, (h * NS + ts[0]) * 3 + 2 * len(ts) + x + 1)
                        dve.scalar_tensor_tensor(out=part(a, t), in0=part(Z, t), scalar=0.0, in1=part(a, t), op0=ALU.max,
                                                 op1=ALU.add).then_inc(s_sp, 1)
                    if len(blocks) > 1:
                        low(*blocks[1])
                    for t in ts:
                        _, i, k0, kw = steps[t]
                        dve.wait_ge(s_sp, h * NS + t + 1)
                        later = 0.0
                        if i >= TILES and k0 == 0:
                            dve.wait_ge(s_sc, h * NS + t)
                            later = s[(t - 1) % NZ][:, 0:1]
                        dve.tensor_tensor_scan(part(s, t)[:, ::-1], part(a, t)[:, ::-1], part(a, t)[:, ::-1], later, ALU.add,
                                               ALU.max).then_inc(s_sc, 1)
                    for t in ts:
                        dve.wait_ge(s_sc, h * NS + t + 1)
                        dve.tensor_tensor(part(a, t), part(Z, t), part(s, t), ALU.subtract).then_inc(s_x, 1)

                def finish(n, slot, c):
                    rows, G = HALF[slot], 2 * (2 * n + slot) + c
                    dve.wait_ge(s_oa, G + 1)
                    dve.tensor_tensor(ot[c][rows, :], ot[c][rows, :], O[c][rows, :], ALU.add).then_inc(s_o, 1)
                    hi, lo = (m[rows, bass.ds(n, 1), c * 512:(c + 1) * 512].rearrange("d o t -> d (o t)") for m in (g.op_hi, g.op_lo))
                    dve.wait_ge(s_o, G + 1)
                    dve.tensor_scalar(hi, ot[c][rows, :], 1.0, None, ALU.mult).then_inc(s_oh, 1)
                    dve.wait_ge(s_oh, G + 1)
                    dve.tensor_tensor(lo, ot[c][rows, :], hi, ALU.subtract)

                heads(dve, group, prep, finish)


def stage_gla(g):
    nc, io = g.nc, g.io
    NSUB = P // SUB
    MID = SUB // 2 - 1
    QS = GK ** -0.5
    HALF = slice(0, GK), slice(GK, P)
    with ExitStack() as ctx:
        sb = lambda *a: g.sb(*a, ctx=ctx)
        q = sb("gl_q", [P, 2, T])
        k = sb("gl_k", [P, 2, T])
        rg = [sb(f"gl_r{i}", [P, GH, P]) for i in range(3)]
        sr = [sb(f"gl_silu{i}", [P, GH, P]) for i in range(2)]
        v = [sb(f"gl_v{i}", [P, GH * GV]) for i in range(3)]
        al = sb("gl_alow", [RANK, T])
        wg = sb("gl_wgate", [RANK, GH * GK])
        negb = sb("gl_negb", [P, 2])
        bc = sb("gl_bc", [P, 2, T])
        nx = sb("gl_nx", [P, 2, T])
        kend = sb("gl_kend", [P, 2, T])
        reset = kend[:, 0, :]
        eb = [sb(f"gl_eb{i}", [P, 2, P]) for i in range(2)]
        qdec = [sb(f"gl_qdec{i}", [P, 2, P]) for i in range(2)]
        qi = [sb(f"gl_qi{i}", [P, 2, 2, P]) for i in range(2)]
        dec = sb("gl_dec", [P, 2, NT + NSEQ])
        ki = [sb(f"gl_ki{i}", [P, 2, NSUB, P]) for i in range(2)]
        kn = [sb(f"gl_kn{i}", [P, 2 * P]) for i in range(2)]
        pt = [sb(f"gl_pt{i}", [P, GH, P]) for i in range(2)]
        st = sb("gl_state", [P, GH, GV])
        on = [sb(f"gl_on{i}", [P, GH, GV]) for i in range(2)]
        fin = [sb(f"gl_fin{i}", [P, GH, P]) for i in range(2)]
        sq = sb("gl_sq", [P, GH, GV])
        rs = sb("gl_rstd", [P, NT + 1, GH])
        tri = sb("gl_tri", [P, P])
        tri8 = sb("gl_tri8", [TS, TS])
        rowm = sb("gl_rowmask", [TS, NSEQ])
        colm = sb("gl_colmask", [P, NSEQ, TS])
        kinv = sb("gl_kinv", [P, 2, TS])
        qs = sb("gl_qs", [P, 2, 2, TS])
        qm = sb("gl_qm", [P, 2, NSEQ, TS])
        kem = [sb(f"gl_kem{i}", [TS, 2 * P]) for i in range(2)]
        s0 = sb("gl_s0", [P, NSEQ, GH, GV])
        wa = [sb(f"ada2_w{i}", [P, 2, 512]) for i in range(2)]
        arow = sb("ada2_rows", [NMOD, 512])
        NADA = 4 * D // 512
        s_wa = [g.sem(f"ada2_w{i}_loaded") for i in range(2)]
        s_am = g.sem("ada2_quarter_summed")
        s_ar = g.sem("ada2_rows_copied")
        s_at = g.sem("ada2_rows_transposed")
        s_ae = g.sem("ada2_mod_done")
        s_gin = g.sem("gl_gate_inputs_loaded")
        s_k = g.sem("gl_k_loaded")
        s_q = g.sem("gl_q_loaded")
        s_r = [g.sem(f"gl_r{i}_loaded") for i in range(3)]
        s_s0 = g.sem("gl_s0_loaded")
        s_c = g.sem("gl_constants")
        s_z = g.sem("gl_zeroed")
        s_nb = g.sem("gl_negb_done")
        s_gate = g.sem("gl_gate_product")
        s_a = g.sem("gl_act_pre")
        s_d = g.sem("gl_dve_pre")
        s_E = g.sem("gl_ki_exp")
        s_D = g.sem("gl_ki_diff")
        s_ki = g.sem("gl_ki_done")
        s_kt = g.sem("gl_kend_transposed")
        s_kn = g.sem("gl_kn_copied")
        s_sc = g.sem("gl_scored")
        s_cl = g.sem("gl_clamped")
        s_pt = g.sem("gl_masked")
        s_oo = g.sem("gl_o")
        s_ds = g.sem("gl_ds")
        s_st = g.sem("gl_state_updated")
        s_sq = g.sem("gl_squares")
        s_rl = g.sem("gl_rstd_ln")
        s_rs = g.sem("gl_rstd_done")
        s_on = g.sem("gl_on_done")
        s_ot = g.sem("gl_on_transposed")
        s_fin = g.sem("gl_fin_done")
        s_fh = g.sem("gl_fin_hi")
        s_fl = g.sem("gl_fin_lo")
        s_out = g.sem("gl_stored")
        s_v = [g.sem(f"gl_v{i}_loaded") for i in range(3)]
        s_eb = g.sem("gl_exp_bc")
        s_qd = g.sem("gl_qdec_done")
        s_se = g.sem("gl_silu_act")
        s_sd = g.sem("gl_silu_exponent")
        s_sm = g.sem("gl_silu_done")
        s_km = g.sem("gl_kem_done")
        s_x = g.sem("gl_sample_dve")
        s_xp = g.sem("gl_sample_pe")
        KT, SC, OB, DS, OT, ADA = g.bank[0], g.bank[1:3], g.bank[3:5], g.bank[5], g.bank[6], g.bank[7]
        N9 = NT + 1

        def tile(i):
            return slice(i * P, i * P + (P if i < NT else TS))

        with nc.Block() as block:
            @block.sync
            def _(sp):
                sp.dma_start(al[:], g.projT[ROW_A:IN_W, :]).then_inc(s_gin, 16)
                sp.dma_start(wg[:], io["w_gla_gate"][0]).then_inc(s_gin, 16)
                sp.dma_start(k[:], g.projT[ROW_KG:ROW_VG, :].rearrange("(m p) t -> p m t", p=P)).then_inc(s_k, 16)
                sp.dma_start(q[:], g.projT[ROW_QG:ROW_KG, :].rearrange("(m p) t -> p m t", p=P)).then_inc(s_q, 16)
                for i in range(2):
                    sp.dma_start(v[i][:], g.vgnat[tile(i)]).then_inc(s_v[i], 16)

                def load_r(i):
                    if i >= 3:
                        sp.wait_ge(s_fin, i - 2)
                    w = P if i < NT else TS
                    sp.dma_start(rg[i % 3][:, :, 0:w], g.projT[ROW_RG:ROW_A, tile(i)].rearrange("(m p) t -> p m t", p=P)).then_inc(s_r[i % 3], 16)

                def weights(i):
                    if i >= 2:
                        sp.wait_ge(s_am, i - 1)
                    chunk, m = divmod(i, 4)
                    part = io["w_ada"][0][m * 2 * P:(m + 1) * 2 * P, 2 * D + chunk * 512:2 * D + (chunk + 1) * 512]
                    sp.dma_start(wa[i % 2][:], part.rearrange("(k p) c -> p k c", p=P)).then_inc(s_wa[i % 2], 16)

                for i in range(2):
                    load_r(i)
                for i in range(10):
                    weights(i)
                sp.wait_ge(s_z, 4)
                s0d = io["state_gla"][0].rearrange("s (m h) k v -> h m k s v", h=2)
                for h in range(2):
                    for m in range(2):
                        sp.dma_start(s0[HALF[h], :, 2 * m + h, :], s0d[h, m]).then_inc(s_s0, 16)
                for i in range(2, N9):
                    if i >= 3:
                        sp.wait_ge(s_ds, i - 2)
                        sp.wait_ge(s_oo, i - 2)
                    sp.dma_start(v[i % 3][0:P if i < NT else TS, :], g.vgnat[tile(i)]).then_inc(s_v[i % 3], 16)
                    for t in range(4 * i + 2, min(4 * i + 6, 4 * NADA)):
                        weights(t)
                    load_r(i)
                sp.wait_ge(s_st, 4 * NT)
                outp = io["state_prompt"][0, 0].rearrange("(m h) k v -> h m k v", h=2)
                for h in range(2):
                    for m in range(2):
                        sp.dma_start(outp[h, m], st[HALF[h], 2 * m + h, :]).then_inc(s_out, 16)
                sp.wait_ge(s_x, 1 + 4 * NSEQ)
                outs = io["state_sample"][0].rearrange("s (m h) k v -> h m k s v", h=2)
                for h in range(2):
                    for m in range(2):
                        sp.dma_start(outs[h, m], s0[HALF[h], :, 2 * m + h, :]).then_inc(s_out, 16)
                sp.wait_ge(s_out, 8 * 16)

            @block.gpsimd
            def _(pool):
                pool.memset(st[:], 0.0).then_inc(s_z, 1)
                pool.memset(qi[0][:], 0.0).then_inc(s_z, 1)
                pool.memset(qi[1][:], 0.0).then_inc(s_z, 1)
                pool.memset(s0[:], 0.0).then_inc(s_z, 1)
                pool.memset(qs[:], 0.0).then_inc(s_z, 1)
                pool.memset(reset, 1.0).then_inc(s_c, 1)
                pool.memset(tri[:], 1.0).then_inc(s_c, 1)
                pool.memset(tri8[:], 1.0).then_inc(s_c, 1)
                pool.memset(rowm[:], 1.0).then_inc(s_c, 1)
                pool.memset(colm[:], 1.0).then_inc(s_c, 1)
                pool.wait_ge(s_c, 5)
                pool.memset(reset[:, 0:TP:P], 0.0).then_inc(s_c, 1)
                pool.memset(reset[:, TP:T:NEW], 0.0).then_inc(s_c, 1)

                def keep(out, pattern, base, mult):
                    pool.affine_select(out=out, in_=out, compare_op=ALU.is_ge, fill=0.0, base=base,
                                       pattern=pattern, channel_multiplier=mult).then_inc(s_c, 1)

                keep(tri[:], [[1, P]], 0, -1)
                t8 = tri8[:].rearrange("k (s q) -> k s q", s=NSEQ)
                keep(t8, [[NEW, NSEQ], [1, NEW]], 0, -1)
                keep(rowm[:], [[-NEW, NSEQ]], 0, 1)
                keep(colm[:], [[-NEW, NSEQ], [1, TS]], 0, 0)
                pool.wait_ge(s_c, 11)
                keep(t8, [[-NEW, NSEQ], [0, NEW]], 0, 1)
                keep(rowm[:], [[NEW, NSEQ]], NEW - 1, -1)
                keep(colm[:], [[NEW, NSEQ], [-1, TS]], NEW - 1, 0)
                for i in range(N9):
                    w = P if i < NT else TS
                    pool.wait_ge(s_fh, i + 1)
                    pool.tensor_tensor(g.op_lo[:, GH:2 * GH, tile(i)], fin[i % 2][:, :, 0:w],
                                       g.op_hi[:, GH:2 * GH, tile(i)], ALU.subtract).then_inc(s_fl, 1)

            @block.scalar
            def _(act):
                act.wait_ge(s_nb, 1)
                n = 0
                for m in range(2):
                    for c, (t0, tw) in enumerate(CHUNKS):
                        act.wait_ge(s_gate, 3 * m + c + 1)
                        act.activation(nx[:, m, t0:t0 + tw], g.bank[3 * m + c][:, 0:tw], ACT.Identity, scale=-1.0,
                                       bias=negb[:, m:m + 1]).then_inc(s_a, 1)
                act.wait_ge(s_a, 6)
                act.activation(bc[:], nx[:], ACT.Abs).then_inc(s_a, 1)
                act.wait_ge(s_a, 7)
                act.activation(bc[:], bc[:], ACT.Exp, scale=-1.0).then_inc(s_a, 1)
                act.wait_ge(s_a, 8)
                act.activation(bc[:], bc[:], ACT.Ln, bias=1.0).then_inc(s_a, 1)
                act.wait_ge(s_d, 3)
                act.activation(dec[:, :, 0:NT], bc[:, :, P - 1:TP:P], ACT.Exp, scale=-GATE)
                act.activation(dec[:, :, NT:], bc[:, :, TP + NEW - 1:T:NEW], ACT.Exp, scale=-GATE).then_inc(s_a, 1)
                act.wait_ge(s_d, 5)
                act.activation(kend[:], kend[:], ACT.Exp, scale=GATE).then_inc(s_a, 1)
                act.wait_ge(s_d, 7)
                act.activation(nx[:, :, 0:TP], nx[:, :, 0:TP], ACT.Exp, scale=-GATE).then_inc(s_a, 1)
                act.activation(kinv[:], bc[:, :, TP:T], ACT.Exp, scale=GATE).then_inc(s_a, 1)
                act.activation(nx[:, :, TP:T], bc[:, :, TP:T], ACT.Exp, scale=-GATE).then_inc(s_a, 1)

                def key_exps(i):
                    if i >= 2:
                        act.wait_ge(s_qd, 3 * (i - 1))
                    act.activation(eb[i % 2][:], bc[:, :, tile(i)], ACT.Exp, scale=-GATE).then_inc(s_eb, 1)
                    for m in range(2):
                        act.wait_ge(s_D, 2 * i + m + 1)
                        act.activation(ki[i % 2][:, m], ki[i % 2][:, m], ACT.Exp, scale=GATE).then_inc(s_E, 1)

                def copy_kn(i):
                    rows = P if i < NT else TS
                    act.wait_ge(s_kt, i + 1)
                    if 2 <= i < NT:
                        act.wait_ge(s_ds, i - 1)
                    act.copy(kn[i % 2][0:rows], KT[0:rows, 0:2 * P]).then_inc(s_kn, 1)

                def norms(i):
                    rows = P if i < NT else TS
                    act.wait_ge(s_oo, i + 1)
                    for h in range(GH):
                        act.activation(sq[0:rows, h], OB[i % 2][0:rows, h * GV:(h + 1) * GV], ACT.Square,
                                       accum_out=rs[0:rows, i, h:h + 1]).then_inc(s_sq, 1)
                    act.wait_ge(s_sq, GH * (i + 1))
                    act.activation(rs[0:rows, i], rs[0:rows, i], ACT.Ln, scale=1.0 / GV, bias=g.eps[0:rows, :]).then_inc(s_rl, 1)
                    act.wait_ge(s_rl, i + 1)
                    act.activation(rs[0:rows, i], rs[0:rows, i], ACT.Exp, scale=-0.5).then_inc(s_rs, 1)

                def gate_ln(i):
                    x = sr[i % 2][:, :, 0:P if i < NT else TS]
                    act.wait_ge(s_r[i % 3], 16 * (i // 3 + 1))
                    if i >= 2:
                        act.wait_ge(s_fin, i - 1)
                    act.activation(x, rg[i % 3][:, :, 0:x.shape[2]], ACT.Abs).then_inc(s_se, 1)
                    act.wait_ge(s_se, 4 * i + 1)
                    act.activation(x, x, ACT.Exp, scale=-1.0).then_inc(s_se, 1)
                    act.wait_ge(s_se, 4 * i + 2)
                    act.activation(x, x, ACT.Ln, bias=1.0).then_inc(s_se, 1)

                def gate_exp(i):
                    x = sr[i % 2][:, :, 0:P if i < NT else TS]
                    act.wait_ge(s_sd, i + 1)
                    act.activation(x, x, ACT.Exp).then_inc(s_se, 1)

                def fin_hi(i):
                    w = P if i < NT else TS
                    act.wait_ge(s_fin, i + 1)
                    act.copy(g.op_hi[:, GH:2 * GH, tile(i)], fin[i % 2][:, :, 0:w]).then_inc(s_fh, 1)

                key_exps(0)
                copy_kn(0)
                for i in range(N9):
                    if i + 1 < NT:
                        key_exps(i + 1)
                    if i + 1 < N9:
                        copy_kn(i + 1)
                    gate_ln(i)
                    norms(i)
                    gate_exp(i)
                    if i > 0:
                        fin_hi(i - 1)
                fin_hi(N9 - 1)

            @block.vector
            def _(dve):
                nd = [0]

                def pre(ins):
                    nd[0] += 1
                    ins.then_inc(s_d, 1)

                dve.tensor_scalar(negb[:], g.vecT[:, 16:18], -1.0, None, ALU.mult).then_inc(s_nb, 1)
                dve.wait_ge(s_a, 9)
                dve.wait_ge(s_c, 7)
                pre(dve.scalar_tensor_tensor(out=nx[:].rearrange("k m t -> k (m t)"), in0=nx[:].rearrange("k m t -> k (m t)"),
                                             scalar=0.0, in1=bc[:].rearrange("k m t -> k (m t)"), op0=ALU.max, op1=ALU.add))
                dve.wait_ge(s_d, 1)
                for m in range(2):
                    pre(dve.tensor_tensor_scan(bc[:, m, :], reset, nx[:, m, :], 0.0, ALU.mult, ALU.add))
                dve.wait_ge(s_d, 3)
                for n, w, t0 in ((NT, P, 0), (NSEQ, NEW, TP)):
                    b = bc[:, :, t0:t0 + n * w].rearrange("k m (n w) -> k m n w", w=w)
                    pre(dve.tensor_tensor(kend[:, :, t0:t0 + n * w].rearrange("k m (n w) -> k m n w", w=w), b,
                                          b[:, :, :, w - 1:w].to_broadcast([P, 2, n, w]), ALU.subtract))
                dve.wait_ge(s_q, 16)
                dve.wait_ge(s_k, 16)
                for m in range(2):
                    b = bc[:, m, 0:TP].rearrange("k (n w) -> k n w", w=SUB)
                    pre(dve.tensor_tensor(nx[:, m, 0:TP].rearrange("k (n w) -> k n w", w=SUB), b,
                                          b[:, :, MID:MID + 1].to_broadcast([P, TP // SUB, SUB]), ALU.subtract))
                def ada_rows(i):
                    dve.wait_ge(s_am, 4 * i + 4)
                    if i > 0:
                        dve.wait_ge(s_at, i)
                    dve.tensor_copy(arow[:], ADA[0:NMOD, :]).then_inc(s_ar, 1)

                def ada_mod(i):
                    dve.wait_ge(s_at, i + 1)
                    add_bias(dve, g, ADA, 0, 2 * KD + 4 * i, 4).then_inc(s_ae, 1)

                ada_rows(0)
                dve.wait_ge(s_a, 11)
                pre(dve.tensor_tensor(kend[:], kend[:], k[:], ALU.mult))
                ada_mod(0)
                dve.wait_ge(s_a, 14)
                dve.wait_ge(s_z, 5)
                pre(dve.scalar_tensor_tensor(out=kinv[:], in0=kinv[:], scalar=BIG, in1=k[:, :, TP:T], op0=ALU.min, op1=ALU.mult))
                for h in range(2):
                    pre(dve.scalar_tensor_tensor(out=qs[HALF[h], :, h, :], in0=nx[HALF[h], :, TP:T], scalar=QS,
                                                 in1=q[HALF[h], :, TP:T], op0=ALU.mult, op1=ALU.mult))
                dve.wait_ge(s_d, 11)
                dve.scalar_tensor_tensor(out=nx[:, :, TP:T], in0=nx[:, :, TP:T], scalar=QS, in1=q[:, :, TP:T],
                                         op0=ALU.mult, op1=ALU.mult).then_inc(s_x, 1)
                dve.wait_ge(s_x, 1)
                dve.wait_ge(s_c, 14)
                for m in range(2):
                    pre(dve.tensor_tensor(qm[:, m], nx[:, m, TP:T].rearrange("k (o t) -> k o t", o=1).to_broadcast([P, NSEQ, TS]),
                                          colm[:], ALU.mult))

                def keys(i):
                    b = bc[:, :, tile(i)]
                    mid = b.rearrange("k m (n w) -> k m n w", w=SUB)[:, :, :, MID:MID + 1]
                    if i >= 2:
                        dve.wait_ge(s_sc, i - 1)
                    for m in range(2):
                        dve.tensor_tensor(ki[i % 2][:, m], b[:, m:m + 1, :].to_broadcast([P, NSUB, P]),
                                          mid[:, m].to_broadcast([P, NSUB, P]), ALU.subtract).then_inc(s_D, 1)
                    for m in range(2):
                        dve.wait_ge(s_E, 2 * i + m + 1)
                        dve.scalar_tensor_tensor(out=ki[i % 2][:, m], in0=ki[i % 2][:, m], scalar=BIG,
                                                 in1=k[:, m:m + 1, tile(i)].to_broadcast([P, NSUB, P]),
                                                 op0=ALU.min, op1=ALU.mult).then_inc(s_ki, 1)
                    if i >= 2:
                        dve.wait_ge(s_oo, i - 1)
                    dve.wait_ge(s_eb, i + 1)
                    dve.scalar_tensor_tensor(out=qdec[i % 2][:], in0=eb[i % 2][:], scalar=QS, in1=q[:, :, tile(i)],
                                             op0=ALU.mult, op1=ALU.mult).then_inc(s_qd, 1)
                    for h in range(2):
                        dve.scalar_tensor_tensor(out=qi[i % 2][HALF[h], :, h, :], in0=nx[HALF[h], :, tile(i)], scalar=QS,
                                                 in1=q[HALF[h], :, tile(i)], op0=ALU.mult, op1=ALU.mult).then_inc(s_qd, 1)

                def scores(i):
                    rows = P if i < NT else TS
                    s = SC[i % 2][0:rows].rearrange("k (h t) -> k h t", h=GH)[:, :, 0:rows]
                    p = pt[i % 2][0:rows, :, 0:rows]
                    dve.wait_ge(s_sc, i + 1)
                    if i >= 2:
                        dve.wait_ge(s_oo, i - 1)
                    dve.tensor_scalar(p, s, BIG, -BIG, ALU.min, ALU.max).then_inc(s_cl, 1)
                    dve.wait_ge(s_cl, i + 1)
                    mask = (tri if i < NT else tri8)[:].rearrange("k (o t) -> k o t", o=1).to_broadcast([rows, GH, rows])
                    dve.tensor_tensor(p, p, mask, ALU.mult).then_inc(s_pt, 1)

                def normed(i):
                    rows = P if i < NT else TS
                    dve.wait_ge(s_rs, i + 1)
                    if i >= 2:
                        dve.wait_ge(s_ot, i - 1)
                    dve.tensor_tensor(on[i % 2][0:rows], OB[i % 2][0:rows].rearrange("t (h v) -> t h v", h=GH),
                                      rs[0:rows, i].rearrange("t (h o) -> t h o", o=1).to_broadcast([rows, GH, GV]),
                                      ALU.mult).then_inc(s_on, 1)

                def gate_exponent(i):
                    w = P if i < NT else TS
                    x = sr[i % 2][:, :, 0:w]
                    dve.wait_ge(s_se, 4 * i + 3)
                    dve.scalar_tensor_tensor(out=x, in0=rg[i % 3][:, :, 0:w], scalar=0.0, in1=x, op0=ALU.min,
                                             op1=ALU.subtract).then_inc(s_sd, 1)

                def gated(i):
                    w = P if i < NT else TS
                    dve.wait_ge(s_ot, i + 1)
                    if i >= 2:
                        dve.wait_ge(s_fl, i - 1)
                    x = sr[i % 2][:, :, 0:w]
                    dve.wait_ge(s_se, 4 * i + 4)
                    dve.tensor_tensor(x, x, rg[i % 3][:, :, 0:w], ALU.mult).then_inc(s_sm, 1)
                    dve.wait_ge(s_sm, i + 1)
                    dve.scalar_tensor_tensor(out=fin[i % 2][:, :, 0:w], in0=OT[:].rearrange("v (h t) -> v h t", h=GH)[:, :, 0:w],
                                             scalar=g.vecT[:, 18:19], in1=x, op0=ALU.mult,
                                             op1=ALU.mult).then_inc(s_fin, 1)

                def state(i):
                    dve.wait_ge(s_ds, i + 1)
                    for h in range(GH):
                        r = HALF[h % 2]
                        dve.scalar_tensor_tensor(out=st[r, h, :], in0=st[r, h, :], scalar=dec[r, h // 2, i:i + 1],
                                                 in1=DS[r, h * GV:(h + 1) * GV], op0=ALU.mult, op1=ALU.add).then_inc(s_st, 1)

                keys(0)
                for i in range(N9):
                    if i + 1 < NT:
                        keys(i + 1)
                    if i + 1 < NADA:
                        ada_rows(i + 1)
                    scores(i)
                    gate_exponent(i)
                    if i > 0:
                        normed(i - 1)
                    if i + 1 < NADA:
                        ada_mod(i + 1)
                    if i < NT:
                        if i > 0:
                            dve.wait_ge(s_st, 4 * i)
                        state(i)
                    if i > 0:
                        gated(i - 1)
                normed(NT)
                gated(NT)
                dve.wait_ge(s_ae, NADA)
                scale_gain(dve, g, g.mul2, SC2, KD)
                dve.wait_ge(s_kn, N9)
                dve.wait_ge(s_s0, 64)
                dve.wait_ge(s_oo, N9)
                for s in range(NSEQ + 1):
                    if s < NSEQ:
                        if s >= 2:
                            dve.wait_ge(s_xp, s - 1)
                        dve.tensor_scalar(kem[s % 2][:], kn[NT % 2][0:TS], rowm[:, s:s + 1], None, ALU.mult).then_inc(s_km, 1)
                    if s == 0:
                        continue
                    dve.wait_ge(s_xp, s)
                    for h in range(GH):
                        r = HALF[h % 2]
                        dve.scalar_tensor_tensor(out=s0[r, s - 1, h, :], in0=s0[r, s - 1, h, :], scalar=dec[r, h // 2, NT + s - 1:NT + s],
                                                 in1=g.bank[s - 1][r, h * GV:(h + 1) * GV], op0=ALU.mult, op1=ALU.add).then_inc(s_x, 1)

            @block.tensor
            def _(pe):
                pe.wait_ge(s_gin, 32)
                for m in range(2):
                    for c, (t0, tw) in enumerate(CHUNKS):
                        pe.matmul(g.bank[3 * m + c][:, 0:tw], wg[:, m * P:(m + 1) * P], al[:, t0:t0 + tw],
                                  start=True, stop=True).then_inc(s_gate, 1)

                def turn_keys(i):
                    rows = P if i < NT else TS
                    if i > 0:
                        pe.wait_ge(s_kn, i)
                    for m in range(2):
                        last = pe.transpose(KT[0:rows, m * P:(m + 1) * P], kend[:, m, tile(i)], g.ident[:])
                    last.then_inc(s_kt, 1)

                def score(i):
                    if i >= 2:
                        pe.wait_ge(s_pt, i - 1)
                    if i < NT:
                        pe.wait_ge(s_qd, 3 * i + 3)
                        out = SC[i % 2][:].rearrange("k (m h t) -> k m h t", m=2, h=2)
                        for m in range(2):
                            for n in range(NSUB):
                                c = slice(n * SUB, (n + 1) * SUB)
                                last = pe.matmul(out[:, m, :, n * SUB:(n + 1) * SUB], ki[i % 2][:, m, n, :], qi[i % 2][:, m, :, c],
                                                 start=True, stop=True)
                    else:
                        out = SC[i % 2][0:TS].rearrange("k (m h t) -> k m h t", m=2, h=2)
                        for m in range(2):
                            last = pe.matmul(out[:, m, :, 0:TS], kinv[:, m, :], qs[:, m], start=True, stop=True)
                    last.then_inc(s_sc, 1)

                def output(i):
                    rows = P if i < NT else TS
                    o = OB[i % 2][0:rows, :]
                    if i >= 2:
                        pe.wait_ge(s_on, i - 1)
                    pe.wait_ge(s_pt, i + 1)
                    pe.wait_ge(s_v[i % 3], 16 * (i // 3 + 1))
                    for h in range(GH):
                        last = pe.matmul(o[:, h * GV:(h + 1) * GV], pt[i % 2][0:rows, h, 0:rows], v[i % 3][0:rows, h * GV:(h + 1) * GV],
                                         start=(h == 0), stop=False, skip_group_check=True)
                    if i < NT:
                        if i > 0:
                            pe.wait_ge(s_st, 4 * i)
                        for m in range(2):
                            last = pe.matmul(o[:, 2 * m * GV:(2 * m + 2) * GV], qdec[i % 2][:, m, :], st[:, 2 * m:2 * m + 2, :],
                                             start=False, stop=True, skip_group_check=True)
                    else:
                        pe.wait_ge(s_s0, 64)
                        for m in range(2):
                            for s in range(NSEQ):
                                last = pe.matmul(o[:, 2 * m * GV:(2 * m + 2) * GV], qm[:, m, s, :], s0[:, s, 2 * m:2 * m + 2, :],
                                                 start=False, stop=(s == NSEQ - 1), skip_group_check=True)
                    last.then_inc(s_oo, 1)

                def outer(i):
                    pe.wait_ge(s_kn, i + 1)
                    if i > 0:
                        pe.wait_ge(s_st, 4 * i)
                    for m in range(2):
                        last = pe.matmul(DS[:, 2 * m * GV:(2 * m + 2) * GV], kn[i % 2][:, m * P:(m + 1) * P],
                                         v[i % 3][:, 2 * m * GV:(2 * m + 2) * GV], start=True, stop=True)
                    last.then_inc(s_ds, 1)

                def turn_out(i):
                    rows = P if i < NT else TS
                    pe.wait_ge(s_on, i + 1)
                    if i >= 1:
                        pe.wait_ge(s_fin, i)
                    for h in range(GH):
                        last = pe.transpose(OT[:, h * P:h * P + rows], on[i % 2][0:rows, h, :], g.ident[0:rows, 0:rows])
                    last.then_inc(s_ot, 1)

                def ada(i):
                    for m in range(4):
                        t = 4 * i + m
                        pe.wait_ge(s_wa[t % 2], 16 * (t // 2 + 1))
                        if m == 0 and i > 0:
                            pe.wait_ge(s_ae, i)
                        condition(pe, g, ADA, wa[t % 2], 2 * m, 2).then_inc(s_am, 1)

                def turn_ada(i):
                    pe.wait_ge(s_ar, i + 1)
                    turn_rows(pe, g, ADA, 0, arow).then_inc(s_at, 1)

                ada(0)
                turn_ada(0)
                ada(1)
                pe.wait_ge(s_d, 13)
                turn_keys(0)
                score(0)

                for i in range(N9):
                    if i + 1 < N9:
                        turn_keys(i + 1)
                        score(i + 1)
                    if i + 1 < NADA:
                        turn_ada(i + 1)
                    output(i)
                    if i < NT:
                        outer(i)
                    if i > 0:
                        turn_out(i - 1)
                    if i + 2 < NADA:
                        ada(i + 2)
                turn_out(NT)
                pe.wait_ge(s_fin, N9)
                for s in range(NSEQ):
                    pe.wait_ge(s_km, s + 1)
                    for m in range(2):
                        last = pe.matmul(g.bank[s][:, 2 * m * GV:(2 * m + 2) * GV], kem[s % 2][:, m * P:(m + 1) * P],
                                         v[NT % 3][0:TS, 2 * m * GV:(2 * m + 2) * GV], start=True, stop=True)
                    last.then_inc(s_xp, 1)


def stage_project_out_and_norm(g, w, w_mlp):
    nc, io = g.nc, g.io
    w_out = io["w_out"][0]
    xp = io["x_prompt"][0]
    xs = io["x_sample"].rearrange("s t d -> (s t) d")
    NP = D // PANEL
    WIN = [(0, 512), (512, 512)]
    with ExitStack() as ctx:
        x = [g.sb(f"out_x{i}", [P, D], ctx=ctx) for i in range(9)]
        tmp = [g.sb(f"out_tmp{i}", [P, TS], ctx=ctx) for i in range(2)]
        sq = [g.sb(f"out_sq{i}", [P, CHUNKS[0][1]], ctx=ctx) for i in range(2)]
        ones = g.sb("out_ones", [P, P], ctx=ctx)
        rb = g.sb("out_rstd", [P, T], ctx=ctx)
        xn = [x[i][:, 0:512] for i in range(4)]
        mod = [x[4 + i][:, 0:512] for i in range(3)]
        xsn = x[7][:, 0:512].rearrange("p (k t) -> p k t", k=KD)
        s_x = [g.sem(f"out_x{i}_loaded") for i in range(9)]
        s_c = g.sem("out_ones_set")
        s_xt = g.sem("out_x_transposed")
        s_xc = g.sem("out_x_copied")
        s_mm = g.sem("out_group_summed")
        s_ev = g.sem("out_added")
        s_tm = g.sem("out_sample_scaled")
        s_sq = g.sem("out_squared")
        s_ss = g.sem("out_squares_summed")
        s_ln = g.sem("n2_ln")
        s_rb = g.sem("n2_rstd_done")
        s_xn = g.sem("n2_normed")
        s_md = g.sem("n2_modulated")
        s_hi = g.sem("n2_hi")
        s_lop = g.sem("n2_pool_lo")
        s_lod = g.sem("n2_dve_lo")
        s_sn = g.sem("n2_sample_steps")
        turns = [None] + [(k, t0) for k in range(KD) for t0 in (0, 4)]
        groups = [(k, c) for k in range(KD) for c in range(3)]
        pieces = [(k, t0, tw) for t0, tw in WIN for k in range(KD)]
        with nc.Block() as block:
            @block.sync
            def _(sp):
                def panel(p):
                    sp.dma_start(w.raw[p % 2][:], w_out[:, p * PANEL:(p + 1) * PANEL].rearrange("(k p) c -> p k c", p=P)).then_inc(w.loaded[p % 2], 16)
                panel(0)
                sp.dma_start(x[8][0:TS], xs).then_inc(s_x[8], 16)
                for i in range(8):
                    sp.dma_start(x[i][:], xp[i * P:(i + 1) * P]).then_inc(s_x[i], 16)
                panel(1)
                for p in range(2, NP):
                    sp.wait_ge(w.lo_done, p - 1)
                    panel(p)
                for p in range(2):
                    sp.wait_ge(w.lo_done, NP - 1 + p)
                    w_mlp.load(sp, io["w_up"][0], slice(p * PANEL, (p + 1) * PANEL), p)

            @block.gpsimd
            def _(pool):
                pool.memset(ones[:], 1.0).then_inc(s_c, 1)
                for p in range(NP):
                    pool.wait_ge(w.hi_done, p + 1)
                    pool.tensor_tensor(w.lo[p % 2][:], w.raw[p % 2][:], w.hi[p % 2][:], ALU.subtract).then_inc(w.lo_done, 1)
                w_mlp.first_lo(pool)
                for j, (k, t0, tw) in enumerate(pieces):
                    if j % 2 == 0:
                        pool.wait_ge(s_md, j // 2 + 1)
                        pool.tensor_tensor(g.op_lo[:, k, t0:t0 + tw], mod[j // 2 % 3], g.op_hi[:, k, t0:t0 + tw], ALU.subtract).then_inc(s_lop, 1)

            @block.scalar
            def _(act):
                def round_hi(p):
                    act.wait_ge(w.loaded[p % 2], 16 * (p // 2 + 1))
                    if p >= 2:
                        act.wait_ge(s_mm, 6 * (p - 1))
                    act.copy(w.hi[p % 2][:], w.raw[p % 2][:]).then_inc(w.hi_done, 1)

                def copy_turn(j):
                    act.wait_ge(s_xt, j + 1)
                    b = g.bank[3 + j % 2]
                    if j == 0:
                        act.copy(g.x1T[:, :, TP:T], b[:].rearrange("p (k t) -> p k t", k=KD)).then_inc(s_xc, 1)
                    else:
                        k, t0 = turns[j]
                        act.copy(g.x1T[:, k, t0 * P:(t0 + 4) * P], b[:]).then_inc(s_xc, 1)

                round_hi(0)
                for j in range(5):
                    copy_turn(j)
                round_hi(1)
                for k in range(KD):
                    for c, (t0, tw) in enumerate(CHUNKS):
                        j = 3 * k + c
                        act.wait_ge(s_ev, j + 1)
                        if j >= 2:
                            act.wait_ge(s_ss, j - 1)
                        act.activation(sq[j % 2][:, 0:tw], g.x1T[:, k, t0:t0 + tw], ACT.Square).then_inc(s_sq, 1)
                    if k + 2 < KD:
                        copy_turn(2 * k + 5)
                        copy_turn(2 * k + 6)
                    if k % 2 and k // 2 + 2 < NP:
                        round_hi(k // 2 + 2)
                    if k == KD - 2:
                        act.wait_ge(s_mm, 6 * (NP - 1))
                        w_mlp.first_hi(act)
                for c, (t0, tw) in enumerate(CHUNKS):
                    act.wait_ge(s_ss, 3 * (KD - 1) + c + 1)
                    act.activation(rb[:, t0:t0 + tw], g.bank[5 + c][:, 0:tw], ACT.Ln, scale=1.0 / D, bias=g.eps[:]).then_inc(s_ln, 1)
                for c, (t0, tw) in enumerate(CHUNKS):
                    act.wait_ge(s_ln, c + 1)
                    act.activation(rb[:, t0:t0 + tw], rb[:, t0:t0 + tw], ACT.Exp, scale=-0.5).then_inc(s_rb, 1)
                for j, (k, t0, tw) in enumerate(pieces):
                    act.wait_ge(s_xn, j + 1)
                    if j % 2:
                        act.activation(g.op_hi[:, k, t0:t0 + tw], xn[j % 4], ACT.Identity, bias=g.mod(SH2, k)).then_inc(s_hi, 1)
                        continue
                    if j >= 6:
                        act.wait_ge(s_lop, j // 2 - 2)
                    for out, done in ((g.op_hi[:, k, t0:t0 + tw], s_hi), (mod[j // 2 % 3], s_md)):
                        act.activation(out, xn[j % 4], ACT.Identity, scale=g.mul2[:, k, 0:1], bias=g.mod(SH2, k)).then_inc(done, 1)

            @block.vector
            def _(dve):
                for j, (kc, c) in enumerate(groups):
                    t0, tw = CHUNKS[c]
                    pw = min(tw, TP - t0)
                    b = g.bank[c]
                    dve.wait_ge(s_mm, j + 1)
                    if c < 2:
                        dve.wait_ge(s_xc, 2 * kc + 2 + c)
                    if c == 2:
                        t = tmp[kc % 2]
                        dve.tensor_tensor(by_seq(t[:]), by_seq(b[:, pw:tw]), seq_row(g.modT[:, GA1 * KD + kc, 1:NMOD]), ALU.mult).then_inc(s_tm, 1)
                        dve.wait_ge(s_tm, kc + 1)
                        dve.tensor_tensor(g.x1T[:, kc, TP:T], g.x1T[:, kc, TP:T], t[:], ALU.add)
                    out = g.x1T[:, kc, t0:t0 + pw]
                    dve.scalar_tensor_tensor(out=out, in0=b[:, 0:pw], scalar=g.mod(GA1, kc), in1=out, op0=ALU.mult,
                                             op1=ALU.add).then_inc(s_ev, 1)

                def low(j):
                    k, t0, tw = pieces[j]
                    dve.wait_ge(s_hi, j + 1)
                    dve.scalar_tensor_tensor(out=g.op_lo[:, k, t0:t0 + tw], in0=xn[j % 4], scalar=g.mod(SH2, k),
                                             in1=g.op_hi[:, k, t0:t0 + tw], op0=ALU.add, op1=ALU.subtract).then_inc(s_lod, 1)

                for j, (k, t0, tw) in enumerate(pieces):
                    if j % KD == 0:
                        dve.wait_ge(s_rb, 3 if t0 else 2)
                    if j >= 4:
                        if j % 2:
                            dve.wait_ge(s_lod, j // 2 - 1)
                        else:
                            dve.wait_ge(s_md, j // 2 - 1)
                    if j % 2:
                        dve.scalar_tensor_tensor(out=xn[j % 4], in0=g.x1T[:, k, t0:t0 + tw], scalar=g.mul2[:, k, 0:1],
                                                 in1=rb[:, t0:t0 + tw], op0=ALU.mult, op1=ALU.mult).then_inc(s_xn, 1)
                    else:
                        dve.tensor_tensor(xn[j % 4], g.x1T[:, k, t0:t0 + tw], rb[:, t0:t0 + tw], ALU.mult).then_inc(s_xn, 1)
                    if j >= 3 and j % 2:
                        low(j - 2)
                low(len(pieces) - 1)
                rows = lambda a: a.rearrange("p k (s o) -> p k s o", o=1).to_broadcast([P, KD, NSEQ, NEW])
                seqs = xsn.rearrange("p k (s t) -> p k s t", s=NSEQ)
                hi, lo = g.op_hi[:, :, TP:T], g.op_lo[:, :, TP:T]
                rstd = rb[:, TP:T].rearrange("p (o t) -> p o t", o=1).to_broadcast([P, KD, TS])
                dve.tensor_tensor(xsn, g.x1T[:, :, TP:T], rstd, ALU.mult).then_inc(s_sn, 1)
                dve.wait_ge(s_sn, 1)
                dve.tensor_tensor(seqs, seqs, rows(g.mul2[:, :, 1:NMOD]), ALU.mult).then_inc(s_sn, 1)
                dve.wait_ge(s_sn, 2)
                dve.tensor_tensor(seqs, seqs, rows(g.modT[:, SH2 * KD:(SH2 + 1) * KD, 1:NMOD]), ALU.add).then_inc(s_sn, 1)
                dve.wait_ge(s_sn, 3)
                dve.tensor_copy(hi, xsn).then_inc(s_sn, 1)
                dve.wait_ge(s_sn, 4)
                dve.tensor_tensor(lo, xsn, hi, ALU.subtract)

            @block.tensor
            def _(pe):
                def turn(j):
                    b = g.bank[3 + j % 2]
                    if j >= 2:
                        pe.wait_ge(s_xc, j - 1)
                    if j == 0:
                        pe.wait_ge(s_x[8], 16)
                        for k in range(KD):
                            last = pe.transpose(b[:, k * TS:(k + 1) * TS], x[8][0:TS, k * P:(k + 1) * P], g.ident[0:TS, 0:TS])
                    else:
                        k, t0 = turns[j]
                        for i in range(4):
                            if k == 0:
                                pe.wait_ge(s_x[t0 + i], 16)
                            last = pe.transpose(b[:, i * P:(i + 1) * P], x[t0 + i][:, k * P:(k + 1) * P], g.ident[:])
                    last.then_inc(s_xt, 1)

                def sum_squares(j):
                    k, c = groups[j]
                    tw = CHUNKS[c][1]
                    pe.wait_ge(s_sq, j + 1)
                    pe.matmul(g.bank[5 + c][:, 0:tw], ones[:], sq[j % 2][:, 0:tw], start=(k == 0), stop=(k == KD - 1)).then_inc(s_ss, 1)

                turn(0)
                turn(1)
                pe.wait_ge(s_c, 1)
                for j, (kc, c) in enumerate(groups):
                    p, m = divmod(kc, 2)
                    t0, tw = CHUNKS[c]
                    if j % 6 == 0:
                        pe.wait_ge(w.lo_done, p + 1)
                    if j >= 3:
                        pe.wait_ge(s_ev, j - 2)
                    for k in range(KD):
                        cols = slice(m * P, (m + 1) * P)
                        last = three_products(pe, g.bank[c][:, 0:tw], w.hi[p % 2][:, k, cols], w.lo[p % 2][:, k, cols],
                                              g.op_hi[:, k, t0:t0 + tw], g.op_lo[:, k, t0:t0 + tw], k, KD)
                    last.then_inc(s_mm, 1)
                    if j == 0:
                        for t in range(2, 5):
                            turn(t)
                    if j >= 2:
                        sum_squares(j - 2)
                    if c == 2 and kc + 2 < KD:
                        turn(2 * kc + 5)
                        turn(2 * kc + 6)
                sum_squares(len(groups) - 2)
                sum_squares(len(groups) - 1)


def stage_mlp(g, w, h_hi, h_lo):
    nc, io = g.nc, g.io
    w_up, w_down = io["w_up"][0], io["w_down"][0]
    FB = 512
    NG = FF // FB
    KF = FB // P
    NUP, NDN = 3 * KF, 3 * KD
    NGR = NUP + NDN
    NBANK = 6
    with ExitStack() as ctx:
        a_hi = g.sb("mlp_a_hi", [P, KF, T], F32R, ctx=ctx)
        a_lo = g.sb("mlp_a_lo", [P, KF, T], F32R, ctx=ctx)
        r = [g.sb(f"mlp_relu{i}", [P, 384], ctx=ctx) for i in range(3)]
        q = [g.sb(f"mlp_sq{i}", [P, 384], ctx=ctx) for i in range(3)]
        tmp = [g.sb(f"mlp_tmp{i}", [P, TS], ctx=ctx) for i in range(2)]
        s_mm = g.sem("mlp_group_summed")
        s_re = g.sem("mlp_relu_done")
        s_sq = g.sem("mlp_squared")
        s_ah = g.sem("mlp_a_hi_done")
        s_al = g.sem("mlp_a_lo_done")
        s_dn = g.sem("mlp_added")
        s_tm = g.sem("mlp_sample_scaled")

        def down_view(t):
            return t[:].rearrange("p k c -> p (k c)").rearrange("p (k c) -> p k c", k=KF)

        def up_groups(u):
            return [(u * NUP // 2 + m * 3 + c, 2 * u + m, c) for m in range(2) for c in range(3)]

        def slot_free(q_):
            return [NUP + NDN // 2 - NGR, 0, NUP // 2, NUP][q_]

        with nc.Block() as block:
            @block.sync
            def _(sp):
                def load(n, block_, p):
                    s = p % 2
                    sp.wait_ge(w.lo_done, n * 4 + (p - 1 if p >= 2 else p + 3))
                    if p < 2:
                        w.load(sp, w_up, bass.ds(block_ * FB + p * PANEL, PANEL), s)
                    else:
                        src = w_down[bass.ds(block_ * FB, FB), (p - 2) * 512:(p - 1) * 512].rearrange("(k p) c -> p k c", p=P)
                        sp.dma_start(down_view(w.raw[s]), src).then_inc(w.loaded[s], 16)

                with sp.Fori(0, NG - 1) as n:
                    load(n, n, 2)
                    load(n, n, 3)
                    load(n, n + 1, 0)
                    load(n, n + 1, 1)
                load(NG - 1, NG - 1, 2)
                load(NG - 1, NG - 1, 3)

            def blocks(eng, split, work):
                def block_(n, more):
                    for p in range(4):
                        if p < 3:
                            split(n, p + 1)
                        elif more:
                            split(n + 1, 0)
                        work(n, p)
                with eng.Fori(0, NG - 1) as n:
                    block_(n, True)
                block_(NG - 1, False)

            @block.gpsimd
            def _(pool):
                def split(n, p):
                    s = p % 2
                    pool.wait_ge(w.hi_done, n * 4 + p + 1)
                    pool.tensor_tensor(w.lo[s][:], w.raw[s][:], w.hi[s][:], ALU.subtract).then_inc(w.lo_done, 1)

                def work(n, p):
                    if p < 2:
                        for i, m, c in up_groups(p):
                            t0, tw = CHUNKS[c]
                            pool.wait_ge(s_ah, n * NUP + i + 1)
                            pool.tensor_tensor(a_lo[:, m, t0:t0 + tw], q[i % 3][:, 0:tw], a_hi[:, m, t0:t0 + tw],
                                               ALU.subtract).then_inc(s_al, 1)

                blocks(pool, split, work)

            @block.scalar
            def _(act):
                act.sem_inc(s_al, 3)

                def split(n, p):
                    s = p % 2
                    act.wait_ge(w.loaded[s], (n * 2 + p // 2) * 16 + 16)
                    act.wait_ge(s_mm, n * NGR + (NGR + slot_free(p)))
                    act.copy(w.hi[s][:], w.raw[s][:]).then_inc(w.hi_done, 1)

                def work(n, p):
                    if p < 2:
                        def hi(i, m, c):
                            t0, tw = CHUNKS[c]
                            act.wait_ge(s_sq, n * NUP + i + 1)
                            act.copy(a_hi[:, m, t0:t0 + tw], q[i % 3][:, 0:tw]).then_inc(s_ah, 1)
                        before = None
                        for i, m, c in up_groups(p):
                            tw = CHUNKS[c][1]
                            act.wait_ge(s_mm, NGR + n * NGR + i + 1)
                            act.wait_ge(s_al, n * NUP + i + 1)
                            act.activation(r[i % 3][:, 0:tw], g.bank[i % NBANK][:, 0:tw], ACT.Relu).then_inc(s_re, 1)
                            if before:
                                hi(*before)
                            before = (i, m, c)
                        hi(*before)

                blocks(act, split, work)

            @block.vector
            def _(dve):
                dve.sem_inc(s_dn, NDN)
                dve.sem_inc(s_tm, 2)
                with dve.Fori(0, NG) as n:
                    for i in range(NUP):
                        tw = CHUNKS[i % 3][1]
                        dve.wait_ge(s_re, n * NUP + i + 1)
                        dve.tensor_tensor(q[i % 3][:, 0:tw], r[i % 3][:, 0:tw], r[i % 3][:, 0:tw], ALU.mult).then_inc(s_sq, 1)
                    for i in range(NDN):
                        kc, c = divmod(i, 3)
                        t0, tw = CHUNKS[c]
                        pw = min(tw, TP - t0)
                        b = g.bank[(NUP + i) % NBANK]
                        dve.wait_ge(s_mm, NGR + n * NGR + NUP + i + 1)
                        dve.wait_ge(s_dn, n * NDN + i + 1)
                        if c == 2:
                            t = tmp[kc % 2]
                            dve.tensor_tensor(by_seq(t[:]), by_seq(b[:, pw:tw]), seq_row(g.modT[:, GA2 * KD + kc, 1:NMOD]),
                                              ALU.mult).then_inc(s_tm, 1)
                            dve.wait_ge(s_tm, n * KD + kc + 3)
                            dve.tensor_tensor(g.x1T[:, kc, TP:T], g.x1T[:, kc, TP:T], t[:], ALU.add)
                        out = g.x1T[:, kc, t0:t0 + pw]
                        dve.scalar_tensor_tensor(out=out, in0=b[:, 0:pw], scalar=g.mod(GA2, kc), in1=out, op0=ALU.mult,
                                                 op1=ALU.add).then_inc(s_dn, 1)

            @block.tensor
            def _(pe):
                pe.sem_inc(s_mm, NGR)
                with pe.Fori(0, NG) as n:
                    def bank_free(i):
                        p = i - NBANK
                        if p < 0:
                            pe.wait_ge(s_dn, n * NDN + NDN + p + 1)
                        elif p < NUP:
                            pe.wait_ge(s_re, n * NUP + p + 1)
                        else:
                            pe.wait_ge(s_dn, n * NDN + NDN + p - NUP + 1)

                    for u in range(2):
                        pe.wait_ge(w.lo_done, n * 4 + u + 1)
                        for i, m, c in up_groups(u):
                            t0, tw = CHUNKS[c]
                            bank_free(i)
                            cols = slice((m % 2) * P, (m % 2 + 1) * P)
                            for k in range(KD):
                                last = three_products(pe, g.bank[i % NBANK][:, 0:tw], w.hi[u][:, k, cols], w.lo[u][:, k, cols],
                                                      h_hi[:, k, t0:t0 + tw], h_lo[:, k, t0:t0 + tw], k, KD)
                            last.then_inc(s_mm, 1)
                    for d in range(2):
                        pe.wait_ge(w.lo_done, n * 4 + d + 3)
                        hi, lo = down_view(w.hi[d]), down_view(w.lo[d])
                        for j in range(NDN // 2):
                            m, c = divmod(j, 3)
                            i = NUP + d * NDN // 2 + j
                            t0, tw = CHUNKS[c]
                            bank_free(i)
                            cols = slice(m * P, (m + 1) * P)
                            for k in range(KF):
                                if d == 0 and j < 3:
                                    pe.wait_ge(s_al, 3 + n * NUP + 3 * k + c + 1)
                                last = three_products(pe, g.bank[i % NBANK][:, 0:tw], hi[:, k, cols], lo[:, k, cols],
                                                      a_hi[:, k, t0:t0 + tw], a_lo[:, k, t0:t0 + tw], k, KF)
                            last.then_inc(s_mm, 1)


def stage_final(g):
    nc, io = g.nc, g.io
    N9 = NT + 1
    yp = io["y_prompt"][0]
    ys = io["y_sample"].rearrange("s t d -> (s t) d")
    with ExitStack() as ctx:
        sb = lambda *a: g.sb(*a, ctx=ctx)
        gain = sb("fin_gain", [P, D])
        sq = [sb(f"fin_sq{i}", [P, D]) for i in range(2)]
        ss = sb("fin_ss", [P, N9, 2])
        rs = sb("fin_rstd", [P, N9])
        y = [sb(f"fin_y{i}", [P, D]) for i in range(3)]
        s_g = g.sem("fin_gain_loaded")
        s_tr = g.sem("fin_turned")
        s_sq = g.sem("fin_squared")
        s_su = g.sem("fin_summed")
        s_ln = g.sem("fin_ln")
        s_rs = g.sem("fin_rstd_done")
        s_y = g.sem("fin_y_done")
        s_out = [g.sem(f"fin_y{i}_stored") for i in range(3)]
        with nc.Block() as block:
            @block.sync
            def _(sp):
                sp.dma_start(gain[:], io["g_final"].rearrange("(o d) -> o d", o=1).to_broadcast([P, D])).then_inc(s_g, 16)
                for i in range(N9):
                    w = P if i < NT else TS
                    sp.wait_ge(s_y, 2 * i + 2)
                    sp.dma_start(yp[i * P:(i + 1) * P] if i < NT else ys, y[i % 3][0:w]).then_inc(s_out[i % 3], 16)
                for i in range(3):
                    sp.wait_ge(s_out[i], 16 * 3)

            @block.tensor
            def _(pe):
                for i in range(N9):
                    w = P if i < NT else TS
                    for half in range(2):
                        if i >= 4:
                            pe.wait_ge(s_y, 2 * (i - 4) + half + 1)
                        for k in range(4):
                            last = pe.transpose(g.bank[(2 * i + half) % 8][0:w, k * P:(k + 1) * P],
                                                g.x1T[:, half * 4 + k, i * P:i * P + w], g.ident[:])
                        last.then_inc(s_tr, 1)

            @block.scalar
            def _(act):
                for i in range(N9):
                    w = P if i < NT else TS
                    for half in range(2):
                        act.wait_ge(s_tr, 2 * i + half + 1)
                        if i >= 2:
                            act.wait_ge(s_sq, 2 * (i - 2) + half + 1)
                        act.activation(sq[i % 2][0:w, half * 512:half * 512 + 512], g.bank[(2 * i + half) % 8][0:w], ACT.Square,
                                       accum_out=ss[0:w, i, half:half + 1]).then_inc(s_sq, 1)
                    act.wait_ge(s_su, i + 1)
                    act.activation(rs[0:w, i:i + 1], rs[0:w, i:i + 1], ACT.Ln, scale=1.0 / D, bias=g.eps[0:w]).then_inc(s_ln, 1)
                    act.wait_ge(s_ln, i + 1)
                    act.activation(rs[0:w, i:i + 1], rs[0:w, i:i + 1], ACT.Exp, scale=-0.5).then_inc(s_rs, 1)

            @block.vector
            def _(dve):
                dve.wait_ge(s_g, 16)
                for i in range(N9):
                    w = P if i < NT else TS
                    dve.wait_ge(s_sq, 2 * i + 2)
                    dve.tensor_tensor(rs[0:w, i:i + 1], ss[0:w, i, 0:1], ss[0:w, i, 1:2], ALU.add).then_inc(s_su, 1)
                    dve.wait_ge(s_rs, i + 1)
                    if i >= 3:
                        dve.wait_ge(s_out[i % 3], 16 * (i // 3))
                    for half in range(2):
                        cols = slice(half * 512, half * 512 + 512)
                        dve.scalar_tensor_tensor(out=y[i % 3][0:w, cols], in0=g.bank[(2 * i + half) % 8][0:w], scalar=rs[0:w, i:i + 1],
                                                 in1=gain[0:w, cols], op0=ALU.mult, op1=ALU.mult).then_inc(s_y, 1)


def build(nc, io):
    with ExitStack() as ctx:
        g = Program(nc, io, ctx)
        g.op_hi = g.sb("op_hi", [P, KD, T], F32R)
        g.op_lo = g.sb("op_lo", [P, KD, T], F32R)
        with ExitStack() as c:
            w_in = Panels(g, c, "in")
            stage_start(g, w_in)
            stage_project_in(g, w_in, g.op_hi, g.op_lo)
        with g.part():
            stage_project_gla_and_sample_attention(g)
        with ExitStack() as c:
            g.vnat = g.sb("vnat", [P, NT + 1, SB], ctx=c)
            with g.part():
                ops = HeadOperands(g, c)
                stage_natural(g, ops)
                stage_prompt_attention(g, ops)
        stage_gla(g)
        g.x1T = g.sb("x1T", [P, KD, T])
        with ExitStack() as c:
            w_out = Panels(g, c, "out")
            w_mlp = Panels(g, c, "mlp", w_out)
            stage_project_out_and_norm(g, w_out, w_mlp)
            stage_mlp(g, w_mlp, g.op_hi, g.op_lo)
        stage_final(g)


OUTS = [("y_prompt", (1, TP, D)), ("y_sample", (NSEQ, NEW, D)),
        ("k_prompt", (1, 1, TP, HEADS, HD)), ("v_prompt", (1, 1, TP, HEADS, HD)),
        ("state_prompt", (1, 1, GH, GK, GV)),
        ("k_sample", (1, NSEQ, NEW, HEADS, HD)), ("v_sample", (1, NSEQ, NEW, HEADS, HD)),
        ("state_sample", (1, NSEQ, GH, GK, GV))]

INS = ["x_prompt", "x_sample", "c_prompt", "c_sample", "cache_k", "cache_v", "state_gla", "page_table", "w_ada", "b_ada",
       "g_mix", "w_in", "b_sb", "w_gla_gate", "b_gla_gate", "g_gla_out", "w_out", "g_ffn", "w_up", "w_down", "g_final"]


def kernel(**inputs):
    import numpy as np
    from concourse import bacc
    from concourse.bass_utils import run_bass_kernel_spmd

    nc = bacc.Bacc("TRN2", target_bir_lowering=False, num_devices=1)
    arrays, io = {}, {}
    for name in INS:
        a = np.ascontiguousarray(inputs[name])
        arrays[f"in_{name}"] = a
        io[name] = nc.dram_tensor(f"in_{name}", a.shape, mybir.dt.from_np(a.dtype), kind="ExternalInput").ap()
    for name, shape in OUTS:
        io[name] = nc.dram_tensor(name, shape, F32, kind="ExternalOutput").ap()
    build(nc, io)
    r = run_bass_kernel_spmd(nc, [arrays], core_ids=[0])
    return tuple(r.results[0][name] for name, _ in OUTS)
```
